# Optimizing a Trainium2 kernel written in Bass

```python
import jax, jax.numpy as jnp
from jax import lax
import numpy as np
import jax
import jax.numpy as jnp

D_MODEL = 1024
BATCH = 1
SEQ = 256
DEPTH = 1

CHUNK = 64
Q_BLOCK = 2 * CHUNK
HEAD_DIM = 64
CONV_CH = 256
CONV_W = 3
SB_HEADS = 6
FOX_HEADS = 6
SB_DIM = SB_HEADS * HEAD_DIM
FOX_DIM = FOX_HEADS * HEAD_DIM
D_MIX = CONV_CH + SB_DIM + FOX_DIM
D_IN = 3 * CONV_CH + 3 * SB_DIM + 3 * FOX_DIM + FOX_HEADS
N_MOD = 6
N_EXPERTS = 32
TOP_K = 4
D_EXPERT = D_MODEL
SWIGLU_ALPHA = 1.702
SWIGLU_LIMIT = 7.0
EPS = 1e-6


def _rms(x):
    xf = x.astype(jnp.float32)
    return (xf * lax.rsqrt(jnp.mean(xf * xf, axis=-1, keepdims=True) + EPS)).astype(x.dtype)

def rms_norm(x, g):
    return _rms(x) * g

def short_conv_mixer(gb, gc, u, conv_w):
    v = gc * u
    y = lax.conv_general_dilated(v, conv_w[:, None, :], window_strides=(1,), padding=[(CONV_W - 1, 0)],
                                 dimension_numbers=('NWC', 'WIO', 'NWC'), feature_group_count=CONV_CH)
    return gb * y

def _query_blocks(t):
    b, h, s = t.shape[:3]
    t = t.reshape((b, h, s // Q_BLOCK, Q_BLOCK) + t.shape[3:])
    return jnp.moveaxis(t, 2, 0)

def _merge_blocks(o):
    nb, b, h, qb, d = o.shape
    return o.transpose(1, 0, 3, 2, 4).reshape(b, nb * qb, h * d)

def stick_breaking_attention(q, k, v):
    s = q.shape[2]
    scale = q.shape[-1] ** -0.5
    kpos = jnp.arange(s)

    def block(args):
        qb, start = args
        z = jnp.einsum('bhqd,bhkd->bhqk', qb, k, preferred_element_type=jnp.float32) * scale
        qpos = start + jnp.arange(Q_BLOCK)
        strict = kpos[None, :] < qpos[:, None]
        log_beta = jax.nn.log_sigmoid(z)
        log_1mb = jnp.where(strict, jax.nn.log_sigmoid(-z), 0.0)
        rest = lax.cumsum(log_1mb, axis=3, reverse=True) - log_1mb
        w = jnp.where(strict, jnp.exp(log_beta + rest), 0.0)
        return jnp.einsum('bhqk,bhkd->bhqd', w.astype(v.dtype), v)

    starts = jnp.arange(s // Q_BLOCK, dtype=jnp.int32) * Q_BLOCK
    return _merge_blocks(lax.map(block, (_query_blocks(q), starts)))

def forgetting_attention(q, k, v, log_f):
    s = q.shape[2]
    scale = q.shape[-1] ** -0.5
    kpos = jnp.arange(s)
    cum = lax.cumsum(log_f, axis=2)

    def block(args):
        qb, fq, start = args
        logits = jnp.einsum('bhqd,bhkd->bhqk', qb, k, preferred_element_type=jnp.float32) * scale
        logits = logits + (fq[..., None] - cum[:, :, None, :])
        qpos = start + jnp.arange(Q_BLOCK)
        causal = kpos[None, :] <= qpos[:, None]
        p = jax.nn.softmax(jnp.where(causal, logits, -jnp.inf), axis=-1)
        return jnp.einsum('bhqk,bhkd->bhqd', p.astype(v.dtype), v)

    starts = jnp.arange(s // Q_BLOCK, dtype=jnp.int32) * Q_BLOCK
    return _merge_blocks(lax.map(block, (_query_blocks(q), _query_blocks(cum), starts)))

def moe_ffn(h, router_w, router_b, w_mlp1, b_mlp1, w_mlp2, b_mlp2):
    b, s, d = h.shape
    xt = h.reshape(b * s, d)
    logits = (xt @ router_w + router_b).astype(jnp.float32)
    top_vals, top_idx = lax.top_k(logits, TOP_K)
    top_w = jax.nn.softmax(top_vals, axis=-1)
    combine = jnp.einsum('tk,tke->et', top_w, jax.nn.one_hot(top_idx, N_EXPERTS, dtype=jnp.float32))

    def expert_step(acc, params):
        w1, b1, w2, b2, gate_e = params
        u = xt @ w1 + b1
        glu = jnp.minimum(u[:, ::2], SWIGLU_LIMIT)
        lin = jnp.clip(u[:, 1::2], -SWIGLU_LIMIT, SWIGLU_LIMIT)
        a = glu * jax.nn.sigmoid(SWIGLU_ALPHA * glu) * (lin + 1)
        out = a @ w2 + b2
        return acc + gate_e[:, None] * out.astype(jnp.float32), None

    acc0 = jnp.zeros((b * s, d), jnp.float32)
    acc, _ = lax.scan(expert_step, acc0, (w_mlp1, b_mlp1, w_mlp2, b_mlp2, combine))
    return acc.astype(h.dtype).reshape(b, s, d)

def hybrid_layer(x, c, norm1_g, w_ada, b_ada, w_in, conv_w, sb_q_g, sb_k_g, fox_q_g, fox_k_g, fox_f_b,
                 out_norm_g, w_out, norm2_g, router_w, router_b, w_mlp1, b_mlp1, w_mlp2, b_mlp2):
    b, s, d = x.shape
    mod = (jax.nn.silu(c) @ w_ada + b_ada).reshape(b, N_MOD, 1, d)
    shift1, scale1, gate1, shift2, scale2, gate2 = (mod[:, i] for i in range(N_MOD))

    h = rms_norm(x, norm1_g) * (1 + scale1) + shift1
    proj = h @ w_in
    cuts = [int(v) for v in np.cumsum([CONV_CH] * 3 + [SB_DIM] * 3 + [FOX_DIM] * 3)]
    cb, cc, cu, sq, sk, sv, fq, fk, fv, flog = jnp.split(proj, cuts, axis=-1)

    def heads(t, n):
        return t.reshape(b, s, n, HEAD_DIM).transpose(0, 2, 1, 3)

    y_conv = short_conv_mixer(cb, cc, cu, conv_w)
    y_sb = stick_breaking_attention(rms_norm(heads(sq, SB_HEADS), sb_q_g),
                                    rms_norm(heads(sk, SB_HEADS), sb_k_g), heads(sv, SB_HEADS))
    log_f = jax.nn.log_sigmoid((flog + fox_f_b).astype(jnp.float32)).transpose(0, 2, 1)
    y_fox = forgetting_attention(rms_norm(heads(fq, FOX_HEADS), fox_q_g),
                                 rms_norm(heads(fk, FOX_HEADS), fox_k_g), heads(fv, FOX_HEADS), log_f)
    y = jnp.concatenate([y_conv, y_sb, y_fox], axis=-1)
    y = _rms(y.reshape(b, s, D_MIX // HEAD_DIM, HEAD_DIM)).reshape(b, s, D_MIX) * out_norm_g
    x = x + gate1 * (y @ w_out)

    h2 = rms_norm(x, norm2_g) * (1 + scale2) + shift2
    return x + gate2 * moe_ffn(h2, router_w, router_b, w_mlp1, b_mlp1, w_mlp2, b_mlp2)

def first_inputs(seed: int = 0) -> dict:
    key = jax.random.key(seed)
    ks = jax.random.split(key, 24)
    nrm = jax.random.normal
    f32 = jnp.float32
    L, D, E = DEPTH, D_MODEL, N_EXPERTS
    return {
        'x': nrm(ks[0], (BATCH, SEQ, D), f32),
        'c': nrm(ks[1], (BATCH, D), f32),
        'norm1_g': 1.0 + 0.05 * nrm(ks[2], (L, D), f32),
        'w_ada': 0.5 * D ** -0.5 * nrm(ks[3], (L, D, N_MOD * D), f32),
        'b_ada': 0.02 * nrm(ks[4], (L, N_MOD * D), f32),
        'w_in': D ** -0.5 * nrm(ks[5], (L, D, D_IN), f32),
        'conv_w': CONV_W ** -0.5 * nrm(ks[6], (L, CONV_W, CONV_CH), f32),
        'sb_q_g': 1.0 + 0.05 * nrm(ks[7], (L, HEAD_DIM), f32),
        'sb_k_g': 1.0 + 0.05 * nrm(ks[8], (L, HEAD_DIM), f32),
        'fox_q_g': 1.0 + 0.05 * nrm(ks[9], (L, HEAD_DIM), f32),
        'fox_k_g': 1.0 + 0.05 * nrm(ks[10], (L, HEAD_DIM), f32),
        'fox_f_b': 2.0 + 0.5 * nrm(ks[11], (L, FOX_HEADS), f32),
        'out_norm_g': 1.0 + 0.05 * nrm(ks[12], (L, D_MIX), f32),
        'w_out': D_MIX ** -0.5 * nrm(ks[13], (L, D_MIX, D), f32),
        'norm2_g': 1.0 + 0.05 * nrm(ks[14], (L, D), f32),
        'router_w': D ** -0.5 * nrm(ks[15], (L, D, E), f32),
        'router_b': 0.01 * nrm(ks[16], (L, E), f32),
        'w_mlp1': D ** -0.5 * nrm(ks[17], (L, E, D, 2 * D_EXPERT), f32),
        'b_mlp1': 0.01 * nrm(ks[18], (L, E, 2 * D_EXPERT), f32),
        'w_mlp2': D_EXPERT ** -0.5 * nrm(ks[19], (L, E, D_EXPERT, D), f32),
        'b_mlp2': 0.01 * nrm(ks[20], (L, E, D), f32),
    }

def first_block(x, c, norm1_g, w_ada, b_ada, w_in, conv_w, sb_q_g, sb_k_g, fox_q_g, fox_k_g, fox_f_b,
              out_norm_g, w_out, norm2_g, router_w, router_b, w_mlp1, b_mlp1, w_mlp2, b_mlp2):
    for l in range(DEPTH):
        x = hybrid_layer(x, c, norm1_g[l], w_ada[l], b_ada[l], w_in[l], conv_w[l], sb_q_g[l], sb_k_g[l],
                         fox_q_g[l], fox_k_g[l], fox_f_b[l], out_norm_g[l], w_out[l], norm2_g[l],
                         router_w[l], router_b[l], w_mlp1[l], b_mlp1[l], w_mlp2[l], b_mlp2[l])
    return x


DEPTH_2 = 2

CTX_LEN = 256
GRID_W = 64

NA_HEADS = 6
NA_WIN_ROWS = 8
NA_WIN_COLS = 16

GLA_HEADS = 4
GLA_DK = 32
GLA_DV = 64
GLA_RANK = 16
GLA_GATE_NORM = 16.0
GLA_CHUNK = 64

GQA_Q_HEADS = 6
GQA_KV_HEADS = 2
GQA_REP = GQA_Q_HEADS // GQA_KV_HEADS
Q_BLOCK_2 = 128
ROPE_THETA = 10000.0
ROPE_AXIS_PAIRS = HEAD_DIM // 4

FFN_HIDDEN = ((8 * D_MODEL + 3 * 256 - 1) // (3 * 256)) * 256

NA_W = NA_HEADS * HEAD_DIM
GLA_KW = GLA_HEADS * GLA_DK
GLA_VW = GLA_HEADS * GLA_DV
GQA_QW = GQA_Q_HEADS * HEAD_DIM
GQA_KVW = GQA_KV_HEADS * HEAD_DIM
MIX_W = NA_W + GLA_VW + GQA_QW
IN_WIDTHS = (NA_W, NA_W, NA_W, GLA_KW, GLA_KW, GLA_VW, GLA_VW, 2 * GLA_RANK, GQA_QW, GQA_KVW, GQA_KVW)
IN_COLS = sum(IN_WIDTHS)
IN_SPLITS = [int(s) for s in np.cumsum(IN_WIDTHS)[:-1]]

DEEPNORM_ALPHA = (2.0 * DEPTH_2) ** 0.25
DEEPNORM_BETA = (8.0 * DEPTH_2) ** -0.25
LN_EPS = 1e-5
RMS_EPS = 1e-6


def layer_norm(x, g, b):
    xf = x.astype(jnp.float32)
    mu = jnp.mean(xf, axis=-1, keepdims=True)
    var = jnp.mean(jnp.square(xf - mu), axis=-1, keepdims=True)
    return ((xf - mu) * lax.rsqrt(var + LN_EPS) * g + b).astype(x.dtype)

def rms_norm_2(x, w):
    xf = x.astype(jnp.float32)
    ms = jnp.mean(jnp.square(xf), axis=-1, keepdims=True)
    return (xf * lax.rsqrt(ms + RMS_EPS) * w).astype(x.dtype)

def modulate(x, shift, scale):
    return x * (1 + scale) + shift

def to_heads(t, n_heads):
    b, n, _ = t.shape
    return t.reshape(b, n, n_heads, -1).transpose(0, 2, 1, 3)

def merge_heads(t):
    b, h, n, d = t.shape
    return t.transpose(0, 2, 1, 3).reshape(b, n, h * d)

def flip_seq(t):
    return jnp.flip(t, axis=2)

def axial_rope_tables(n_tokens):
    t = jnp.arange(n_tokens)
    row = (t // GRID_W).astype(jnp.float32)
    col = (t % GRID_W).astype(jnp.float32)
    inv_freq = ROPE_THETA ** (-jnp.arange(ROPE_AXIS_PAIRS, dtype=jnp.float32) / ROPE_AXIS_PAIRS)
    ang_r = row[:, None] * inv_freq
    ang_c = col[:, None] * inv_freq
    ang = jnp.concatenate([ang_r, ang_r, ang_c, ang_c], axis=-1)
    return jnp.cos(ang), jnp.sin(ang)

def apply_axial_rope(x, cos, sin):
    xf = x.astype(jnp.float32)
    x1, x2, x3, x4 = jnp.split(xf, 4, axis=-1)
    rot = jnp.concatenate([-x2, x1, -x4, x3], axis=-1)
    return (xf * cos + rot * sin).astype(x.dtype)

def context_attention(q, k, v):
    s = jnp.einsum('bgrqd,bgkd->bgrqk', q, k, preferred_element_type=jnp.float32) * (q.shape[-1] ** -0.5)
    p = jax.nn.softmax(s, axis=-1).astype(v.dtype)
    return jnp.einsum('bgrqk,bgkd->bgrqd', p, v)

def neighborhood_attention(q, k, v, k_ctx, v_ctx, rpb):
    B, H, N, d = q.shape
    rows = N // GRID_W
    wr = min(NA_WIN_ROWS, rows)
    scale = d ** -0.5
    qg = q.reshape(B, H, rows, GRID_W, d)
    kg = k.reshape(B, H, rows, GRID_W, d)
    vg = v.reshape(B, H, rows, GRID_W, d)
    cols = jnp.arange(GRID_W)
    col_start = jnp.clip(cols - NA_WIN_COLS // 2, 0, GRID_W - NA_WIN_COLS)
    col_in = (cols[None, :] >= col_start[:, None]) & (cols[None, :] < col_start[:, None] + NA_WIN_COLS)
    dc_idx = jnp.clip(cols[None, :] - cols[:, None], -(NA_WIN_COLS - 1), NA_WIN_COLS - 1) + (NA_WIN_COLS - 1)

    def row_block(r):
        rs = jnp.clip(r - wr // 2, 0, rows - wr)
        q_r = lax.dynamic_index_in_dim(qg, r, axis=2, keepdims=False)
        k_s = lax.dynamic_slice_in_dim(kg, rs, wr, axis=2)
        v_s = lax.dynamic_slice_in_dim(vg, rs, wr, axis=2)
        dr_idx = rs + jnp.arange(wr) - r + (NA_WIN_ROWS - 1)
        bias = rpb[:, dr_idx[None, :, None], dc_idx[:, None, :]]
        s_lat = jnp.einsum('bhqd,bhrkd->bhqrk', q_r, k_s, preferred_element_type=jnp.float32) * scale + bias.astype(jnp.float32)
        s_lat = jnp.where(col_in[:, None, :], s_lat, -jnp.inf).reshape(B, H, GRID_W, wr * GRID_W)
        s_ctx = jnp.einsum('bhqd,bhcd->bhqc', q_r, k_ctx, preferred_element_type=jnp.float32) * scale
        p = jax.nn.softmax(jnp.concatenate([s_lat, s_ctx], axis=-1), axis=-1).astype(v.dtype)
        p_lat = p[..., : wr * GRID_W].reshape(B, H, GRID_W, wr, GRID_W)
        p_ctx = p[..., wr * GRID_W:]
        return jnp.einsum('bhqrk,bhrkd->bhqd', p_lat, v_s) + jnp.einsum('bhqc,bhcd->bhqd', p_ctx, v_ctx)

    o = lax.map(row_block, jnp.arange(rows))
    return o.transpose(1, 2, 0, 3, 4).reshape(B, H, N, d)

def gqa_latent_attention(q, k, v, k_ctx, v_ctx):
    B, G, R, N, d = q.shape
    nb = N // Q_BLOCK_2
    keys = jnp.concatenate([k, k_ctx], axis=2)
    vals = jnp.concatenate([v, v_ctx], axis=2)
    qb = q.reshape(B, G, R, nb, Q_BLOCK_2, d).transpose(3, 0, 1, 2, 4, 5)

    def block(q_blk):
        s = jnp.einsum('bgrqd,bgkd->bgrqk', q_blk, keys, preferred_element_type=jnp.float32) * (d ** -0.5)
        p = jax.nn.softmax(s, axis=-1).astype(vals.dtype)
        return jnp.einsum('bgrqk,bgkd->bgrqd', p, vals)

    o = lax.map(block, qb)
    return o.transpose(1, 2, 3, 0, 4, 5).reshape(B, G * R, N, d)

def gla_log_gates(lr, wa2, ba):
    B, N, _ = lr.shape
    z = jnp.einsum('bner,erk->ebnk', lr.reshape(B, N, 2, GLA_RANK), wa2) + ba[:, None, None, :]
    la = jax.nn.log_sigmoid(z.astype(jnp.float32)) / GLA_GATE_NORM
    la = la.reshape(2, B, N, GLA_HEADS, GLA_DK).transpose(0, 1, 3, 2, 4)
    return la[0], la[1]

def gla_chunked(q, k, v, log_a, s0):
    B, H, N, dk = q.shape
    dv = v.shape[-1]
    nc = N // GLA_CHUNK

    def to_chunks(t):
        return t.astype(jnp.float32).reshape(B, H, nc, GLA_CHUNK, t.shape[-1]).transpose(2, 0, 1, 3, 4)

    causal = jnp.tril(jnp.ones((GLA_CHUNK, GLA_CHUNK), dtype=bool))

    def step(S, xs):
        qi, ki, vi, gi = xs
        b = jnp.cumsum(gi, axis=-2)
        b_last = b[..., -1:, :]
        diff = b[..., :, None, :] - b[..., None, :, :]
        decay = jnp.exp(jnp.where(causal[:, :, None], diff, -jnp.inf))
        A = jnp.einsum('bhtd,bhsd,bhtsd->bhts', qi, ki, decay)
        o = jnp.einsum('bhts,bhsv->bhtv', A, vi) + jnp.einsum('bhtd,bhdv->bhtv', qi * jnp.exp(b), S)
        S = jnp.exp(b_last)[..., 0, :, None] * S + jnp.einsum('bhsd,bhsv->bhdv', ki * jnp.exp(b_last - b), vi)
        return S, o

    S, o = lax.scan(step, s0.astype(jnp.float32), (to_chunks(q), to_chunks(k), to_chunks(v), to_chunks(log_a)))
    return o.transpose(1, 2, 0, 3, 4).reshape(B, H, N, dv).astype(v.dtype), S

def gla_final_state(k, v, log_a):
    b = jnp.cumsum(log_a.astype(jnp.float32), axis=2)
    w = jnp.exp(b[:, :, -1:, :] - b)
    return jnp.einsum('bhsd,bhsv->bhdv', k.astype(jnp.float32) * w, v.astype(jnp.float32))

def gla_bidirectional(q, k, v, la_f, la_b, s_f, s_b):
    o_f, s_f_end = gla_chunked(q, k, v, la_f, s_f)
    o_b, s_b_end = gla_chunked(flip_seq(q), flip_seq(k), flip_seq(v), flip_seq(la_b), s_b)
    return o_f + flip_seq(o_b), s_f_end, s_b_end

def gla_output(o, norm_w, g):
    return merge_heads(rms_norm_2(o, norm_w)) * jax.nn.silu(g)

def token_mixers(u, uc, w_in, rpb, gla_wa2, gla_ba, gla_norm_w, q_norm_w, k_norm_w, rope_cos, rope_sin, ctx_out):
    B, N, _ = u.shape
    (na_q, na_k, na_v, gl_q, gl_k, gl_v, gl_g, gl_lr, ga_q, ga_k, ga_v) = jnp.split(u @ w_in, IN_SPLITS, axis=-1)
    (na_qc, na_kc, na_vc, gl_qc, gl_kc, gl_vc, gl_gc, gl_lrc, ga_qc, ga_kc, ga_vc) = jnp.split(uc @ w_in, IN_SPLITS, axis=-1)

    k_na_c = to_heads(na_kc, NA_HEADS)
    v_na_c = to_heads(na_vc, NA_HEADS)
    o_na = neighborhood_attention(to_heads(na_q, NA_HEADS), to_heads(na_k, NA_HEADS), to_heads(na_v, NA_HEADS), k_na_c, v_na_c, rpb)

    la_f, la_b = gla_log_gates(gl_lr, gla_wa2, gla_ba)
    la_fc, la_bc = gla_log_gates(gl_lrc, gla_wa2, gla_ba)
    k_gl_c = to_heads(gl_kc, GLA_HEADS)
    v_gl_c = to_heads(gl_vc, GLA_HEADS)
    if ctx_out:
        s0 = jnp.zeros((B, GLA_HEADS, GLA_DK, GLA_DV), jnp.float32)
        q_gl_c = to_heads(gl_qc, GLA_HEADS) * GLA_DK ** -0.5
        oc_gl, s_f, s_b = gla_bidirectional(q_gl_c, k_gl_c, v_gl_c, la_fc, la_bc, s0, s0)
    else:
        s_f = gla_final_state(k_gl_c, v_gl_c, la_fc)
        s_b = gla_final_state(flip_seq(k_gl_c), flip_seq(v_gl_c), flip_seq(la_bc))
    o_gl, _, _ = gla_bidirectional(to_heads(gl_q, GLA_HEADS) * GLA_DK ** -0.5, to_heads(gl_k, GLA_HEADS), to_heads(gl_v, GLA_HEADS), la_f, la_b, s_f, s_b)

    q_ga = apply_axial_rope(rms_norm_2(to_heads(ga_q, GQA_Q_HEADS), q_norm_w), rope_cos, rope_sin)
    k_ga = apply_axial_rope(rms_norm_2(to_heads(ga_k, GQA_KV_HEADS), k_norm_w), rope_cos, rope_sin)
    k_ga_c = rms_norm_2(to_heads(ga_kc, GQA_KV_HEADS), k_norm_w)
    v_ga_c = to_heads(ga_vc, GQA_KV_HEADS)
    o_ga = gqa_latent_attention(q_ga.reshape(B, GQA_KV_HEADS, GQA_REP, N, HEAD_DIM), k_ga, to_heads(ga_v, GQA_KV_HEADS), k_ga_c, v_ga_c)

    o = jnp.concatenate([merge_heads(o_na), gla_output(o_gl, gla_norm_w, gl_g), merge_heads(o_ga)], axis=-1)
    if not ctx_out:
        return o, None

    L = uc.shape[1]
    oc_na = context_attention(to_heads(na_qc, NA_HEADS)[:, :, None], k_na_c, v_na_c)[:, :, 0]
    q_ga_c = rms_norm_2(to_heads(ga_qc, GQA_Q_HEADS), q_norm_w).reshape(B, GQA_KV_HEADS, GQA_REP, L, HEAD_DIM)
    oc_ga = context_attention(q_ga_c, k_ga_c, v_ga_c).reshape(B, GQA_Q_HEADS, L, HEAD_DIM)
    oc = jnp.concatenate([merge_heads(oc_na), gla_output(oc_gl, gla_norm_w, gl_gc), merge_heads(oc_ga)], axis=-1)
    return o, oc

def swiglu(u, w_ffn_in, w_ffn_out):
    a, b = jnp.split(u @ w_ffn_in, 2, axis=-1)
    return (jax.nn.silu(a) * b) @ w_ffn_out

def second_inputs(seed: int = 0) -> dict:
    key = jax.random.key(seed)
    ks = jax.random.split(key, 20)

    def nrm(k, shape, scale):
        return jax.random.normal(k, shape, jnp.float32) * scale

    L = DEPTH_2
    return {
        'x': nrm(ks[0], (BATCH, SEQ, D_MODEL), 1.0),
        'c': nrm(ks[1], (BATCH, D_MODEL), 1.0),
        'ctx': nrm(ks[2], (BATCH, CTX_LEN, D_MODEL), 1.0),
        'c_ctx': nrm(ks[3], (D_MODEL,), 1.0),
        'w_ada': nrm(ks[4], (L, D_MODEL, 6 * D_MODEL), 0.5 * D_MODEL ** -0.5),
        'b_ada': nrm(ks[5], (L, 6 * D_MODEL), 0.02),
        'w_in': nrm(ks[6], (L, D_MODEL, IN_COLS), D_MODEL ** -0.5),
        'na_rpb': nrm(ks[7], (L, NA_HEADS, 2 * NA_WIN_ROWS - 1, 2 * NA_WIN_COLS - 1), 0.1),
        'gla_wa2': nrm(ks[8], (L, 2, GLA_RANK, GLA_KW), GLA_RANK ** -0.5),
        'gla_ba': nrm(ks[9], (L, 2, GLA_KW), 0.02),
        'gla_norm_w': 1.0 + nrm(ks[10], (L, GLA_DV), 0.05),
        'gqa_qnorm_w': 1.0 + nrm(ks[11], (L, HEAD_DIM), 0.05),
        'gqa_knorm_w': 1.0 + nrm(ks[12], (L, HEAD_DIM), 0.05),
        'w_out': nrm(ks[13], (L, MIX_W, D_MODEL), DEEPNORM_BETA * MIX_W ** -0.5),
        'ln1_g': 1.0 + nrm(ks[14], (L, D_MODEL), 0.05),
        'ln1_b': nrm(ks[15], (L, D_MODEL), 0.02),
        'w_ffn_in': nrm(ks[16], (L, D_MODEL, 2 * FFN_HIDDEN), D_MODEL ** -0.5),
        'w_ffn_out': nrm(ks[17], (L, FFN_HIDDEN, D_MODEL), DEEPNORM_BETA * FFN_HIDDEN ** -0.5),
        'ln2_g': 1.0 + nrm(ks[18], (L, D_MODEL), 0.05),
        'ln2_b': nrm(ks[19], (L, D_MODEL), 0.02),
    }

def second_block(x, c, ctx, c_ctx, w_ada, b_ada, w_in, na_rpb, gla_wa2, gla_ba, gla_norm_w, gqa_qnorm_w, gqa_knorm_w, w_out, ln1_g, ln1_b, w_ffn_in, w_ffn_out, ln2_g, ln2_b):
    rope_cos, rope_sin = axial_rope_tables(x.shape[1])
    silu_c = jax.nn.silu(c)
    silu_cc = jax.nn.silu(c_ctx)
    xc = ctx
    for l in range(DEPTH_2):
        ctx_out = l < DEPTH_2 - 1
        mod = (silu_c @ w_ada[l] + b_ada[l])[:, None, :]
        mod_c = silu_cc @ w_ada[l] + b_ada[l]
        sh1, sc1, g1, sh2, sc2, g2 = jnp.split(mod, 6, axis=-1)
        sh1c, sc1c, g1c, sh2c, sc2c, g2c = jnp.split(mod_c, 6, axis=-1)

        o, oc = token_mixers(modulate(x, sh1, sc1), modulate(xc, sh1c, sc1c), w_in[l], na_rpb[l], gla_wa2[l], gla_ba[l], gla_norm_w[l], gqa_qnorm_w[l], gqa_knorm_w[l], rope_cos, rope_sin, ctx_out)
        x = layer_norm(DEEPNORM_ALPHA * x + g1 * (o @ w_out[l]), ln1_g[l], ln1_b[l])
        x = layer_norm(DEEPNORM_ALPHA * x + g2 * swiglu(modulate(x, sh2, sc2), w_ffn_in[l], w_ffn_out[l]), ln2_g[l], ln2_b[l])
        if ctx_out:
            xc = layer_norm(DEEPNORM_ALPHA * xc + g1c * (oc @ w_out[l]), ln1_g[l], ln1_b[l])
            xc = layer_norm(DEEPNORM_ALPHA * xc + g2c * swiglu(modulate(xc, sh2c, sc2c), w_ffn_in[l], w_ffn_out[l]), ln2_g[l], ln2_b[l])
    return x


def setup_inputs(seed=0):
    out = dict(first_inputs(seed))
    for name, value in second_inputs(seed + 1).items():
        if name != "x":
            out[name + "_2"] = value
    return out


def reference(
    x, c, norm1_g, w_ada, b_ada, w_in, conv_w, sb_q_g, sb_k_g, fox_q_g, fox_k_g, fox_f_b,
    out_norm_g, w_out, norm2_g, router_w, router_b, w_mlp1, b_mlp1, w_mlp2, b_mlp2, c_2, ctx_2,
    c_ctx_2, w_ada_2, b_ada_2, w_in_2, na_rpb_2, gla_wa2_2, gla_ba_2, gla_norm_w_2,
    gqa_qnorm_w_2, gqa_knorm_w_2, w_out_2, ln1_g_2, ln1_b_2, w_ffn_in_2, w_ffn_out_2, ln2_g_2,
    ln2_b_2,
):
    x = first_block(
        x, c, norm1_g, w_ada, b_ada, w_in, conv_w, sb_q_g, sb_k_g, fox_q_g, fox_k_g, fox_f_b,
        out_norm_g, w_out, norm2_g, router_w, router_b, w_mlp1, b_mlp1, w_mlp2, b_mlp2,
    )
    return second_block(
        x, c_2, ctx_2, c_ctx_2, w_ada_2, b_ada_2, w_in_2, na_rpb_2, gla_wa2_2, gla_ba_2,
        gla_norm_w_2, gqa_qnorm_w_2, gqa_knorm_w_2, w_out_2, ln1_g_2, ln1_b_2, w_ffn_in_2,
        w_ffn_out_2, ln2_g_2, ln2_b_2,
    )


_drawn_inputs = setup_inputs


def setup_inputs(seed=0):
    import zlib

    import numpy as np

    out = dict(_drawn_inputs(seed))
    spreads = {}
    factors = {'sb_q_g': 5.863,
     'sb_k_g': 6.691,
     'fox_q_g': 6.221,
     'fox_k_g': 4.97,
     'router_b': 3.468,
     'b_mlp1': 8.0,
     'b_mlp2': 8.0,
     'ctx_2': 4.228,
     'b_ada_2': 5.556,
     'na_rpb_2': 64.0,
     'gla_wa2_2': 6.472,
     'gla_ba_2': 45.082,
     'gla_norm_w_2': 8.0,
     'gqa_qnorm_w_2': 8.0,
     'gqa_knorm_w_2': 8.0}
    for name, (base, spread) in spreads.items():
        noise = np.random.default_rng([zlib.crc32(name.encode()), seed]).standard_normal(out[name].shape)
        drawn = base * np.exp(spread * noise) if base else spread * noise
        out[name] = jnp.asarray(drawn.astype(out[name].dtype))
    for name, factor in factors.items():
        out[name] = (out[name] * factor).astype(out[name].dtype)
    return out
```

```python
from contextlib import ExitStack, contextmanager

import numpy as np
import concourse.bass as bass
from concourse import mybir

F32 = mybir.dt.float32
U32 = mybir.dt.uint32
I32 = mybir.dt.int32
ALU = mybir.AluOpType
ACT = mybir.ActivationFunctionType
AX_X = mybir.AxisListType.X

P = 128
D = 1024
KC = D // P
S = 256
HD = 64
HEADS = 6
CONV = 256
EXPERTS = 32
TOPK = 4
HIDDEN = 2816
FC = HIDDEN // P
LAYERS = 2
GH, GDK, GDV = 4, 32, 64
KV_HEADS = 2
LEVELS = (128, 64, 32, 16, 8, 4, 2, 1)
EPS_RMS = 1e-6
EPS_LN = 1e-5
ALPHA = (2.0 * LAYERS) ** 0.25
NEG = -1e30
SWIGLU_LIMIT = 7.0
SWIGLU_ALPHA = 1.702
PIECES = ((0, 8), (8, 16), (16, 22))
SLOTS = 6
CW = 256

NAQ, NAK, NAV, GLV, GAQ, GAK, GAV, TOKW = 0, 384, 768, 1152, 1408, 1792, 1920, 2048
IN2 = [(0, 256), (256, 256), (512, 256), (768, 256), (1024, 128), (1152, 256), (1408, 256), (1664, 256),
       (1920, 32), (1952, 256), (2208, 256), (2464, 128)]


def shape_tables():
    i = np.arange(P)
    f = np.float32
    t = {
        "ident": np.eye(P, dtype=f),
        "ident2": 2 * np.eye(P, dtype=f),
        "upto": (i[:, None] <= i[None, :]).astype(f),
        "ones": np.ones((P, 256), f),
        "halves": (i[:, None] // 64 == i[None, :] // 64).astype(f),
        "headmask": ((i[:, None] // GDK == np.arange(GH)[None, :]) * GDK ** -0.5).astype(f),
        "headdiag": (i[:, None] // GDK == np.arange(GH * GDV)[None, :] // GDV).astype(f),
        "iota": np.tile(np.arange(EXPERTS, dtype=f), (P, 1)),
    }
    z = np.zeros((P, P), f)
    causal = i[None, :] <= i[:, None]
    strict = i[None, :] < i[:, None]
    t["causal"] = np.concatenate([z, np.where(causal, 0, NEG)], 1).astype(f)
    t["strictneg"] = np.concatenate([z, np.where(strict, 0, NEG)], 1).astype(f)
    t["strict01"] = np.concatenate([z + 1, strict], 1).astype(f)
    c, k = i % 64, np.arange(64)
    lo = np.clip(c - 8, 0, 48)
    t["colneg"] = np.where((k >= lo[:, None]) & (k < lo[:, None] + 16), 0, NEG).astype(f)
    cosr, sinr = [], []
    inv = 10000.0 ** (-np.arange(16, dtype=f) / 16)
    for tile in range(2):
        tok = tile * P + i
        r, cc = (tok // 64).astype(f)[:, None] * inv, (tok % 64).astype(f)[:, None] * inv
        ang = np.concatenate([r, r, cc, cc], 1).astype(f)
        sign = np.where((np.arange(64) // 16) % 2 == 0, -1, 1).astype(f)
        cosr.append(np.cos(ang))
        sinr.append(np.sin(ang) * sign)
    t["cos"] = np.concatenate(cosr, 1).astype(f)
    t["sin"] = np.concatenate(sinr, 1).astype(f)
    return t


def level_masks():
    i, t = np.arange(P), {}
    for direction in range(2):
        for m in LEVELS[1:]:
            s_even = (i[:, None] // m) % 2 == 0
            t_odd = (i[None, :] // m) % 2 == 1
            mask = s_even & t_odd & (i[:, None] // (2 * m) == i[None, :] // (2 * m))
            t[f"level{direction}_{m}"] = (mask if direction == 0 else mask.T).astype(np.float32)
    return np.concatenate(list(t.values()), axis=1)


def pack(parts):
    at, where = 0, {}
    for name, a in parts.items():
        where[name] = (at, a.shape[1])
        at += a.shape[1]
    return np.ascontiguousarray(np.concatenate(list(parts.values()), axis=1)), where


def feature_columns(v):
    return np.asarray(v).reshape(-1, P).T


def row(v):
    return np.tile(np.asarray(v).reshape(1, -1), (P, 1))


def packed_vectors(a):
    v = {
        "c": feature_columns(a["c"][0]),
        "cc": np.stack([feature_columns(a["c_2"][0]), feature_columns(a["c_ctx_2"])], 2).reshape(P, -1),
        "norm1_g": feature_columns(a["norm1_g"][0]),
        "norm2_g": feature_columns(a["norm2_g"][0]),
        "out_norm_g": feature_columns(a["out_norm_g"][0]),
        "b_ada": feature_columns(a["b_ada"][0]),
        "conv_w": a["conv_w"][0].reshape(3, 2, P).transpose(2, 1, 0).reshape(P, 6),
        "b_glu": a["b_mlp1"][0][:, ::2].reshape(EXPERTS * KC, P).T,
        "b_lin": a["b_mlp1"][0][:, 1::2].reshape(EXPERTS * KC, P).T,
        "router_b": row(a["router_b"][0]),
        "router_w": a["router_w"][0].reshape(KC, P, EXPERTS).transpose(1, 0, 2).reshape(P, -1),
        "w_f": a["w_in"][0][:, 3072:3078].reshape(KC, P, 6).transpose(1, 0, 2).reshape(P, -1),
        "f_b": row(a["fox_f_b"][0]),
        "sb_q_g": row(a["sb_q_g"][0]), "sb_k_g": row(a["sb_k_g"][0]),
        "fox_q_g": row(a["fox_q_g"][0]), "fox_k_g": row(a["fox_k_g"][0]),
    }
    for l in range(LAYERS):
        v[f"b_ada{l}"] = feature_columns(a["b_ada_2"][l])
        v[f"gla_ba{l}"] = a["gla_ba_2"][l].T
        v[f"gla_nw{l}"] = np.tile(a["gla_norm_w_2"][l], 2).reshape(P, 1)
        v[f"qn{l}"] = row(a["gqa_qnorm_w_2"][l])
        v[f"kn{l}"] = row(a["gqa_knorm_w_2"][l])
        for n in ("ln1_g", "ln1_b", "ln2_g", "ln2_b"):
            v[f"{n}{l}"] = feature_columns(a[n + "_2"][l])
    return v


def neighbour_bias(rpb):
    q, k = np.arange(S)[:, None], np.arange(S)[None, :]
    dr = k // 64 - q // 64 + 7
    dc = np.clip(k % 64 - q % 64, -15, 15) + 15
    b = np.asarray(rpb)[:, :, dr, dc]
    return np.ascontiguousarray(b.reshape(LAYERS, HEADS, 2, P, S).transpose(0, 3, 2, 1, 4))


class Counter:

    def __init__(self, sem):
        self.sem, self.base, self.count = sem, 0, 0

    def one(self):
        self.count += 1
        return 1

    def at(self, n):
        return self.base + n


class Builder:
    def __init__(self, nc, dram, where):
        self.nc, self.dram, self.where = nc, dram, where
        self.ctx = ExitStack()
        self.counters = []
        self.names = {}

    def sb(self, name, shape, dt=F32, ctx=None):
        self.names[name] = self.names.get(name, 0) + 1
        if self.names[name] > 1:
            name += f"_{self.names[name]}"
        return (ctx or self.ctx).enter_context(self.nc.sbuf_tensor(name, shape, dt))

    def counter(self, name):
        s = Counter(self.ctx.enter_context(self.nc.semaphore(name)))
        self.counters.append(s)
        return s

    @contextmanager
    def stage(self):
        with self.nc.Block(no_gpsimd_drain=True) as block:
            yield block
        for s in self.counters:
            s.base = s.count

    def vec(self, name):
        at, n = self.where[name]
        return self.vecs[:, at:at + n]

    def tab(self, name):
        at, n = self.twhere[name]
        return self.tables[:, at:at + n]

    def allocate(self):
        nc = self.nc
        self.bank = [self.ctx.enter_context(nc.psum_tensor(f"bank{i}", [P, 512], F32)) for i in range(8)]
        self.ring = self.sb("ring", [P, SLOTS, KC, CW])
        self.landed = [self.ctx.enter_context(nc.semaphore(f"landed{i}")) for i in range(SLOTS)]
        self.loaded = self.ctx.enter_context(nc.semaphore("loaded"))
        self.n_loaded = 0
        self.sums_ready = self.counter("sums_ready")
        self.sums_taken = self.counter("sums_taken")
        self.pe_ready = self.counter("pe_ready")
        self.dve_ready = self.counter("dve_ready")
        self.act_ready = self.counter("act_ready")
        self.pool_ready = self.counter("pool_ready")
        self.dve_step = self.counter("dve_step")
        self.act_step = self.counter("act_step")
        self.pool_step = self.counter("pool_step")
        self.scores_ready = self.counter("scores_ready")
        self.logits_ready = self.counter("logits_ready")
        self.mass_ready = self.counter("mass_ready")
        self.probs_ready = self.counter("probs_ready")
        self.turned = self.counter("turned")
        self.turned_copied = self.counter("turned_copied")
        self.mixed = self.counter("mixed")
        self.mixed_taken = self.counter("mixed_taken")
        self.glu_ready = self.counter("glu_ready")
        self.gate_ready = self.counter("gate_ready")
        self.act_done = self.counter("hidden_ready")
        self.vecs = self.sb("vecs", [P, self.dram["vecs"].shape[1]])
        self.tables = self.sb("tables", [P, self.dram["tables"].shape[1]])
        self.res = self.sb("res", [P, KC, 2 * S])
        self.h = self.sb("h", [P, KC, 2 * S])
        self.mod = self.sb("mod", [P, 6, KC, 2])
        self.cond = self.sb("cond", [P, KC, 2])
        self.amp = self.sb("amp", [P, KC])
        self.stat = self.sb("stat", [P, 2, 512])

    def plan_chunks(self):
        d, plan = self.dram, []

        def square(w, c0, width):
            a = w.rearrange("(c p) n -> p c n", p=P)
            plan.append([((slice(0, 4), slice(0, width)), a[:, 0:4, c0:c0 + width]),
                         ((slice(4, 8), slice(0, width)), a[:, 4:8, c0:c0 + width])])

        for i in range(24):
            square(d["w_ada"][0], i * CW, CW)
        for i in range(12):
            square(d["w_in"][0], i * CW, CW)
        for i in range(4):
            square(d["w_out"][0], i * CW, CW)
        self.n_moe = len(plan)
        for e in range(EXPERTS):
            for j in range(8):
                square(d["w_mlp1"][0, e], j * CW, CW)
            for j in range(4):
                square(d["w_mlp2"][0, e], j * CW, CW)
        for l in range(LAYERS):
            for i in range(24):
                square(d["w_ada_2"][l], i * CW, CW)
            for c0, w in IN2:
                square(d["w_in_2"][l], c0, w)
            for i in range(4):
                square(d["w_out_2"][l], i * CW, CW)
            a = d["w_ffn_in_2"][l].rearrange("(c p) n -> p c n", p=P)
            for f in range(FC):
                plan.append([((slice(0, 8), slice(P * s, P * s + P)),
                              a[:, :, s * HIDDEN + f * P:s * HIDDEN + f * P + P]) for s in range(2)])
            a = d["w_ffn_out_2"][l].rearrange("(c p) n -> p c n", p=P)
            for i in range(4):
                for k0, k1 in PIECES:
                    half = (k1 - k0) // 2
                    plan.append([((slice(0, half), slice(0, CW)), a[:, k0:k0 + half, i * CW:i * CW + CW]),
                                 ((slice(half, k1 - k0), slice(0, CW)),
                                  a[:, k0 + half:k1, i * CW:i * CW + CW])])
        self.plan = plan
        self.used_at = []
        self.next_issue = 0
        self.next_use = 0

    def issue(self, sp, n):
        if n >= len(self.plan):
            return
        if n >= SLOTS:
            sp.wait_ge(self.sums_ready.sem, self.used_at[n - SLOTS])
        for (kk, cc), src in self.plan[n]:
            sp.dma_start(self.ring[:, n % SLOTS, kk, cc], src).then_inc(self.landed[n % SLOTS], 16)

    def plan_use(self, groups):
        v = self.sums_ready.count
        for g in groups:
            v += g
            self.used_at.append(v)
        return len(groups)

    def refill(self, sp, chunks):
        for _ in range(chunks):
            self.issue(sp, self.next_issue)
            self.next_issue += 1

    def take(self, pe):
        n = self.next_use
        self.next_use += 1
        pe.wait_ge(self.landed[n % SLOTS], 32 * (n // SLOTS + 1))
        return self.ring[:, n % SLOTS, :, :]

    def load(self, eng, dst, src):
        eng.dma_start(dst, src).then_inc(self.loaded, 16)
        self.n_loaded += 16

    def start(self):
        nc = self.nc
        with self.stage() as block:
            @block.sync
            def _(sp):
                self.load(sp, self.vecs[:, :], self.dram["vecs"])
                self.load(sp, self.tables[:, :], self.dram["tables"])
                self.load(sp, self.res[:, :, 0:S], self.dram["x"])
                self.load(sp, self.res[:, :, S:2 * S], self.dram["ctx"])
                self.refill(sp, SLOTS)
                sp.wait_ge(self.loaded, self.n_loaded)

    def modulation(self, cond, bias, nv):
        nc = self.nc
        c = self.cond[:, :, 0:nv]
        src = self.vec(cond).rearrange("p (k v) -> p k v", v=nv)
        out = self.bank[0][:, 0:48 * nv].rearrange("p (i v) -> p i v", v=nv)
        n = self.plan_use([1] * 24)
        with self.stage() as block:
            @block.scalar
            def _(act):
                nc.scalar.activation(c, src, ACT.Sigmoid).then_inc(self.act_ready.sem, self.act_ready.one())

            @block.vector
            def _(dve):
                dve.wait_ge(self.act_ready.sem, self.act_ready.at(1))
                nc.vector.tensor_tensor(c, c, src, ALU.mult).then_inc(self.dve_ready.sem, self.dve_ready.one())
                dve.wait_ge(self.sums_ready.sem, self.sums_ready.at(24))
                b = self.vec(bias).unsqueeze(2).to_broadcast([P, 48, nv])
                m = self.mod[:, :, :, 0:nv].rearrange("p i c v -> p (i c) v")
                nc.vector.tensor_tensor(m, out, b, ALU.add)

            @block.tensor
            def _(pe):
                pe.wait_ge(self.dve_ready.sem, self.dve_ready.at(1))
                for i in range(24):
                    w = self.take(pe)
                    for t in range(2):
                        for k in range(KC):
                            mm = nc.tensor.matmul(out[:, 2 * i + t, :], w[:, k, P * t:P * t + P], c[:, k, :],
                                                  start=(k == 0), stop=(k == KC - 1))
                    mm.then_inc(self.sums_ready.sem, self.sums_ready.one())

            @block.sync
            def _(sp):
                self.refill(sp, n)

    def rms_modulate(self, gain, shift, scale):
        nc = self.nc
        total = self.bank[0][:, 0:S]
        rstd = self.stat[:, 0, 0:S]
        with self.stage() as block:
            @block.vector
            def _(dve):
                for k in range(KC):
                    nc.vector.tensor_tensor(self.h[:, k, S:2 * S], self.res[:, k, 0:S],
                                                               self.res[:, k, 0:S], ALU.mult)\
                                                                   .then_inc(self.dve_ready.sem, self.dve_ready.one())
                nc.vector.scalar_tensor_tensor(
                    self.amp[:, :], self.mod[:, scale, :, 0], 1.0, self.vec(gain), ALU.add, ALU.mult)\
                        .then_inc(self.dve_ready.sem, self.dve_ready.one())
                dve.wait_ge(self.pe_ready.sem, self.pe_ready.at(1))
                nc.vector.tensor_scalar(rstd, total, 1.0 / D, EPS_RMS, ALU.mult, ALU.add)\
                    .then_inc(self.dve_ready.sem, self.dve_ready.one())
                dve.wait_ge(self.act_ready.sem, self.act_ready.at(1))
                for k in range(KC):
                    nc.vector.tensor_tensor(self.h[:, k, 0:S], self.res[:, k, 0:S], rstd,
                                                               ALU.mult)\
                                                                   .then_inc(self.dve_ready.sem, self.dve_ready.one())

            @block.tensor
            def _(pe):
                for k in range(KC):
                    pe.wait_ge(self.dve_ready.sem, self.dve_ready.at(k + 1))
                    mm = nc.tensor.matmul(total, self.tab("ones")[:, 0:P], self.h[:, k, S:2 * S],
                                          start=(k == 0), stop=(k == KC - 1))
                mm.then_inc(self.pe_ready.sem, self.pe_ready.one())

            @block.scalar
            def _(act):
                act.wait_ge(self.dve_ready.sem, self.dve_ready.at(KC + 2))
                nc.scalar.activation(rstd, rstd, ACT.Ln).then_inc(self.act_step.sem, self.act_step.one())
                act.wait_ge(self.act_step.sem, self.act_step.count)
                nc.scalar.activation(rstd, rstd, ACT.Exp, scale=-0.5)\
                    .then_inc(self.act_ready.sem, self.act_ready.one())
                for k in range(KC):
                    act.wait_ge(self.dve_ready.sem, self.dve_ready.at(KC + 3 + k))
                    nc.scalar.activation(self.h[:, k, 0:S], self.h[:, k, 0:S], ACT.Identity,
                                         bias=self.mod[:, shift, k, 0:1], scale=self.amp[:, k:k + 1])

    def project(self, layout, width, tok, feat):
        nc = self.nc
        tiles = width // P
        n = self.plan_use([sum(tiles if kind == "tok" else 1 for _, kind, _ in parts) for parts in layout])

        def groups():
            for i, parts in enumerate(layout):
                for cols, kind, place in parts:
                    for t in range(tiles if kind == "tok" else 1):
                        yield i, cols, kind, place, t

        with self.stage() as block:
            @block.tensor
            def _(pe):
                at = -1
                for g, (i, (c0, c1), kind, place, t) in enumerate(groups()):
                    if i != at:
                        w, at = self.take(pe), i
                    if g >= 8:
                        pe.wait_ge(self.sums_taken.sem, self.sums_taken.at(g - 7))
                    for k in range(KC):
                        if kind == "tok":
                            mm = nc.tensor.matmul(self.bank[g % 8][:, 0:c1 - c0], self.h[:, k, P * t:P * t + P],
                                                  w[:, k, c0:c1], start=(k == 0), stop=(k == KC - 1))
                        else:
                            mm = nc.tensor.matmul(self.bank[g % 8][0:c1 - c0, 0:width], w[:, k, c0:c1],
                                                  self.h[:, k, 0:width], start=(k == 0), stop=(k == KC - 1))
                    mm.then_inc(self.sums_ready.sem, self.sums_ready.one())

            @block.scalar
            def _(act):
                for g, (i, (c0, c1), kind, place, t) in enumerate(groups()):
                    act.wait_ge(self.sums_ready.sem, self.sums_ready.at(g + 1))
                    if kind == "tok":
                        cp = nc.scalar.copy(tok[:, t, place:place + c1 - c0], self.bank[g % 8][:, 0:c1 - c0])
                    else:
                        cp = nc.scalar.copy(feat[place], self.bank[g % 8][0:c1 - c0, 0:width])
                    cp.then_inc(self.sums_taken.sem, self.sums_taken.one())

            @block.sync
            def _(sp):
                self.refill(sp, n)

    def transposes(self, jobs):
        nc = self.nc
        with self.stage() as block:
            @block.tensor
            def _(pe):
                for g, (sources, rows, _) in enumerate(jobs):
                    if g >= 8:
                        before = self.act_ready if g % 2 == 0 else self.dve_ready
                        pe.wait_ge(before.sem, before.at((g - 8) // 2 + 1))
                    for b, src in enumerate(sources):
                        mm = nc.tensor.transpose(self.bank[g % 8][0:rows, P * b:P * b + P], src, self.tab("ident"))
                    mm.then_inc(self.pe_ready.sem, self.pe_ready.one())

            @block.scalar
            def _(act):
                for g in range(0, len(jobs), 2):
                    sources, rows, dst = jobs[g]
                    act.wait_ge(self.pe_ready.sem, self.pe_ready.at(g + 1))
                    nc.scalar.copy(dst, self.bank[g % 8][0:rows, 0:P * len(sources)])\
                        .then_inc(self.act_ready.sem, self.act_ready.one())

            @block.vector
            def _(dve):
                for g in range(1, len(jobs), 2):
                    sources, rows, dst = jobs[g]
                    dve.wait_ge(self.pe_ready.sem, self.pe_ready.at(g + 1))
                    nc.vector.tensor_copy(dst, self.bank[g % 8][0:rows, 0:P * len(sources)])\
                        .then_inc(self.dve_ready.sem, self.dve_ready.one())

    def attention(self, units, name):
        nc = self.nc
        count = len(units)
        ident = self.tab("ident")
        S_, T_, O_ = self.bank[0:2], self.bank[2:4], self.bank[4:6]
        with ExitStack() as ctx, self.stage() as block:
            logits = self.sb(name + "_logits", [P, 2, S], ctx=ctx)
            soft = self.sb(name + "_soft", [P, 2, S], ctx=ctx)
            probs = self.sb(name + "_probs", [P, 2, 2 * S], ctx=ctx)
            turned = self.sb(name + "_turned", [P, 2, 2 * S], ctx=ctx)
            peak = self.sb(name + "_peak", [P, 2], ctx=ctx)
            mass = self.sb(name + "_mass", [P, 4], ctx=ctx)
            part = self.sb(name + "_part", [P, 2], ctx=ctx)
            sizes = [u["key"].shape[1] for u in units]

            @block.tensor
            def _(pe):
                for i in range(count + 2):
                    if i < count:
                        u = units[i]
                        mm = nc.tensor.matmul(S_[i % 2][:, 0:sizes[i]], u["q"], u["key"], start=True,
                                              stop=not u["add"], skip_group_check=True)
                        for x, (add, c0) in enumerate(u["add"]):
                            mm = nc.tensor.matmul(S_[i % 2][:, c0:c0 + add.shape[1]], ident, add, start=False,
                                                  stop=True, skip_group_check=True)
                        mm.then_inc(self.scores_ready.sem, self.scores_ready.one())
                    if 1 <= i <= count:
                        j = i - 1
                        pe.wait_ge(self.probs_ready.sem, self.probs_ready.at(j + 1))
                        if j >= 2:
                            pe.wait_ge(self.turned_copied.sem, self.turned_copied.at(j - 1))
                        for b in range(sizes[j] // P):
                            mm = nc.tensor.transpose(T_[j % 2][:, P * b:P * b + P],
                                                     probs[:, j % 2, P * b:P * b + P], ident)
                        mm.then_inc(self.turned.sem, self.turned.one())
                    if i >= 2:
                        j = i - 2
                        nb = sizes[j] // P
                        pe.wait_ge(self.turned_copied.sem, self.turned_copied.at(j + 1))
                        if j >= 2:
                            pe.wait_ge(self.mixed_taken.sem, self.mixed_taken.at(j - 1))
                        for b in range(nb):
                            mm = nc.tensor.matmul(O_[j % 2][:, 0:HD], turned[:, j % 2, P * b:P * b + P],
                                                  units[j]["values"][b], start=(b == 0), stop=(b == nb - 1))
                        mm.then_inc(self.mixed.sem, self.mixed.one())

            @block.vector
            def _(dve):
                for i in range(count + 2):
                    if i < count:
                        u, b, n = units[i], i % 2, sizes[i]
                        sc = S_[b][:, 0:n]
                        if i >= 2:
                            dve.wait_ge(self.probs_ready.sem, self.probs_ready.at(i - 1))
                        if u["hide"] is None:
                            dve.wait_ge(self.scores_ready.sem, self.scores_ready.at(i + 1))
                            nc.vector.reduce_max(peak[:, b:b + 1], sc, AX_X, negate=True)\
                                .then_inc(self.logits_ready.sem, self.logits_ready.one())
                        else:
                            sf, lg = soft[:, b, 0:n], logits[:, b, 0:n]
                            dve.wait_ge(self.mass_ready.sem, self.mass_ready.at(i + 1))
                            nc.vector.scalar_tensor_tensor(
                                sf, sc, 0.0, sf, ALU.max, ALU.add).then_inc(self.dve_step.sem, self.dve_step.one())
                            dve.wait_ge(self.dve_step.sem, self.dve_step.count)
                            nc.vector.tensor_tensor(sf, sf, u["hide"][0], ALU.mult)\
                                .then_inc(self.dve_step.sem, self.dve_step.one())
                            dve.wait_ge(self.dve_step.sem, self.dve_step.count)
                            nc.vector.tensor_tensor_scan(
                                lg[:, ::-1], self.tab("ones")[:, 0:n], sf[:, ::-1], 0.0, ALU.mult, ALU.add)\
                                    .then_inc(self.dve_step.sem, self.dve_step.one())
                            dve.wait_ge(self.dve_step.sem, self.dve_step.count)
                            nc.vector.tensor_tensor(lg, sc, lg, ALU.subtract)\
                                .then_inc(self.dve_step.sem, self.dve_step.one())
                            dve.wait_ge(self.dve_step.sem, self.dve_step.count)
                            nc.vector.tensor_tensor(lg, lg, u["hide"][1], ALU.add)\
                                .then_inc(self.logits_ready.sem, self.logits_ready.one())
                    if i >= 2:
                        j = i - 2
                        u, b = units[j], j % 2
                        o = O_[b][:, 0:HD]
                        dve.wait_ge(self.mixed.sem, self.mixed.at(j + 1))
                        if u["hide"] is None:
                            nc.vector.reciprocal(part[:, b:b + 1], mass[:, j % 4:j % 4 + 1])\
                                .then_inc(self.dve_step.sem, self.dve_step.one())
                            dve.wait_ge(self.dve_step.sem, self.dve_step.count)
                            nc.vector.tensor_scalar(u["out"], o, part[:, b:b + 1], None, ALU.mult)\
                                .then_inc(self.mixed_taken.sem, self.mixed_taken.one())
                        else:
                            nc.vector.tensor_copy(u["out"], o)\
                                .then_inc(self.mixed_taken.sem, self.mixed_taken.one())

            @block.scalar
            def _(act):
                for i in range(count + 1):
                    if i < count:
                        u, b, n = units[i], i % 2, sizes[i]
                        sc, pr = S_[b][:, 0:n], probs[:, b, 0:n]
                        if u["hide"] is not None:
                            sf = soft[:, b, 0:n]
                            act.wait_ge(self.scores_ready.sem, self.scores_ready.at(i + 1))
                            nc.scalar.activation(sf, sc, ACT.Abs).then_inc(self.act_step.sem, self.act_step.one())
                            act.wait_ge(self.act_step.sem, self.act_step.count)
                            nc.scalar.activation(sf, sf, ACT.Exp, scale=-1.0)\
                                .then_inc(self.act_step.sem, self.act_step.one())
                            act.wait_ge(self.act_step.sem, self.act_step.count)
                            nc.scalar.activation(sf, sf, ACT.Ln, bias=1.0)\
                                .then_inc(self.mass_ready.sem, self.mass_ready.one())
                        act.wait_ge(self.logits_ready.sem, self.logits_ready.at(i + 1))
                        if i >= 2:
                            act.wait_ge(self.turned.sem, self.turned.at(i - 1))
                        if u["hide"] is None:
                            if i >= 4:
                                act.wait_ge(self.mixed_taken.sem, self.mixed_taken.at(i - 3))
                            nc.scalar.activation(
                                pr, sc, ACT.Exp, bias=peak[:, b:b + 1], accum_out=mass[:, i % 4:i % 4 + 1])\
                                    .then_inc(self.probs_ready.sem, self.probs_ready.one())
                        else:
                            nc.scalar.activation(pr, logits[:, b, 0:n], ACT.Exp)\
                                .then_inc(self.probs_ready.sem, self.probs_ready.one())
                    if i >= 1:
                        j = i - 1
                        act.wait_ge(self.turned.sem, self.turned.at(j + 1))
                        if j >= 2:
                            act.wait_ge(self.mixed.sem, self.mixed.at(j - 1))
                        nc.scalar.copy(turned[:, j % 2, 0:sizes[j]], T_[j % 2][:, 0:sizes[j]])\
                            .then_inc(self.turned_copied.sem, self.turned_copied.one())

    def out_project(self, width, vectors, scaled):
        nc = self.nc
        n = self.plan_use([2] * 4)
        with self.stage() as block:
            @block.tensor
            def _(pe):
                for g in range(KC):
                    if g % 2 == 0:
                        w = self.take(pe)
                    for k in range(KC):
                        mm = nc.tensor.matmul(self.bank[g][:, 0:width], w[:, k, P * (g % 2):P * (g % 2) + P],
                                              self.h[:, k, 0:width], start=(k == 0), stop=(k == KC - 1))
                    mm.then_inc(self.sums_ready.sem, self.sums_ready.one())

            @block.vector
            def _(dve):
                if scaled:
                    nc.vector.tensor_scalar(
                        self.res[:, :, 0:width], self.res[:, :, 0:width], ALPHA, None, ALU.mult)\
                            .then_inc(self.dve_step.sem, self.dve_step.one())
                    dve.wait_ge(self.dve_step.sem, self.dve_step.count)
                for g in range(KC):
                    dve.wait_ge(self.sums_ready.sem, self.sums_ready.at(g + 1))
                    for v in range(vectors):
                        r = self.res[:, g, S * v:S * v + S]
                        nc.vector.scalar_tensor_tensor(r, self.bank[g][:, S * v:S * v + S],
                                                       self.mod[:, 2, g, v:v + 1], r, ALU.mult, ALU.add)

            @block.sync
            def _(sp):
                self.refill(sp, n)

    def first_block(self):
        nc = self.nc
        self.modulation("c", "b_ada", 1)
        self.rms_modulate("norm1_g", 0, 1)
        with ExitStack() as ctx:
            tok = self.sb("b1_tok", [P, 2, 2310], ctx=ctx)
            conv = self.sb("b1_conv", [P, 6, S], ctx=ctx)
            vpad = self.sb("b1_vpad", [P, 2, S + 2], ctx=ctx)
            ytok = self.sb("b1_y", [P, 2, 2 * HEADS * HD], ctx=ctx)
            qk = self.sb("b1_qk", [66, 4 * HEADS, S], ctx=ctx)
            layout = [[((0, P), "feat", 2 * i), ((P, CW), "feat", 2 * i + 1)] for i in range(3)]
            layout += [[((0, CW), "tok", i * CW)] for i in range(9)]
            self.project(layout, S, tok, [conv[:, i, :] for i in range(6)])
            self.conv_and_gates(tok, conv, vpad, ctx)
            fox = self.fox
            self.transposes([([tok[:, t, HD * h:HD * h + HD] for h in (2 * i, 2 * i + 1) for t in range(2)], HD,
                              qk[0:HD, 2 * i:2 * i + 2, :]) for i in range(6)]
                            + [([fox[:, t, h, :] for h in (2 * i, 2 * i + 1) for t in range(2)], 66,
                                qk[0:66, 12 + 2 * i:14 + 2 * i, :]) for i in range(6)])
            tok_v = lambda off, h, b: tok[:, b, off + HD * h:off + HD * h + HD]
            units = []
            for kind in range(2):
                for h in range(HEADS):
                    for t in range(2):
                        n, c0 = P * (t + 1), P * (1 - t)
                        d = HD if kind == 0 else HD + 2
                        units.append(dict(
                            q=qk[0:d, 12 * kind + h, P * t:P * t + P], key=qk[0:d, 12 * kind + 6 + h, 0:n],
                            add=[] if kind == 0 else [(self.tab("causal")[:, P:2 * P], P * t)],
                            hide=None if kind else (self.tab("strict01")[:, c0:2 * P],
                                                    self.tab("strictneg")[:, c0:2 * P]),
                            values=[tok_v(768 + 1152 * kind, h, b) for b in range(t + 1)],
                            out=ytok[:, t, 384 * kind + HD * h:384 * kind + HD * h + HD]))
            self.attention(units, "b1")
            self.transposes([([ytok[:, t, P * (2 * i + c):P * (2 * i + c) + P] for c in range(2) for t in range(2)], P,
                              self.h[:, 2 + 2 * i:4 + 2 * i, 0:S]) for i in range(3)])
            self.group_norm()
        self.out_project(S, 1, False)
        self.rms_modulate("norm2_g", 3, 4)
        self.experts()

    def conv_and_gates(self, tok, conv, vpad, ctx):
        nc = self.nc
        sq = self.sb("b1_sq", [P, 768], ctx=ctx)
        ms = self.sb("b1_ms", [P, 2, 2, 12], ctx=ctx)
        fox = self.sb("b1_fox", [P, 2, 12, 66], ctx=ctx)
        lf = self.sb("b1_lf", [P, 3, 2, 6], ctx=ctx)
        tmp = self.sb("b1_ctmp", [P, 2, 3, S], ctx=ctx)
        flog = self.bank[7][:, 0:12].rearrange("p (t h) -> p t h", h=HEADS)
        cum = self.bank[6][:, 0:12].rearrange("p (t h) -> p t h", h=HEADS)
        w = self.vec("conv_w").rearrange("p (c j) -> p c j", j=3)
        heads = lambda t, kind: tok[:, t, 1152 * kind:1152 * kind + 768].rearrange("p (h d) -> p h d", d=HD)
        with self.stage() as block:
            @block.gpsimd
            def _(pool):
                step = self.pool_step
                nc.gpsimd.memset(vpad[:, :, 0:2], 0.0).then_inc(step.sem, step.one())
                pool.wait_ge(step.sem, step.count)
                nc.gpsimd.tensor_tensor(vpad[:, :, 2:S + 2], conv[:, 2:4, :], conv[:, 4:6, :], ALU.mult)\
                    .then_inc(step.sem, step.one())
                pool.wait_ge(step.sem, step.count)
                for c in range(2):
                    for j in range(3):
                        nc.gpsimd.tensor_scalar(tmp[:, c, j, :], vpad[:, c, j:j + S], w[:, c, j:j + 1],
                                                         None, ALU.mult).then_inc(step.sem, step.one())
                pool.wait_ge(step.sem, step.count)
                nc.gpsimd.tensor_tensor(tmp[:, :, 0, :], tmp[:, :, 0, :], tmp[:, :, 1, :], ALU.add)\
                    .then_inc(step.sem, step.one())
                pool.wait_ge(step.sem, step.count)
                nc.gpsimd.tensor_tensor(tmp[:, :, 0, :], tmp[:, :, 0, :], tmp[:, :, 2, :], ALU.add)\
                    .then_inc(step.sem, step.one())
                pool.wait_ge(step.sem, step.count)
                pool.wait_ge(self.pe_ready.sem, self.pe_ready.at(1))
                nc.gpsimd.tensor_tensor(self.h[:, 0:2, 0:S], tmp[:, :, 0, :], conv[:, 0:2, :], ALU.mult)\
                    .then_inc(step.sem, step.one())
                pool.wait_ge(step.sem, step.count)

            @block.tensor
            def _(pe):
                wf = self.vec("w_f").rearrange("p (k n) -> p k n", n=HEADS)
                for t in range(2):
                    for k in range(KC):
                        mm = nc.tensor.matmul(flog[:, t, :], self.h[:, k, P * t:P * t + P], wf[:, k, :],
                                              start=(k == 0), stop=(k == KC - 1))
                mm.then_inc(self.pe_ready.sem, self.pe_ready.one())
                pe.wait_ge(self.dve_ready.sem, self.dve_ready.at(3))
                for t in range(2):
                    for s in range(t + 1):
                        mm = nc.tensor.matmul(cum[:, t, :], self.tab("upto") if s == t else self.tab("ones")[:, 0:P],
                                              lf[:, 2, s, :], start=(s == 0), stop=(s == t))
                mm.then_inc(self.pe_ready.sem, self.pe_ready.one())

            @block.scalar
            def _(act):
                act.wait_ge(self.dve_ready.sem, self.dve_ready.at(1))
                nc.scalar.activation(lf[:, 1, :, :], lf[:, 1, :, :], ACT.Exp, scale=-1.0)\
                    .then_inc(self.act_step.sem, self.act_step.one())
                act.wait_ge(self.act_step.sem, self.act_step.count)
                nc.scalar.activation(lf[:, 1, :, :], lf[:, 1, :, :], ACT.Ln, bias=1.0)\
                    .then_inc(self.act_ready.sem, self.act_ready.one())
                act.wait_ge(self.dve_ready.sem, self.dve_ready.at(2))
                nc.scalar.activation(ms[:, :, :, :], ms[:, :, :, :], ACT.Ln)\
                    .then_inc(self.act_step.sem, self.act_step.one())
                act.wait_ge(self.act_step.sem, self.act_step.count)
                nc.scalar.activation(ms[:, :, :, :], ms[:, :, :, :], ACT.Exp, scale=-0.5)\
                    .then_inc(self.act_ready.sem, self.act_ready.one())

            @block.vector
            def _(dve):
                step = self.dve_step
                dve.wait_ge(self.pe_ready.sem, self.pe_ready.at(1))
                nc.vector.tensor_tensor(lf[:, 0, :, :], flog,
                                                       self.vec("f_b").unsqueeze(1).to_broadcast([P, 2, HEADS]), ALU.add)\
                                                           .then_inc(step.sem, step.one())
                dve.wait_ge(step.sem, step.count)
                nc.vector.scalar_tensor_tensor(lf[:, 1, :, :], lf[:, 0, :, :], -1.0,
                                                                  lf[:, 0, :, :], ALU.mult, ALU.max)\
                                                                      .then_inc(self.dve_ready.sem, self.dve_ready.one())
                for t in range(2):
                    for kind in range(2):
                        v = sq[:, :].rearrange("p (h d) -> p h d", d=HD)
                        nc.vector.tensor_tensor(v, heads(t, kind), heads(t, kind), ALU.mult)\
                            .then_inc(step.sem, step.one())
                        dve.wait_ge(step.sem, step.count)
                        nc.vector.reduce_sum(ms[:, t, kind, :], v, AX_X).then_inc(step.sem, step.one())
                        dve.wait_ge(step.sem, step.count)
                nc.vector.tensor_scalar(ms[:, :, :, :], ms[:, :, :, :], 1.0 / HD, EPS_RMS,
                                                           ALU.mult, ALU.add)\
                                                               .then_inc(self.dve_ready.sem, self.dve_ready.one())
                dve.wait_ge(self.act_ready.sem, self.act_ready.at(1))
                nc.vector.scalar_tensor_tensor(
                    lf[:, 2, :, :].rearrange("p t h -> p (t h)"), lf[:, 0, :, :].rearrange("p t h -> p (t h)"), 0.0,
                    lf[:, 1, :, :].rearrange("p t h -> p (t h)"), ALU.min, ALU.subtract)\
                        .then_inc(self.dve_ready.sem, self.dve_ready.one())
                dve.wait_ge(self.act_ready.sem, self.act_ready.at(2))
                nc.vector.tensor_scalar(ms[:, :, :, 0:6], ms[:, :, :, 0:6], HD ** -0.5, None, ALU.mult)\
                    .then_inc(step.sem, step.one())
                dve.wait_ge(step.sem, step.count)
                for t in range(2):
                    for kind in range(2):
                        v, r = heads(t, kind), ms[:, t, kind, :]
                        s = sq[:, :].rearrange("p (h d) -> p h d", d=HD)
                        nc.vector.tensor_tensor(s, v, r.unsqueeze(2).to_broadcast([P, 12, HD]), ALU.mult)\
                            .then_inc(step.sem, step.one())
                        dve.wait_ge(step.sem, step.count)
                        for q in range(2):
                            g = self.vec(("sb_" if kind == 0 else "fox_") + ("q_g" if q == 0 else "k_g"))
                            dst = v[:, 6 * q:6 * q + 6, :] if kind == 0 else fox[:, t, 6 * q:6 * q + 6, 0:HD]
                            nc.vector.tensor_tensor(dst, s[:, 6 * q:6 * q + 6, :],
                                                             g.unsqueeze(1).to_broadcast([P, 6, HD]), ALU.mult)\
                                                                 .then_inc(step.sem, step.one())
                        dve.wait_ge(step.sem, step.count)
                dve.wait_ge(self.pe_ready.sem, self.pe_ready.at(2))
                nc.vector.tensor_copy(fox[:, :, 0:6, 64], cum).then_inc(step.sem, step.one())
                nc.vector.memset(fox[:, :, 0:6, 65], 1.0).then_inc(step.sem, step.one())
                nc.vector.memset(fox[:, :, 6:12, 64], 1.0).then_inc(step.sem, step.one())
                nc.vector.tensor_scalar(fox[:, :, 6:12, 65], cum, -1.0, None, ALU.mult)\
                    .then_inc(step.sem, step.one())

        self.fox = fox

    def group_norm(self):
        nc = self.nc
        with ExitStack() as ctx, self.stage() as block:
            sq = self.sb("gn_sq", [P, KC, S], ctx=ctx)

            @block.vector
            def _(dve):
                for c in range(4):
                    y = self.h[:, 2 * c:2 * c + 2, 0:S]
                    nc.vector.tensor_tensor(sq[:, 2 * c:2 * c + 2, :], y, y, ALU.mult)\
                        .then_inc(self.dve_ready.sem, self.dve_ready.one())
                for c in range(4):
                    dve.wait_ge(self.pe_ready.sem, self.pe_ready.at(c + 1))
                    nc.vector.tensor_scalar(
                        sq[:, 2 * c:2 * c + 2, :], self.bank[c][:, :].rearrange("p (c t) -> p c t", t=S),
                        1.0 / HD, EPS_RMS, ALU.mult, ALU.add).then_inc(self.dve_ready.sem, self.dve_ready.one())
                for c in range(4):
                    dve.wait_ge(self.act_ready.sem, self.act_ready.at(c + 1))
                    for k in (2 * c, 2 * c + 1):
                        nc.vector.scalar_tensor_tensor(self.h[:, k, 0:S], self.h[:, k, 0:S],
                                                       self.vec("out_norm_g")[:, k:k + 1], sq[:, k, :],
                                                       ALU.mult, ALU.mult)

            @block.tensor
            def _(pe):
                for c in range(4):
                    pe.wait_ge(self.dve_ready.sem, self.dve_ready.at(c + 1))
                    nc.tensor.matmul(self.bank[c][:, :], self.tab("halves"),
                                                       sq[:, 2 * c:2 * c + 2, :], start=True, stop=True)\
                                                           .then_inc(self.pe_ready.sem, self.pe_ready.one())

            @block.scalar
            def _(act):
                for c in range(4):
                    v = sq[:, 2 * c:2 * c + 2, :]
                    act.wait_ge(self.dve_ready.sem, self.dve_ready.at(4 + c + 1))
                    nc.scalar.activation(v, v, ACT.Ln).then_inc(self.act_step.sem, self.act_step.one())
                    act.wait_ge(self.act_step.sem, self.act_step.count)
                    nc.scalar.activation(v, v, ACT.Exp, scale=-0.5)\
                        .then_inc(self.act_ready.sem, self.act_ready.one())

    def experts(self):
        nc = self.nc
        with ExitStack() as ctx:
            comb = self.sb("moe_comb", [P, 2, EXPERTS], ctx=ctx)
            comb_t = self.sb("moe_comb_t", [EXPERTS, S], ctx=ctx)
            gates = self.sb("moe_gates", [P, EXPERTS, S], ctx=ctx)
            b2 = self.sb("moe_b2", [EXPERTS, D], ctx=ctx)
            self.route(comb, comb_t, gates, b2, ctx)
            self.mixture(comb_t, gates, b2, ctx)

    def route(self, comb, comb_t, gates, b2, ctx):
        nc = self.nc
        lg = self.sb("rt_lg", [P, 2, EXPERTS], ctx=ctx)
        top = self.sb("rt_top", [P, 2, 8], ctx=ctx)
        idx = self.sb("rt_idx", [P, 2, 8], U32, ctx=ctx)
        idf = self.sb("rt_idf", [P, 2, 8], ctx=ctx)
        wts = self.sb("rt_w", [P, 2, 4], ctx=ctx)
        neg = self.sb("rt_neg", [P, 2], ctx=ctx)
        mass = self.sb("rt_mass", [P, 2], ctx=ctx)
        hot = self.sb("rt_hot", [P, 2, 4, EXPERTS], ctx=ctx)
        raw = self.bank[0][:, 0:2 * EXPERTS].rearrange("p (t e) -> p t e", e=EXPERTS)
        rw = self.vec("router_w").rearrange("p (k e) -> p k e", e=EXPERTS)
        with self.stage() as block:
            @block.sync
            def _(sp):
                self.load(sp, b2[:, :], self.dram["b_mlp2"][0])
                sp.wait_ge(self.loaded, self.n_loaded)

            @block.tensor
            def _(pe):
                for t in range(2):
                    for k in range(KC):
                        mm = nc.tensor.matmul(raw[:, t, :], self.h[:, k, P * t:P * t + P], rw[:, k, :],
                                              start=(k == 0), stop=(k == KC - 1))
                mm.then_inc(self.pe_ready.sem, self.pe_ready.one())
                pe.wait_ge(self.dve_ready.sem, self.dve_ready.at(2))
                for t in range(2):
                    mm = nc.tensor.transpose(self.bank[1][0:EXPERTS, P * t:P * t + P], comb[:, t, :], self.tab("ident"))
                mm.then_inc(self.pe_ready.sem, self.pe_ready.one())
                for g in range(EXPERTS // 2):
                    if g >= 6:
                        pe.wait_ge(self.act_ready.sem, self.act_ready.at(1 + g - 5))
                    for e in (2 * g, 2 * g + 1):
                        for t in range(2):
                            c0 = S * (e % 2) + P * t
                            mm = nc.tensor.matmul(self.bank[2 + g % 6][:, c0:c0 + P],
                                                  comb[:, t, e:e + 1].to_broadcast([P, P]), self.tab("ident"),
                                                  start=True, stop=True)
                    mm.then_inc(self.pe_ready.sem, self.pe_ready.one())

            @block.vector
            def _(dve):
                step = self.dve_step
                dve.wait_ge(self.pe_ready.sem, self.pe_ready.at(1))
                nc.vector.tensor_tensor(
                    lg[:, :, :], raw, self.vec("router_b").unsqueeze(1).to_broadcast([P, 2, EXPERTS]), ALU.add)\
                        .then_inc(step.sem, step.one())
                dve.wait_ge(step.sem, step.count)
                for t in range(2):
                    nc.vector.max(top[:, t, :], lg[:, t, :]).then_inc(step.sem, step.one())
                    dve.wait_ge(step.sem, step.count)
                    nc.vector.max_index(idx[:, t, :], top[:, t, :], lg[:, t, :]).then_inc(step.sem, step.one())
                    dve.wait_ge(step.sem, step.count)
                nc.vector.tensor_copy(idf[:, :, :], idx[:, :, :]).then_inc(step.sem, step.one())
                dve.wait_ge(step.sem, step.count)
                nc.vector.tensor_scalar(neg[:, :], top[:, :, 0], -1.0, None, ALU.mult)\
                    .then_inc(self.dve_ready.sem, self.dve_ready.one())
                dve.wait_ge(self.act_ready.sem, self.act_ready.at(1))
                nc.vector.reciprocal(mass[:, :], mass[:, :]).then_inc(step.sem, step.one())
                dve.wait_ge(step.sem, step.count)
                for t in range(2):
                    nc.vector.tensor_scalar(wts[:, t, :], wts[:, t, :], mass[:, t:t + 1], None, ALU.mult)\
                        .then_inc(step.sem, step.one())
                    dve.wait_ge(step.sem, step.count)
                    for k in range(TOPK):
                        nc.vector.tensor_scalar(hot[:, t, k, :], self.tab("iota"), idf[:, t, k:k + 1],
                                                         wts[:, t, k:k + 1], ALU.is_equal, ALU.mult)\
                                                             .then_inc(step.sem, step.one())
                dve.wait_ge(step.sem, step.count)
                nc.vector.tensor_tensor(hot[:, :, 0:2, :], hot[:, :, 0:2, :], hot[:, :, 2:4, :], ALU.add)\
                    .then_inc(step.sem, step.one())
                dve.wait_ge(step.sem, step.count)
                nc.vector.tensor_tensor(comb[:, :, :], hot[:, :, 0, :], hot[:, :, 1, :], ALU.add)\
                    .then_inc(self.dve_ready.sem, self.dve_ready.one())
                dve.wait_ge(self.pe_ready.sem, self.pe_ready.at(2))
                nc.vector.tensor_copy(comb_t[:, :], self.bank[1][0:EXPERTS, 0:S])

            @block.scalar
            def _(act):
                act.wait_ge(self.dve_ready.sem, self.dve_ready.at(1))
                for t in range(2):
                    e = nc.scalar.activation(wts[:, t, :], top[:, t, 0:4], ACT.Exp, bias=neg[:, t:t + 1],
                                             accum_out=mass[:, t:t + 1])
                e.then_inc(self.act_ready.sem, self.act_ready.one())
                for g in range(EXPERTS // 2):
                    act.wait_ge(self.pe_ready.sem, self.pe_ready.at(3 + g))
                    nc.scalar.copy(gates[:, 2 * g:2 * g + 2, :],
                                                      self.bank[2 + g % 6][:, :].rearrange("p (e t) -> p e t", t=S))\
                                                          .then_inc(self.act_ready.sem, self.act_ready.one())

    def mixture(self, comb_t, gates, b2, ctx):
        nc = self.nc
        hid = self.sb("moe_hid", [P, KC, S], ctx=ctx)
        glu = self.sb("moe_glu", [P, 2, S], ctx=ctx)
        lin = self.sb("moe_lin", [P, 2, S], ctx=ctx)
        sig = self.sb("moe_sig", [P, 2, S], ctx=ctx)
        pair = self.bank[0:4]
        acc = lambda d: self.bank[4 + d // 2][:, S * (d % 2):S * (d % 2) + S]
        base = self.sums_ready.count
        per = 12
        assert per % SLOTS == 0 and self.n_moe == self.next_use
        visit = lambda j: ((self.n_moe + j) % SLOTS, (self.n_moe + j) // SLOTS + 1)
        loads = per // SLOTS
        for m in range(per * EXPERTS):
            self.used_at.append(base + m + 1)
        with self.stage() as block:
            @block.tensor
            def _(pe):
                for d in range(KC):
                    nc.tensor.matmul(acc(d), b2[:, P * d:P * d + P], comb_t[:, :], start=(d % 2 == 0), stop=False,
                                     skip_group_check=True)
                with pe.Fori(0, EXPERTS) as e:
                    for j in range(per):
                        slot, v = visit(j)
                        w = self.ring[:, slot, :, :]
                        pe.wait_ge(self.landed[slot], e * (32 * loads) + 32 * v)
                        if j < KC:
                            pe.wait_ge(self.sums_taken.sem, e * KC + (self.sums_taken.count + j + 1))
                            for half in range(2):
                                for k in range(KC):
                                    mm = nc.tensor.matmul(pair[j % 4][:, S * half:S * half + S],
                                                          w[:, k, half:CW:2], self.h[:, k, 0:S],
                                                          start=(k == 0), stop=(k == KC - 1))
                        else:
                            for k in range(KC):
                                if j == KC:
                                    pe.wait_ge(self.act_done.sem, e * KC + (self.act_done.count + k + 1))
                                for d in (2 * (j - KC), 2 * (j - KC) + 1):
                                    mm = nc.tensor.matmul(acc(d), w[:, k, P * (d % 2):P * (d % 2) + P],
                                                          hid[:, k, :], start=False, stop=False,
                                                          skip_group_check=True)
                        mm.then_inc(self.sums_ready.sem, 1)

            @block.vector
            def _(dve):
                taken, done = self.sums_taken.count, self.act_done.count
                step, glus = self.dve_step.count, self.glu_ready.count
                for i in range(4):
                    nc.vector.memset(lin[:, 0, i:i + 1], 0.0).then_inc(self.sums_taken.sem, 1)
                dve.wait_ge(self.sums_taken.sem, taken + 4)
                with dve.Fori(0, EXPERTS) as e:
                    for j in range(KC):
                        b = j % 2
                        g, l, s = glu[:, b, :], lin[:, b, :], sig[:, b, :]
                        bg = self.vec("b_glu")[:, bass.ds(e * KC + j, 1)]
                        bl = self.vec("b_lin")[:, bass.ds(e * KC + j, 1)]
                        dve.wait_ge(self.sums_ready.sem, e * per + (base + j + 1))
                        nc.vector.tensor_scalar(g, pair[j % 4][:, 0:S], bg, SWIGLU_LIMIT, ALU.add, ALU.min)\
                            .then_inc(self.glu_ready.sem, 1)
                        nc.vector.tensor_scalar(l, pair[j % 4][:, S:2 * S], bl, SWIGLU_LIMIT, ALU.add, ALU.min)\
                            .then_inc(self.sums_taken.sem, 1)
                        dve.wait_ge(self.sums_taken.sem, e * KC + (taken + 4 + j + 1))
                        nc.vector.tensor_scalar(l, l, -SWIGLU_LIMIT, 1.0, ALU.max, ALU.add)\
                            .then_inc(self.dve_step.sem, 1)
                        dve.wait_ge(self.dve_step.sem, e * (3 * KC) + (step + 3 * j + 1))
                        nc.vector.tensor_tensor(l, l, gates[:, bass.ds(e, 1), :].rearrange("p e t -> p (e t)"), ALU.mult)\
                            .then_inc(self.dve_step.sem, 1)
                        dve.wait_ge(self.gate_ready.sem, e * KC + (self.gate_ready.count + j + 1))
                        nc.vector.tensor_tensor(g, g, s, ALU.mult).then_inc(self.dve_step.sem, 1)
                        dve.wait_ge(self.dve_step.sem, e * (3 * KC) + (step + 3 * j + 3))
                        nc.vector.tensor_tensor(hid[:, j, :], g, l, ALU.mult).then_inc(self.act_done.sem, 1)

            @block.scalar
            def _(act):
                with act.Fori(0, EXPERTS) as e:
                    for j in range(KC):
                        b = j % 2
                        act.wait_ge(self.glu_ready.sem, e * KC + (self.glu_ready.count + j + 1))
                        nc.scalar.activation(sig[:, b, :], glu[:, b, :], ACT.Sigmoid, scale=SWIGLU_ALPHA)\
                            .then_inc(self.gate_ready.sem, 1)

            @block.sync
            def _(sp):
                w1 = self.dram["w_mlp1"][0].rearrange("e (c p) n -> e p c n", p=P)
                w2 = self.dram["w_mlp2"][0].rearrange("e (c p) n -> e p c n", p=P)
                with sp.Fori(0, EXPERTS - 1) as e:
                    for jj in range(per):
                        m = SLOTS + jj
                        ahead, j = m // per, m % per
                        slot, _ = visit(m)
                        w, c = (w1, j) if j < KC else (w2, j - KC)
                        sp.wait_ge(self.sums_ready.sem, e * per + (base + jj + 1))
                        for half in range(2):
                            src = w[bass.ds(e + ahead, 1), :, 4 * half:4 * half + 4, c * CW:(c + 1) * CW]
                            sp.dma_start(self.ring[:, slot, 4 * half:4 * half + 4, :],
                                         src.rearrange("e p c n -> (e p) c n")).then_inc(self.landed[slot], 16)
                self.next_issue += per * (EXPERTS - 1)
                self.refill(sp, per)
            self.sums_ready.count += per * EXPERTS
            self.next_use += per * EXPERTS
            self.sums_taken.count += 4 + KC * EXPERTS
            self.act_done.count += KC * EXPERTS
            self.dve_step.count += 3 * KC * EXPERTS
            self.glu_ready.count += KC * EXPERTS
            self.gate_ready.count += KC * EXPERTS
        with self.stage() as block:
            @block.vector
            def _(dve):
                for d in range(KC):
                    nc.vector.scalar_tensor_tensor(self.res[:, d, 0:S], acc(d), self.mod[:, 5, d, 0:1],
                                                   self.res[:, d, 0:S], ALU.mult, ALU.add)

    def modulate(self, width, vectors, shift, scale):
        nc = self.nc
        with self.stage() as block:
            @block.vector
            def _(dve):
                for v in range(vectors):
                    nc.vector.tensor_scalar(self.amp[:, :], self.mod[:, scale, :, v], 1.0, None,
                                                                    ALU.add)\
                                                                        .then_inc(self.dve_step.sem, self.dve_step.one())
                    dve.wait_ge(self.dve_step.sem, self.dve_step.count)
                    for k in range(KC):
                        c = slice(S * v, S * v + S)
                        o = nc.vector.tensor_scalar(self.h[:, k, c], self.res[:, k, c], self.amp[:, k:k + 1],
                                                    self.mod[:, shift, k, v:v + 1], ALU.mult, ALU.add)
                    o.then_inc(self.dve_step.sem, self.dve_step.one())
                    dve.wait_ge(self.dve_step.sem, self.dve_step.count)

    def layer_norm(self, width, gain, bias, l):
        nc = self.nc
        total, spread = self.bank[0][:, 0:width], self.bank[1][:, 0:width]
        mean, rstd = self.stat[:, 0, 0:width], self.stat[:, 1, 0:width]
        g, b = self.vec(f"{gain}{l}"), self.vec(f"{bias}{l}")
        with self.stage() as block:
            @block.tensor
            def _(pe):
                for k in range(KC):
                    mm = nc.tensor.matmul(total, self.tab("ones")[:, 0:P], self.res[:, k, 0:width],
                                          start=(k == 0), stop=(k == KC - 1))
                mm.then_inc(self.pe_ready.sem, self.pe_ready.one())
                for k in range(KC):
                    pe.wait_ge(self.act_ready.sem, self.act_ready.at(k + 1))
                    mm = nc.tensor.matmul(spread, self.tab("ones")[:, 0:P], self.h[:, k, 0:width],
                                          start=(k == 0), stop=(k == KC - 1))
                mm.then_inc(self.pe_ready.sem, self.pe_ready.one())

            @block.vector
            def _(dve):
                dve.wait_ge(self.pe_ready.sem, self.pe_ready.at(1))
                nc.vector.tensor_scalar(mean, total, 1.0 / D, None, ALU.mult)\
                    .then_inc(self.dve_step.sem, self.dve_step.one())
                dve.wait_ge(self.dve_step.sem, self.dve_step.count)
                for k in range(KC):
                    r = self.res[:, k, 0:width]
                    nc.vector.tensor_tensor(r, r, mean, ALU.subtract)\
                        .then_inc(self.dve_ready.sem, self.dve_ready.one())
                dve.wait_ge(self.pe_ready.sem, self.pe_ready.at(2))
                nc.vector.tensor_scalar(rstd, spread, 1.0 / D, EPS_LN, ALU.mult, ALU.add)\
                    .then_inc(self.dve_ready.sem, self.dve_ready.one())
                dve.wait_ge(self.act_ready.sem, self.act_ready.at(KC + 1))
                for k in range(KC):
                    r = self.res[:, k, 0:width]
                    nc.vector.tensor_tensor(r, r, rstd, ALU.mult).then_inc(self.dve_ready.sem, self.dve_ready.one())

            @block.scalar
            def _(act):
                for k in range(KC):
                    act.wait_ge(self.dve_ready.sem, self.dve_ready.at(k + 1))
                    nc.scalar.activation(self.h[:, k, 0:width], self.res[:, k, 0:width], ACT.Square)\
                        .then_inc(self.act_ready.sem, self.act_ready.one())
                act.wait_ge(self.dve_ready.sem, self.dve_ready.at(KC + 1))
                nc.scalar.activation(rstd, rstd, ACT.Ln).then_inc(self.act_step.sem, self.act_step.one())
                act.wait_ge(self.act_step.sem, self.act_step.count)
                nc.scalar.activation(rstd, rstd, ACT.Exp, scale=-0.5)\
                    .then_inc(self.act_ready.sem, self.act_ready.one())
                for k in range(KC):
                    act.wait_ge(self.dve_ready.sem, self.dve_ready.at(KC + 2 + k))
                    nc.scalar.activation(self.res[:, k, 0:width], self.res[:, k, 0:width], ACT.Identity,
                                         bias=b[:, k:k + 1], scale=g[:, k:k + 1])

    def feed_forward(self, width, vectors):
        nc = self.nc
        with ExitStack() as ctx:
            hid = self.sb("ff_hid", [P, FC, width], ctx=ctx)
            sig = self.sb("ff_sig", [P, 2, width], ctx=ctx)
            n = self.plan_use([1] * FC)
            with self.stage() as block:
                @block.tensor
                def _(pe):
                    for f in range(FC):
                        w = self.take(pe)
                        if f >= 4:
                            pe.wait_ge(self.sums_taken.sem, self.sums_taken.at(f - 3))
                        for side in range(2):
                            for k in range(KC):
                                mm = nc.tensor.matmul(self.bank[2 * (f % 4) + side][:, 0:width],
                                                      w[:, k, P * side:P * side + P], self.h[:, k, 0:width],
                                                      start=(k == 0), stop=(k == KC - 1))
                        mm.then_inc(self.sums_ready.sem, self.sums_ready.one())

                @block.scalar
                def _(act):
                    for f in range(FC):
                        act.wait_ge(self.sums_ready.sem, self.sums_ready.at(f + 1))
                        if f >= 2:
                            act.wait_ge(self.sums_taken.sem, self.sums_taken.at(f - 1))
                        nc.scalar.activation(sig[:, f % 2, :], self.bank[2 * (f % 4)][:, 0:width],
                                                                 ACT.Sigmoid)\
                                                                     .then_inc(self.gate_ready.sem, self.gate_ready.one())

                @block.vector
                def _(dve):
                    nc.vector.tensor_scalar(self.res[:, :, 0:width], self.res[:, :, 0:width], ALPHA,
                                                              None, ALU.mult)\
                                                                  .then_inc(self.dve_step.sem, self.dve_step.one())
                    for f in range(FC):
                        s = sig[:, f % 2, :]
                        dve.wait_ge(self.gate_ready.sem, self.gate_ready.at(f + 1))
                        nc.vector.tensor_tensor(s, self.bank[2 * (f % 4)][:, 0:width], s, ALU.mult)\
                            .then_inc(self.dve_step.sem, self.dve_step.one())
                        dve.wait_ge(self.dve_step.sem, self.dve_step.count)
                        nc.vector.tensor_tensor(hid[:, f, :], self.bank[2 * (f % 4) + 1][:, 0:width],
                                                                    s, ALU.mult)\
                                                                        .then_inc(self.sums_taken.sem, self.sums_taken.one())

                @block.sync
                def _(sp):
                    self.refill(sp, n)

            n = self.plan_use([1] * 12)
            with self.stage() as block:
                @block.tensor
                def _(pe):
                    for i in range(4):
                        for k0, k1 in PIECES:
                            w = self.take(pe)
                            for d in (2 * i, 2 * i + 1):
                                for k in range(k0, k1):
                                    mm = nc.tensor.matmul(self.bank[d][:, 0:width],
                                                          w[:, k - k0, P * (d % 2):P * (d % 2) + P], hid[:, k, :],
                                                          start=(k == 0), stop=(k == FC - 1))
                            mm.then_inc(self.sums_ready.sem, self.sums_ready.one())

                @block.vector
                def _(dve):
                    for d in range(KC):
                        dve.wait_ge(self.sums_ready.sem, self.sums_ready.at(3 * (d // 2) + 3))
                        for v in range(vectors):
                            r = self.res[:, d, S * v:S * v + S]
                            nc.vector.scalar_tensor_tensor(r, self.bank[d][:, S * v:S * v + S],
                                                           self.mod[:, 5, d, v:v + 1], r, ALU.mult, ALU.add)

                @block.sync
                def _(sp):
                    self.refill(sp, n)

    def neighbour_window(self, bias, l):
        nc = self.nc
        with self.stage() as block:
            @block.sync
            def _(sp):
                self.load(sp, bias[:, :, :, :], self.dram["na_bias"][l])
                sp.wait_ge(self.loaded, self.n_loaded)

            @block.vector
            def _(dve):
                dve.wait_ge(self.loaded, self.n_loaded)
                mask = self.tab("colneg").unsqueeze(1).to_broadcast([P, HEADS * 4, 64])
                for t in range(2):
                    v = bias[:, t, :, :].rearrange("p h (r c) -> p (h r) c", c=64)
                    nc.vector.tensor_tensor(v, v, mask, ALU.add)

    def linear_and_norms(self, tok, vz, tiles, l):
        nc = self.nc
        with ExitStack() as ctx, self.stage() as block:
            sq = self.sb("nn_sq", [P, 8, HD], ctx=ctx)
            rot = self.sb("nn_rot", [P, 8, HD], ctx=ctx)
            ms = self.sb("nn_ms", [P, 4, 8], ctx=ctx)
            heads = lambda t: tok[:, t, GAQ:GAQ + 8 * HD].rearrange("p (h d) -> p h d", d=HD)

            @block.gpsimd
            def _(pool):
                nc.gpsimd.memset(vz[:, :, :, :], 0.0).then_inc(self.pool_step.sem, self.pool_step.one())
                pool.wait_ge(self.pool_step.sem, self.pool_step.count)
                for t in range(4):
                    for q in range(2):
                        v = tok[:, t, GLV:GLV + 256].rearrange("p (a b d) -> p a b d", b=2, d=GDV)[:, :, q, :]
                        nc.gpsimd.tensor_copy(vz[:, t, q:4:2, GDV * q:GDV * q + GDV], v)\
                            .then_inc(self.pool_step.sem, self.pool_step.one())
                pool.wait_ge(self.pool_step.sem, self.pool_step.count)

            @block.scalar
            def _(act):
                act.wait_ge(self.dve_ready.sem, self.dve_ready.at(1))
                m = ms[:, 0:tiles, :]
                nc.scalar.activation(m, m, ACT.Ln).then_inc(self.act_step.sem, self.act_step.one())
                act.wait_ge(self.act_step.sem, self.act_step.count)
                nc.scalar.activation(m, m, ACT.Exp, scale=-0.5).then_inc(self.act_ready.sem, self.act_ready.one())

            @block.vector
            def _(dve):
                step = self.dve_step
                for t in range(tiles):
                    nc.vector.tensor_tensor(sq[:, :, :], heads(t), heads(t), ALU.mult)\
                        .then_inc(step.sem, step.one())
                    dve.wait_ge(step.sem, step.count)
                    nc.vector.reduce_sum(ms[:, t, :], sq[:, :, :], AX_X).then_inc(step.sem, step.one())
                    dve.wait_ge(step.sem, step.count)
                m = ms[:, 0:tiles, :]
                nc.vector.tensor_scalar(m, m, 1.0 / HD, EPS_RMS, ALU.mult, ALU.add)\
                    .then_inc(self.dve_ready.sem, self.dve_ready.one())
                for t in range(tiles):
                    q = tok[:, t, NAQ:NAQ + 384]
                    nc.vector.tensor_scalar(q, q, HD ** -0.5, None, ALU.mult).then_inc(step.sem, step.one())
                dve.wait_ge(self.act_ready.sem, self.act_ready.at(1))
                nc.vector.tensor_scalar(ms[:, 0:tiles, 0:6], ms[:, 0:tiles, 0:6], HD ** -0.5, None, ALU.mult)\
                    .then_inc(step.sem, step.one())
                dve.wait_ge(step.sem, step.count)
                for t in range(tiles):
                    x = heads(t)
                    nc.vector.tensor_tensor(
                        x, x, ms[:, t, :].unsqueeze(2).to_broadcast([P, 8, HD]), ALU.mult)\
                            .then_inc(step.sem, step.one())
                    dve.wait_ge(step.sem, step.count)
                    for a, b, g in ((0, 6, "qn"), (6, 8, "kn")):
                        nc.vector.tensor_tensor(x[:, a:b, :], x[:, a:b, :],
                                                         self.vec(f"{g}{l}").unsqueeze(1).to_broadcast([P, b - a, HD]),
                                                         ALU.mult).then_inc(step.sem, step.one())
                    dve.wait_ge(step.sem, step.count)
                    if t >= 2:
                        continue
                    cos = self.tab("cos")[:, HD * t:HD * t + HD].unsqueeze(1).to_broadcast([P, 8, HD])
                    for half in range(2):
                        for axis in range(2):
                            c0, c1 = 32 * axis + 16 * half, 32 * axis + 16 * (1 - half)
                            sin = self.tab("sin")[:, HD * t + c0:HD * t + c0 + 16].unsqueeze(1).to_broadcast([P, 8, 16])
                            nc.vector.tensor_tensor(rot[:, :, c0:c0 + 16], x[:, :, c1:c1 + 16], sin, ALU.mult)\
                                .then_inc(step.sem, step.one())
                    dve.wait_ge(step.sem, step.count)
                    nc.vector.tensor_tensor(x, x, cos, ALU.mult).then_inc(step.sem, step.one())
                    dve.wait_ge(step.sem, step.count)
                    nc.vector.tensor_tensor(x, x, rot[:, :, :], ALU.add).then_inc(step.sem, step.one())
                    dve.wait_ge(step.sem, step.count)

    def linear_attention(self, l, streams, gq, gk, gg, lr, tok, vz):
        nc = self.nc
        with ExitStack() as ctx:
            cum = self.sb("gl_cum", [P, 2, 2, S + 1], ctx=ctx)
            state = self.sb("gl_state", [P, 2, 2 * P], ctx=ctx)
            levels = self.sb("gl_levels", [P, 2, 7, P], ctx=ctx)
            self.gates_and_ends(l, lr, gk, tok, cum, state, levels)
            for s in streams:
                self.linear_stream(l, s, gq, gk, gg, vz, cum, state, levels)

    def gates_and_ends(self, l, lr, gk, tok, cum, state, levels):
        nc = self.nc
        with ExitStack() as ctx:
            wa = self.sb("gl_wa", [32, 2, P], ctx=ctx)
            gate = self.sb("gl_gate", [P, 2, 2 * S], ctx=ctx)
            tmp = self.sb("gl_tmp", [P, 2, 2 * S], ctx=ctx)
            kend = self.sb("gl_kend", [P, 2, S], ctx=ctx)
            kend_t = self.sb("gl_kend_t", [P, 2, 2, P], ctx=ctx)
            with self.stage() as block:
                @block.sync
                def _(sp):
                    self.load(sp, levels[:, :, :, :].rearrange("p e m t -> p (e m t)"), self.dram["levels"])
                    sp.wait_ge(self.pool_ready.sem, self.pool_ready.at(1))
                    for e in range(2):
                        self.load(sp, wa[16 * e:16 * e + 16, e, :], self.dram["gla_wa2_2"][l, e])
                    sp.wait_ge(self.loaded, self.n_loaded)

                @block.gpsimd
                def _(pool):
                    nc.gpsimd.memset(wa[:, :, :], 0.0).then_inc(self.pool_ready.sem, self.pool_ready.one())
                    nc.gpsimd.memset(cum[:, :, :, 0:1], 0.0).then_inc(self.pool_ready.sem, self.pool_ready.one())
                    pool.wait_ge(self.pool_ready.sem, self.pool_ready.at(2))

                @block.tensor
                def _(pe):
                    pe.wait_ge(self.loaded, self.n_loaded)
                    for e in range(2):
                        mm = nc.tensor.matmul(self.bank[e][:, :], wa[:, e, :], lr, start=True, stop=True)
                    mm.then_inc(self.pe_ready.sem, self.pe_ready.one())

                @block.scalar
                def _(act):
                    act.wait_ge(self.dve_ready.sem, self.dve_ready.at(1))
                    nc.scalar.activation(tmp[:, :, :], tmp[:, :, :], ACT.Exp, scale=-1.0)\
                        .then_inc(self.act_step.sem, self.act_step.one())
                    act.wait_ge(self.act_step.sem, self.act_step.count)
                    nc.scalar.activation(tmp[:, :, :], tmp[:, :, :], ACT.Ln, bias=1.0)\
                        .then_inc(self.act_ready.sem, self.act_ready.one())

                @block.vector
                def _(dve):
                    step = self.dve_step
                    dve.wait_ge(self.pe_ready.sem, self.pe_ready.at(1))
                    for e in range(2):
                        nc.vector.tensor_scalar(gate[:, e, :], self.bank[e][:, :],
                                                         self.vec(f"gla_ba{l}")[:, e:e + 1], None, ALU.add)\
                                                             .then_inc(step.sem, step.one())
                    dve.wait_ge(step.sem, step.count)
                    nc.vector.scalar_tensor_tensor(tmp[:, :, :], gate[:, :, :], -1.0,
                                                                      gate[:, :, :], ALU.mult, ALU.max)\
                                                                          .then_inc(self.dve_ready.sem, self.dve_ready.one())
                    dve.wait_ge(self.act_ready.sem, self.act_ready.at(1))
                    flat = lambda x: x[:, :, :].rearrange("p e t -> p (e t)")
                    nc.vector.scalar_tensor_tensor(flat(gate), flat(gate), 0.0, flat(tmp), ALU.min,
                                                                  ALU.subtract).then_inc(step.sem, step.one())
                    dve.wait_ge(step.sem, step.count)
                    nc.vector.tensor_scalar(flat(gate), flat(gate), 1.0 / 16.0, None, ALU.mult)\
                        .then_inc(step.sem, step.one())
                    dve.wait_ge(step.sem, step.count)
                    dve.wait_ge(self.pool_ready.sem, self.pool_ready.at(2))
                    for e in range(2):
                        for s in range(2):
                            nc.vector.tensor_tensor_scan(cum[:, e, s, 1:S + 1], self.tab("ones"),
                                                                  gate[:, e, S * s:S * s + S], 0.0, ALU.mult, ALU.add)\
                                                                      .then_inc(step.sem, step.one())

            with self.stage() as block:
                @block.vector
                def _(dve):
                    step = self.dve_step
                    nc.vector.tensor_scalar(tmp[:, 0, 0:S], cum[:, 0, 1, 1:S + 1],
                                                           cum[:, 0, 1, S:S + 1], -1.0, ALU.subtract, ALU.mult)\
                                                               .then_inc(step.sem, step.one())
                    dve.wait_ge(step.sem, step.count)
                    nc.vector.tensor_copy(tmp[:, 1, 0:S], cum[:, 1, 1, 0:S])\
                        .then_inc(self.dve_ready.sem, self.dve_ready.one())
                    dve.wait_ge(self.act_ready.sem, self.act_ready.at(1))
                    for e in range(2):
                        nc.vector.tensor_tensor(kend[:, e, :], gk[:, S:2 * S], tmp[:, e, 0:S], ALU.mult)\
                            .then_inc(self.dve_ready.sem, self.dve_ready.one())
                    dve.wait_ge(self.pe_ready.sem, self.pe_ready.at(1))
                    nc.vector.tensor_copy(kend_t[:, :, :, :].rearrange("p e t d -> p (e t d)"),
                                                             self.bank[0][:, :])\
                                                                 .then_inc(self.dve_ready.sem, self.dve_ready.one())
                    dve.wait_ge(self.pe_ready.sem, self.pe_ready.at(2))
                    for e in range(2):
                        nc.vector.tensor_tensor(state[:, e, :], self.bank[1 + e][:, 0:2 * P], self.tab("headdiag"), ALU.mult)

                @block.scalar
                def _(act):
                    act.wait_ge(self.dve_ready.sem, self.dve_ready.at(1))
                    nc.scalar.activation(tmp[:, :, 0:S], tmp[:, :, 0:S], ACT.Exp)\
                        .then_inc(self.act_ready.sem, self.act_ready.one())

                @block.tensor
                def _(pe):
                    pe.wait_ge(self.dve_ready.sem, self.dve_ready.at(3))
                    for e in range(2):
                        for t in range(2):
                            mm = nc.tensor.transpose(self.bank[0][:, P * (2 * e + t):P * (2 * e + t) + P],
                                                     kend[:, e, P * t:P * t + P], self.tab("ident"))
                    mm.then_inc(self.pe_ready.sem, self.pe_ready.one())
                    pe.wait_ge(self.dve_ready.sem, self.dve_ready.at(4))
                    for e in range(2):
                        for t in range(2):
                            mm = nc.tensor.matmul(self.bank[1 + e][:, 0:2 * P], kend_t[:, e, t, :],
                                                  tok[:, 2 + t, GLV:GLV + 2 * P], start=(t == 0), stop=(t == 1))
                    mm.then_inc(self.pe_ready.sem, self.pe_ready.one())

    def linear_stream(self, l, s, gq, gk, gg, vz, cum, state, levels):
        nc = self.nc
        with ExitStack() as ctx:
            q4 = self.h[:, 0:2, :].rearrange("p c (a t) -> p (c a) t", t=S)
            decay = self.sb("gs_decay", [P, 2, 8, S], ctx=ctx)
            keys = self.sb("gs_keys", [P, 2, 8, S], ctx=ctx)
            moving = self.sb("gs_moving", [P, 2, GH, P], ctx=ctx)
            att = self.sb("gs_att", [P, 2, GH, S], ctx=ctx)
            carry = self.stat[:, :, 0:S]
            out = self.h[:, 5:8, :].rearrange("p x (c t) -> p x c t", t=S)
            q, k = gq[:, S * s:S * s + S], gk[:, S * s:S * s + S]
            hm = self.tab("headmask").unsqueeze(2).to_broadcast([P, GH, S])
            products = [(None, None, t, t) for t in range(2)] + [(0, 0, 1, 0), (1, 0, 0, 1)]
            products += [(e, i, t, t) for e in range(2) for i in range(1, 8) for t in range(2)]
            with self.stage() as block:
                @block.vector
                def _(dve):
                    step = self.dve_step
                    nc.vector.tensor_tensor(q4[:, :, :], q.unsqueeze(1).to_broadcast([P, GH, S]),
                                                               hm, ALU.mult)\
                                                                   .then_inc(self.dve_ready.sem, self.dve_ready.one())
                    for e in range(2):
                        b = cum[:, e, s, 1 - e:S + 1 - e]
                        for i, m in enumerate(LEVELS):
                            blocks = S // (2 * m)
                            border = cum[:, e, s, m:S:2 * m].unsqueeze(2).to_broadcast([P, blocks, 2 * m])
                            nc.vector.tensor_tensor(
                                decay[:, e, i, :].rearrange("p (b w) -> p b w", w=2 * m),
                                b.rearrange("p (b w) -> p b w", w=2 * m), border, ALU.subtract)\
                                    .then_inc(step.sem, step.one())
                        dve.wait_ge(step.sem, step.count)
                        nc.vector.scalar_tensor_tensor(decay[:, e, :, :], decay[:, e, :, :], -1.0,
                                                                          decay[:, e, :, :], ALU.mult, ALU.max)\
                                                                              .then_inc(self.dve_ready.sem, self.dve_ready.one())
                    for e in range(2):
                        dve.wait_ge(self.act_ready.sem, self.act_ready.at(e + 1))
                        nc.vector.tensor_tensor(
                            keys[:, e, :, :], k.unsqueeze(1).to_broadcast([P, 8, S]), decay[:, e, :, :], ALU.mult)\
                                .then_inc(self.dve_ready.sem, self.dve_ready.one())
                    for g, (e, i, t, sp) in enumerate(products):
                        dst = att[:, sp, :, P * t:P * t + P]
                        src = self.bank[g % 4][:, :].rearrange("p (h t) -> p h t", t=P)
                        dve.wait_ge(self.sums_ready.sem, self.sums_ready.at(g + 1))
                        if e is None:
                            mask = self.tab("ident2").unsqueeze(1).to_broadcast([P, GH, P])
                            o = nc.vector.tensor_tensor(dst, src, mask, ALU.mult)
                        elif i == 0:
                            o = nc.vector.tensor_copy(dst, src)
                        else:
                            mask = levels[:, e, i - 1, :].bitcast(I32).unsqueeze(1).to_broadcast([P, GH, P])
                            if g >= 2:
                                dve.wait_ge(self.sums_taken.sem, self.sums_taken.at(g))
                            o = nc.vector.copy_predicated(dst, mask, src)
                        o.then_inc(self.sums_taken.sem, self.sums_taken.one())
                    if s == 0:
                        dve.wait_ge(self.act_ready.sem, self.act_ready.at(4))
                        for e in range(2):
                            nc.vector.tensor_tensor(carry[:, e, :], carry[:, e, :], q, ALU.mult)\
                                .then_inc(step.sem, step.one())
                        dve.wait_ge(step.sem, step.count)
                        nc.vector.tensor_scalar(carry[:, :, :], carry[:, :, :], GDK ** -0.5, None,
                                                                   ALU.mult)\
                                                                       .then_inc(self.dve_ready.sem, self.dve_ready.one())
                    else:
                        nc.vector.tensor_copy(carry[:, 0, 0:1], q[:, 0:1])\
                            .then_inc(self.dve_ready.sem, self.dve_ready.one())
                    dve.wait_ge(self.pe_ready.sem, self.pe_ready.at(1))
                    o = self.bank[4][:, :].rearrange("p (c t) -> p c t", t=S)
                    nc.vector.tensor_copy(out[:, 0, :, :], o).then_inc(step.sem, step.one())
                    dve.wait_ge(step.sem, step.count)
                    nc.vector.tensor_tensor(out[:, 1, :, :], out[:, 0, :, :], out[:, 0, :, :], ALU.mult)\
                        .then_inc(self.dve_ready.sem, self.dve_ready.one())
                    dve.wait_ge(self.pe_ready.sem, self.pe_ready.at(2))
                    nc.vector.tensor_scalar(
                        out[:, 1, :, :], self.bank[5][:, :].rearrange("p (c t) -> p c t", t=S), 1.0 / GDV, EPS_RMS,
                        ALU.mult, ALU.add).then_inc(self.dve_ready.sem, self.dve_ready.one())
                    flat = lambda x: out[:, x, :, :].rearrange("p c t -> p (c t)")
                    dve.wait_ge(self.act_ready.sem, self.act_ready.at(6 if s == 0 else 4))
                    nc.vector.scalar_tensor_tensor(flat(0), flat(0), self.vec(f"gla_nw{l}"), flat(1),
                                                                  ALU.mult, ALU.mult).then_inc(step.sem, step.one())
                    dve.wait_ge(step.sem, step.count)
                    g = gg[:, :, S * s:S * s + S]
                    nc.vector.tensor_tensor(out[:, 2, :, :], out[:, 2, :, :], g, ALU.mult)\
                        .then_inc(step.sem, step.one())
                    dve.wait_ge(step.sem, step.count)
                    nc.vector.tensor_tensor(self.h[:, 3:5, S * s:S * s + S], out[:, 0, :, :], out[:, 2, :, :], ALU.mult)

                @block.scalar
                def _(act):
                    for e in range(2):
                        act.wait_ge(self.dve_ready.sem, self.dve_ready.at(2 + e))
                        nc.scalar.activation(decay[:, e, :, :], decay[:, e, :, :], ACT.Exp, scale=-1.0)\
                            .then_inc(self.act_ready.sem, self.act_ready.one())
                    if s == 0:
                        nc.scalar.activation(carry[:, 0, :], cum[:, 0, s, 1:S + 1], ACT.Exp)\
                            .then_inc(self.act_ready.sem, self.act_ready.one())
                        nc.scalar.activation(carry[:, 1, :], cum[:, 1, s, 0:S], ACT.Exp, scale=-1.0,
                                                                bias=cum[:, 1, s, S:S + 1])\
                                                                    .then_inc(self.act_ready.sem, self.act_ready.one())
                    act.wait_ge(self.dve_ready.sem, self.dve_ready.at(8))
                    nc.scalar.activation(out[:, 1, :, :], out[:, 1, :, :], ACT.Ln)\
                        .then_inc(self.act_step.sem, self.act_step.one())
                    act.wait_ge(self.act_step.sem, self.act_step.count)
                    nc.scalar.activation(out[:, 1, :, :], out[:, 1, :, :], ACT.Exp, scale=-0.5)\
                        .then_inc(self.act_ready.sem, self.act_ready.one())
                    nc.scalar.activation(out[:, 2, :, :], gg[:, :, S * s:S * s + S], ACT.Sigmoid)\
                        .then_inc(self.act_ready.sem, self.act_ready.one())

                @block.gpsimd
                def _(pool):
                    pool.wait_ge(self.dve_ready.sem, self.dve_ready.at(1))
                    for g, (e, i, t, sp) in enumerate(products[2:]):
                        if i == 0 or (g >= 2 and i == 1 and t == 0):
                            pool.wait_ge(self.dve_ready.sem, self.dve_ready.at(4 + e))
                        if g >= 2:
                            pool.wait_ge(self.sums_ready.sem, self.sums_ready.at(g + 1))
                        nc.gpsimd.tensor_tensor(
                            moving[:, g % 2, :, :], q4[:, :, P * t:P * t + P],
                            decay[:, e, i, P * t:P * t + P].unsqueeze(1).to_broadcast([P, GH, P]), ALU.mult)\
                                .then_inc(self.pool_ready.sem, self.pool_ready.one())
                    pool.wait_ge(self.pool_ready.sem, self.pool_ready.count)

                @block.tensor
                def _(pe):
                    pe.wait_ge(self.dve_ready.sem, self.dve_ready.at(1))
                    for g, (e, i, t, sp) in enumerate(products):
                        if g >= 4:
                            pe.wait_ge(self.sums_taken.sem, self.sums_taken.at(g - 3))
                        if e is None:
                            lhs, rhs = k[:, P * sp:P * sp + P], q4[:, :, P * t:P * t + P]
                        else:
                            pe.wait_ge(self.pool_ready.sem, self.pool_ready.at(g - 1))
                            if i == 0:
                                pe.wait_ge(self.dve_ready.sem, self.dve_ready.at(4 + e))
                            lhs, rhs = keys[:, e, i, P * sp:P * sp + P], moving[:, g % 2, :, :]
                        nc.tensor.matmul(self.bank[g % 4][:, :].rearrange("p (h t) -> p h t", t=P),
                                                             lhs, rhs, start=True, stop=True)\
                                                                 .then_inc(self.sums_ready.sem, self.sums_ready.one())
                    pe.wait_ge(self.sums_taken.sem, self.sums_taken.at(len(products)))
                    pe.wait_ge(self.dve_ready.sem, self.dve_ready.at(6))
                    for c in range(2):
                        o = self.bank[4][:, S * c:S * c + S]
                        last = None
                        terms = [(vz[:, 2 * s + sp, h, :], att[:, sp, h, :]) for sp in range(2) for h in (2 * c, 2 * c + 1)]
                        if s == 0:
                            terms += [(state[:, e, P * c:P * c + P], carry[:, e, :]) for e in range(2)]
                        for x, (lhs, rhs) in enumerate(terms):
                            mm = nc.tensor.matmul(o, lhs, rhs, start=(x == 0), stop=(x == len(terms) - 1))
                    mm.then_inc(self.pe_ready.sem, self.pe_ready.one())
                    pe.wait_ge(self.dve_ready.sem, self.dve_ready.at(7))
                    nc.tensor.matmul(self.bank[5][:, :], self.tab("halves"), out[:, 1, :, :],
                                                       start=True, stop=True)\
                                                           .then_inc(self.pe_ready.sem, self.pe_ready.one())

    def second_block(self):
        nc = self.nc
        for l in range(LAYERS):
            context_out = l < LAYERS - 1
            v = 2 if context_out else 1
            width = S * v
            self.modulation("cc", f"b_ada{l}", 2)
            self.modulate(2 * S, 2, 0, 1)
            with ExitStack() as ctx:
                tok = self.sb(f"b2_tok{l}", [P, 4, TOKW], ctx=ctx)
                gq = self.sb(f"b2_gq{l}", [P, 2 * S], ctx=ctx)
                gk = self.sb(f"b2_gk{l}", [P, 2 * S], ctx=ctx)
                gg = self.sb(f"b2_gg{l}", [P, 2, 2 * S], ctx=ctx)
                lr = self.sb(f"b2_lr{l}", [32, 2 * S], ctx=ctx)
                feat = [gq[:, :], gk[:, :], gg[:, 0, :], gg[:, 1, :], lr[:, :]]
                layout = [[((0, w), "tok", c0)] for c0, w in IN2[:5]]
                layout += [[((0, P), "feat", 0), ((P, CW), "feat", 1)], [((0, CW), "tok", GLV)],
                           [((0, P), "feat", 2), ((P, CW), "feat", 3)], [((0, 32), "feat", 4)]]
                layout += [[((0, w), "tok", c0 - 1952 + GAQ)] for c0, w in IN2[9:]]
                self.project(layout, 2 * S, tok, feat)
                with ExitStack() as inner:
                    vz = self.sb(f"b2_vz{l}", [P, 4, GH, P], ctx=inner)
                    self.linear_and_norms(tok, vz, 4, l)
                    self.linear_attention(l, (1, 0) if context_out else (0,), gq[:, :], gk[:, :], gg, lr[:, :], tok, vz)
                ytok = self.sb(f"b2_y{l}", [P, 4, HEADS * HD], ctx=ctx)
                bias = self.sb(f"b2_bias{l}", [P, 2, HEADS, S], ctx=ctx)
                self.neighbour_window(bias, l)
                for kind in range(2):
                    with ExitStack() as inner:
                        nk = HEADS if kind == 0 else KV_HEADS
                        qk = self.sb(f"b2_qk{l}{kind}", [HD, HEADS + nk, 2 * S], ctx=inner)
                        q0 = NAQ if kind == 0 else GAQ
                        v0 = NAV if kind == 0 else GAV
                        self.transposes([([tok[:, t, q0 + HD * h:q0 + HD * h + HD] for t in range(4)], HD, qk[:, h, :])
                                         for h in range(HEADS + nk)])
                        units = []
                        for h in range(HEADS):
                            kv = h if kind == 0 else h // (HEADS // KV_HEADS)
                            for t in range(2 * v):
                                k0 = 0 if t < 2 else 2
                                units.append(dict(
                                    q=qk[:, h, P * t:P * t + P], key=qk[:, HEADS + kv, P * k0:2 * S],
                                    add=[(bias[:, t, h, :], 0)] if kind == 0 and t < 2 else [], hide=None,
                                    values=[tok[:, b, v0 + HD * kv:v0 + HD * kv + HD] for b in range(k0, 4)],
                                    out=ytok[:, t, HD * h:HD * h + HD]))
                        self.attention(units, f"b2a{l}{kind}")
                        self.transposes([([ytok[:, t, P * c:P * c + P] for t in range(2 * v)], P,
                                          self.h[:, 5 * kind + c, 0:width]) for c in range(3)])
            self.out_project(width, v, True)
            self.layer_norm(width, "ln1_g", "ln1_b", l)
            self.modulate(width, v, 3, 4)
            self.feed_forward(width, v)
            self.layer_norm(width, "ln2_g", "ln2_b", l)

    def finish(self):
        nc = self.nc
        with self.stage() as block:
            @block.sync
            def _(sp):
                self.load(sp, self.dram["out"], self.res[:, :, 0:S])
                sp.wait_ge(self.loaded, self.n_loaded)


def hybrid_then_latent_kernel(nc, dram, where, twhere):
    b = Builder(nc, dram, where)
    b.twhere = twhere
    with b.ctx:
        b.allocate()
        b.plan_chunks()
        b.start()
        b.first_block()
        b.second_block()
        b.finish()


_WHOLE = ["w_ada", "w_in", "w_out", "w_mlp1", "w_mlp2", "b_mlp2", "w_ada_2", "w_in_2", "gla_wa2_2", "w_out_2",
          "w_ffn_in_2", "w_ffn_out_2"]


def kernel(**inputs):
    import concourse.bacc as bacc
    from concourse.bass_utils import run_bass_kernel_spmd as run

    inputs = {k: np.asarray(v) for k, v in inputs.items()}
    tokens = lambda a: np.ascontiguousarray(a[0].T.reshape(KC, P, S).transpose(1, 0, 2))
    arrays = {n: np.ascontiguousarray(inputs[n]) for n in _WHOLE}
    arrays["x"], arrays["ctx"] = tokens(inputs["x"]), tokens(inputs["ctx_2"])
    arrays["vecs"], where = pack(packed_vectors(inputs))
    arrays["tables"], twhere = pack(shape_tables())
    arrays["levels"] = level_masks()
    arrays["na_bias"] = neighbour_bias(inputs["na_rpb_2"])
    nc = bacc.Bacc("TRN2", target_bir_lowering=False, num_devices=1)
    dram = {n: nc.dram_tensor(f"in_{n}", a.shape, mybir.dt.from_np(a.dtype), kind="ExternalInput").ap()
            for n, a in arrays.items()}
    dram["out"] = nc.dram_tensor("out_0", (P, KC, S), F32, kind="ExternalOutput").ap()
    hybrid_then_latent_kernel(nc, dram, where, twhere)
    r = run(nc, [{f"in_{n}": a for n, a in arrays.items()}], core_ids=[0])
    out = r.results[0]["out_0"]
    return np.ascontiguousarray(out.transpose(1, 0, 2).reshape(D, S).T)[None]
```

```python
from contextlib import ExitStack, contextmanager

import numpy as np
import concourse.bass as bass
from concourse import mybir

F32 = mybir.dt.float32
F32R = mybir.dt.float32r
U32 = mybir.dt.uint32
I32 = mybir.dt.int32
ALU = mybir.AluOpType
ACT = mybir.ActivationFunctionType
AX_X = mybir.AxisListType.X

P = 128
D = 1024
KC = D // P
S = 256
HD = 64
HEADS = 6
CONV = 256
EXPERTS = 32
TOPK = 4
HIDDEN = 2816
FC = HIDDEN // P
LAYERS = 2
GH, GDK, GDV = 4, 32, 64
KV_HEADS = 2
LEVELS = (128, 64, 32, 16, 8, 4, 2, 1)
EPS_RMS = 1e-6
EPS_LN = 1e-5
ALPHA = (2.0 * LAYERS) ** 0.25
NEG = -1e30
SWIGLU_LIMIT = 7.0
SWIGLU_ALPHA = 1.702
PARTS = 2
PIECES = ((0, 6), (6, 11))
SLOTS = 4
CW = 256

NAQ, NAK, NAV, GLV, GAQ, GAK, GAV, TOKW = 0, 384, 768, 1152, 1408, 1792, 1920, 2048
IN2 = [(0, 256), (256, 256), (512, 256), (768, 256), (1024, 128), (1152, 256), (1408, 256), (1664, 256),
       (1920, 32), (1952, 256), (2208, 256), (2464, 128)]


def shape_tables():
    i = np.arange(P)
    f = np.float32
    t = {
        "ident": np.eye(P, dtype=f),
        "ident2": 2 * np.eye(P, dtype=f),
        "upto": (i[:, None] <= i[None, :]).astype(f),
        "ones": np.ones((P, 256), f),
        "halves": (i[:, None] // 64 == i[None, :] // 64).astype(f),
        "headmask": ((i[:, None] // GDK == np.arange(GH)[None, :]) * GDK ** -0.5).astype(f),
        "headdiag": (i[:, None] // GDK == np.arange(GH * GDV)[None, :] // GDV).astype(f),
        "iota": np.tile(np.arange(EXPERTS, dtype=f), (P, 1)),
    }
    z = np.zeros((P, P), f)
    causal = i[None, :] <= i[:, None]
    strict = i[None, :] < i[:, None]
    t["causal"] = np.concatenate([z, np.where(causal, 0, NEG)], 1).astype(f)
    t["strictneg"] = np.concatenate([z, np.where(strict, 0, NEG)], 1).astype(f)
    t["strict01"] = np.concatenate([z + 1, strict], 1).astype(f)
    c, k = i % 64, np.arange(64)
    lo = np.clip(c - 8, 0, 48)
    t["colneg"] = np.where((k >= lo[:, None]) & (k < lo[:, None] + 16), 0, NEG).astype(f)
    cosr, sinr = [], []
    inv = 10000.0 ** (-np.arange(16, dtype=f) / 16)
    for tile in range(2):
        tok = tile * P + i
        r, cc = (tok // 64).astype(f)[:, None] * inv, (tok % 64).astype(f)[:, None] * inv
        ang = np.concatenate([r, r, cc, cc], 1).astype(f)
        sign = np.where((np.arange(64) // 16) % 2 == 0, -1, 1).astype(f)
        cosr.append(np.cos(ang))
        sinr.append(np.sin(ang) * sign)
    t["cos"] = np.concatenate(cosr, 1).astype(f)
    t["sin"] = np.concatenate(sinr, 1).astype(f)
    return t


def level_masks():
    i, t = np.arange(P), {}
    for direction in range(2):
        for m in LEVELS[1:]:
            s_even = (i[:, None] // m) % 2 == 0
            t_odd = (i[None, :] // m) % 2 == 1
            mask = s_even & t_odd & (i[:, None] // (2 * m) == i[None, :] // (2 * m))
            t[f"level{direction}_{m}"] = (mask if direction == 0 else mask.T).astype(np.float32)
    return np.concatenate(list(t.values()), axis=1)


def pack(parts):
    at, where = 0, {}
    for name, a in parts.items():
        where[name] = (at, a.shape[1])
        at += a.shape[1]
    return np.ascontiguousarray(np.concatenate(list(parts.values()), axis=1)), where


def feature_columns(v):
    return np.asarray(v).reshape(-1, P).T


def row(v):
    return np.tile(np.asarray(v).reshape(1, -1), (P, 1))


def packed_vectors(a):
    v = {
        "c": feature_columns(a["c"][0]),
        "cc": np.stack([feature_columns(a["c_2"][0]), feature_columns(a["c_ctx_2"])], 2).reshape(P, -1),
        "norm1_g": feature_columns(a["norm1_g"][0]),
        "norm2_g": feature_columns(a["norm2_g"][0]),
        "out_norm_g": feature_columns(a["out_norm_g"][0]),
        "b_ada": feature_columns(a["b_ada"][0]),
        "conv_w": a["conv_w"][0].reshape(3, 2, P).transpose(2, 1, 0).reshape(P, 6),
        "b_glu": a["b_mlp1"][0][:, ::2].reshape(EXPERTS * KC, P).T,
        "b_lin": a["b_mlp1"][0][:, 1::2].reshape(EXPERTS * KC, P).T,
        "router_b": row(a["router_b"][0]),
        "router_w": a["router_w"][0].reshape(KC, P, EXPERTS).transpose(1, 0, 2).reshape(P, -1),
        "w_f": a["w_in"][0][:, 3072:3078].reshape(KC, P, 6).transpose(1, 0, 2).reshape(P, -1),
        "f_b": row(a["fox_f_b"][0]),
        "sb_q_g": row(a["sb_q_g"][0]), "sb_k_g": row(a["sb_k_g"][0]),
        "fox_q_g": row(a["fox_q_g"][0]), "fox_k_g": row(a["fox_k_g"][0]),
    }
    for l in range(LAYERS):
        v[f"b_ada{l}"] = feature_columns(a["b_ada_2"][l])
        v[f"gla_ba{l}"] = a["gla_ba_2"][l].T
        v[f"gla_nw{l}"] = np.tile(a["gla_norm_w_2"][l], 2).reshape(P, 1)
        v[f"qn{l}"] = row(a["gqa_qnorm_w_2"][l])
        v[f"kn{l}"] = row(a["gqa_knorm_w_2"][l])
        for n in ("ln1_g", "ln1_b", "ln2_g", "ln2_b"):
            v[f"{n}{l}"] = feature_columns(a[n + "_2"][l])
    return v


def neighbour_bias(rpb):
    q, k = np.arange(S)[:, None], np.arange(S)[None, :]
    dr = k // 64 - q // 64 + 7
    dc = np.clip(k % 64 - q % 64, -15, 15) + 15
    b = np.asarray(rpb)[:, :, dr, dc]
    return np.ascontiguousarray(b.reshape(LAYERS, HEADS, 2, P, S).transpose(0, 3, 2, 1, 4))


def rows(w):
    return w.rearrange("(c p) n -> p c n", p=P)


class Counter:

    def __init__(self, sem):
        self.sem, self.base, self.count = sem, 0, 0

    def one(self):
        self.count += 1
        return 1

    def at(self, n):
        return self.base + n


class Builder:
    def __init__(self, nc, dram, where):
        self.nc, self.dram, self.where = nc, dram, where
        self.ctx = ExitStack()
        self.counters = []
        self.names = {}

    def sb(self, name, shape, dt=F32, ctx=None):
        self.names[name] = self.names.get(name, 0) + 1
        if self.names[name] > 1:
            name += f"_{self.names[name]}"
        return (ctx or self.ctx).enter_context(self.nc.sbuf_tensor(name, shape, dt))

    def counter(self, name):
        s = Counter(self.ctx.enter_context(self.nc.semaphore(name)))
        self.counters.append(s)
        return s

    @contextmanager
    def stage(self):
        with self.nc.Block(no_gpsimd_drain=True) as block:
            yield block
        for s in self.counters:
            s.base = s.count

    def vec(self, name):
        at, n = self.where[name]
        return self.vecs[:, at:at + n]

    def tab(self, name):
        at, n = self.twhere[name]
        return self.tables[:, at:at + n]

    def allocate(self):
        nc = self.nc
        self.bank = [self.ctx.enter_context(nc.psum_tensor(f"bank{i}", [P, 512], F32)) for i in range(8)]
        self.ring = self.sb("ring", [P, SLOTS, KC, CW])
        self.landed = [self.ctx.enter_context(nc.semaphore(f"landed{i}")) for i in range(SLOTS)]
        self.loaded = self.ctx.enter_context(nc.semaphore("loaded"))
        self.n_loaded = 0
        self.sums_ready = self.counter("sums_ready")
        self.hi_ready = self.counter("hi_ready")
        self.lo_ready = self.counter("lo_ready")
        self.xhi_ready = self.counter("xhi_ready")
        self.xlo_ready = self.counter("xlo_ready")
        self.sums_taken = self.counter("sums_taken")
        self.pe_ready = self.counter("pe_ready")
        self.dve_ready = self.counter("dve_ready")
        self.act_ready = self.counter("act_ready")
        self.pool_ready = self.counter("pool_ready")
        self.dve_step = self.counter("dve_step")
        self.act_step = self.counter("act_step")
        self.pool_step = self.counter("pool_step")
        self.scores_ready = self.counter("scores_ready")
        self.logits_ready = self.counter("logits_ready")
        self.mass_ready = self.counter("mass_ready")
        self.probs_ready = self.counter("probs_ready")
        self.turned = self.counter("turned")
        self.turned_copied = self.counter("turned_copied")
        self.mixed = self.counter("mixed")
        self.mixed_taken = self.counter("mixed_taken")
        self.glu_ready = self.counter("glu_ready")
        self.gate_ready = self.counter("gate_ready")
        self.hidden_ready = self.counter("hidden_ready")
        self.vecs = self.sb("vecs", [P, self.dram["vecs"].shape[1]])
        self.tables = self.sb("tables", [P, self.dram["tables"].shape[1]])
        self.res = self.sb("res", [P, KC, 2 * S])
        self.h = self.sb("h", [P, KC, 2 * S])
        self.mod = self.sb("mod", [P, 6, KC, 2])
        self.cond = self.sb("cond", [P, KC, 2])
        self.amp = self.sb("amp", [P, KC])
        self.stat = self.sb("stat", [P, 2, 512])

    def plan_chunks(self):
        d, plan, shape = self.dram, [], []

        def add(a, k0, kn, c0, width):
            half = (kn + 1) // 2
            plan.append([((slice(0, half), slice(0, width)), a[:, k0:k0 + half, c0:c0 + width]),
                         ((slice(half, kn), slice(0, width)), a[:, k0 + half:k0 + kn, c0:c0 + width])])
            shape.append((kn, width))

        for i in range(24):
            add(rows(d["w_ada"][0]), 0, KC, i * CW, CW)
        for i in range(12):
            add(rows(d["w_in"][0]), 0, KC, i * CW, CW)
        for i in range(4):
            add(rows(d["w_out"][0]), 0, KC, i * CW, CW)
        self.n_moe = len(plan)
        for e in range(EXPERTS):
            for j in range(8):
                add(rows(d["w_mlp1"][0, e]), 0, KC, j * CW, CW)
            for j in range(4):
                add(rows(d["w_mlp2"][0, e]), 0, KC, j * CW, CW)
        for l in range(LAYERS):
            for i in range(24):
                add(rows(d["w_ada_2"][l]), 0, KC, i * CW, CW)
            for c0, w in IN2:
                add(rows(d["w_in_2"][l]), 0, KC, c0, w)
            for i in range(4):
                add(rows(d["w_out_2"][l]), 0, KC, i * CW, CW)
            a, b = rows(d["w_ffn_in_2"][l]), rows(d["w_ffn_out_2"][l])
            for part in range(PARTS):
                for f in range(FC // PARTS * part, FC // PARTS * (part + 1)):
                    plan.append([((slice(0, 8), slice(P * s, P * s + P)),
                                  a[:, :, s * HIDDEN + f * P:s * HIDDEN + f * P + P]) for s in range(2)])
                    shape.append((KC, CW))
                for i in range(4):
                    for k0, k1 in PIECES:
                        add(b, FC // PARTS * part + k0, k1 - k0, i * CW, CW)
        self.plan, self.shape = plan, shape
        self.free_at = []
        self.done_at = []
        self.next_issue = 0
        self.next_use = 0

    def refill(self, sp, chunks):
        for n in range(self.next_issue, min(self.next_issue + chunks, len(self.plan))):
            if n >= SLOTS:
                counter, value = self.free_at[n - SLOTS]
                sp.wait_ge(counter.sem, value)
            for (kk, cc), src in self.plan[n]:
                sp.dma_start(self.ring[:, n % SLOTS, kk, cc], src).then_inc(self.landed[n % SLOTS], 16)
        self.next_issue += chunks

    def plan_use(self, groups, whole=()):
        v, split, first = self.sums_ready.count, self.lo_ready.count, self.next_use
        for x, g in enumerate(groups):
            v += g
            self.done_at.append(v)
            if x in whole:
                self.free_at.append((self.sums_ready, v))
            else:
                split += 1
                self.free_at.append((self.lo_ready, split))
        self.next_use += len(groups)
        return first

    def slot(self, n):
        kn, width = self.shape[n]
        return self.ring[:, n % SLOTS, 0:kn, 0:width], 32 * (n // SLOTS + 1)

    def split_buffers(self, name, depth, ctx):
        return [self.sb(f"{name}_{part}", [P, depth, KC, CW], F32R, ctx=ctx) for part in ("whi", "wlo")]

    def split_high(self, act, bufs, first, x):
        depth = bufs[0].shape[1]
        kn, width = self.shape[first + x]
        src, landed = self.slot(first + x)
        act.wait_ge(self.landed[(first + x) % SLOTS], landed)
        if x >= depth:
            act.wait_ge(self.sums_ready.sem, self.done_at[first + x - depth])
        self.nc.scalar.copy(bufs[0][:, x % depth, 0:kn, 0:width], src)\
            .then_inc(self.hi_ready.sem, self.hi_ready.one())

    def split_low(self, dve, bufs, first, x, nth):
        depth = bufs[0].shape[1]
        kn, width = self.shape[first + x]
        src, _ = self.slot(first + x)
        dve.wait_ge(self.hi_ready.sem, self.hi_ready.at(nth))
        self.nc.vector.tensor_tensor(bufs[1][:, x % depth, 0:kn, 0:width], src,
                                     bufs[0][:, x % depth, 0:kn, 0:width].bitcast(F32), ALU.subtract)\
            .then_inc(self.lo_ready.sem, self.lo_ready.one())

    def load(self, eng, dst, src):
        eng.dma_start(dst, src).then_inc(self.loaded, 16)
        self.n_loaded += 16

    def start(self):
        nc = self.nc
        with self.stage() as block:
            @block.sync
            def _(sp):
                self.load(sp, self.vecs[:, :], self.dram["vecs"])
                self.load(sp, self.tables[:, :], self.dram["tables"])
                self.load(sp, self.res[:, :, 0:S], self.dram["x"])
                self.load(sp, self.res[:, :, S:2 * S], self.dram["ctx"])
                self.refill(sp, SLOTS)
                sp.wait_ge(self.loaded, self.n_loaded)

    def modulation(self, cond, bias, nv):
        nc = self.nc
        c = self.cond[:, :, 0:nv]
        src = self.vec(cond).rearrange("p (k v) -> p k v", v=nv)
        out = self.bank[7][:, 0:48 * nv].rearrange("p (i v) -> p i v", v=nv)
        n = self.plan_use([1] * 24, whole=range(24))
        with ExitStack() as ctx, self.stage() as block:
            line = self.sb("mod_line", [nv, 24 * CW], ctx=ctx)

            @block.scalar
            def _(act):
                nc.scalar.activation(c, src, ACT.Sigmoid).then_inc(self.act_ready.sem, self.act_ready.one())
                for i in range(24):
                    act.wait_ge(self.sums_ready.sem, self.sums_ready.at(i + 1))
                    nc.scalar.copy(line[:, i * CW:(i + 1) * CW], self.bank[i % 4][0:nv, 0:CW])\
                        .then_inc(self.sums_taken.sem, self.sums_taken.one())

            @block.vector
            def _(dve):
                dve.wait_ge(self.act_ready.sem, self.act_ready.at(1))
                nc.vector.tensor_tensor(c, c, src, ALU.mult).then_inc(self.dve_ready.sem, self.dve_ready.one())
                dve.wait_ge(self.pe_ready.sem, self.pe_ready.at(1))
                b = self.vec(bias).unsqueeze(2).to_broadcast([P, 48, nv])
                m = self.mod[:, :, :, 0:nv].rearrange("p i c v -> p (i c) v")
                nc.vector.tensor_tensor(m, out, b, ALU.add)

            @block.tensor
            def _(pe):
                pe.wait_ge(self.dve_ready.sem, self.dve_ready.at(1))
                for i in range(25):
                    if i < 24:
                        w, landed = self.slot(n + i)
                        pe.wait_ge(self.landed[(n + i) % SLOTS], landed)
                        if i >= 4:
                            pe.wait_ge(self.sums_taken.sem, self.sums_taken.at(i - 3))
                        for k in range(KC):
                            mm = nc.tensor.matmul(self.bank[i % 4][0:nv, 0:CW], c[:, k, :], w[:, k, :],
                                                  start=(k == 0), stop=(k == KC - 1))
                        mm.then_inc(self.sums_ready.sem, self.sums_ready.one())
                    if i >= 1:
                        pe.wait_ge(self.sums_taken.sem, self.sums_taken.at(i))
                        for j in (2 * i - 2, 2 * i - 1):
                            mm = nc.tensor.transpose(out[:, j, :], line[:, P * j:P * j + P],
                                                     self.tab("ident")[0:nv, 0:nv])
                mm.then_inc(self.pe_ready.sem, self.pe_ready.one())

            @block.sync
            def _(sp):
                self.refill(sp, 24)

    def rms_modulate(self, gain, shift, scale):
        nc = self.nc
        total = self.bank[0][:, 0:S]
        rstd = self.stat[:, 0, 0:S]
        with self.stage() as block:
            @block.vector
            def _(dve):
                for k in range(KC):
                    nc.vector.tensor_tensor(self.h[:, k, S:2 * S], self.res[:, k, 0:S],
                                                               self.res[:, k, 0:S], ALU.mult)\
                                                                   .then_inc(self.dve_ready.sem, self.dve_ready.one())
                nc.vector.scalar_tensor_tensor(
                    self.amp[:, :], self.mod[:, scale, :, 0], 1.0, self.vec(gain), ALU.add, ALU.mult)\
                        .then_inc(self.dve_ready.sem, self.dve_ready.one())
                dve.wait_ge(self.pe_ready.sem, self.pe_ready.at(1))
                nc.vector.tensor_scalar(rstd, total, 1.0 / D, EPS_RMS, ALU.mult, ALU.add)\
                    .then_inc(self.dve_ready.sem, self.dve_ready.one())
                dve.wait_ge(self.act_ready.sem, self.act_ready.at(1))
                for k in range(KC):
                    nc.vector.tensor_tensor(self.h[:, k, 0:S], self.res[:, k, 0:S], rstd,
                                                               ALU.mult)\
                                                                   .then_inc(self.dve_ready.sem, self.dve_ready.one())

            @block.tensor
            def _(pe):
                for k in range(KC):
                    pe.wait_ge(self.dve_ready.sem, self.dve_ready.at(k + 1))
                    mm = nc.tensor.matmul(total, self.tab("ones")[:, 0:P], self.h[:, k, S:2 * S],
                                          start=(k == 0), stop=(k == KC - 1))
                mm.then_inc(self.pe_ready.sem, self.pe_ready.one())

            @block.scalar
            def _(act):
                act.wait_ge(self.dve_ready.sem, self.dve_ready.at(KC + 2))
                nc.scalar.activation(rstd, rstd, ACT.Ln).then_inc(self.act_step.sem, self.act_step.one())
                act.wait_ge(self.act_step.sem, self.act_step.count)
                nc.scalar.activation(rstd, rstd, ACT.Exp, scale=-0.5)\
                    .then_inc(self.act_ready.sem, self.act_ready.one())
                for k in range(KC):
                    act.wait_ge(self.dve_ready.sem, self.dve_ready.at(KC + 3 + k))
                    nc.scalar.activation(self.h[:, k, 0:S], self.h[:, k, 0:S], ACT.Identity,
                                         bias=self.mod[:, shift, k, 0:1], scale=self.amp[:, k:k + 1])

    def split_input(self, name, ctx, width):
        return [self.sb(f"{name}_{part}", [P, KC, width], F32R, ctx=ctx) for part in ("xhi", "xlo")]

    def input_high(self, act, x, width):
        for k in range(0, KC, 2):
            self.nc.scalar.copy(x[0][:, k:k + 2, :], self.h[:, k:k + 2, 0:width])\
                .then_inc(self.xhi_ready.sem, self.xhi_ready.one())

    def input_low(self, dve, x, width):
        for k in range(0, KC, 2):
            dve.wait_ge(self.xhi_ready.sem, self.xhi_ready.at(k // 2 + 1))
            self.nc.vector.tensor_tensor(x[1][:, k:k + 2, :], self.h[:, k:k + 2, 0:width],
                                         x[0][:, k:k + 2, :].bitcast(F32), ALU.subtract)\
                .then_inc(self.xlo_ready.sem, self.xlo_ready.one())

    def project(self, layout, width, tok, feat):
        nc = self.nc
        tiles = width // P
        chunks = len(layout)
        narrow = [i for i in range(chunks) if self.shape[self.next_use + i][1] < P]
        n = self.plan_use([sum(tiles if kind == "tok" else 1 for _, kind, _ in parts) for parts in layout],
                          whole=narrow)
        nth = {}
        for i in range(chunks):
            if i not in narrow:
                nth[i] = len(nth) + 1

        def groups():
            for i, parts in enumerate(layout):
                for cols, kind, place in parts:
                    for t in range(tiles if kind == "tok" else 1):
                        yield i, cols, kind, place, t

        with ExitStack() as ctx, self.stage() as block:
            bufs = self.split_buffers("pr", 2, ctx)
            x = self.split_input("pr", ctx, width)

            @block.tensor
            def _(pe):
                at = -1
                for g, (i, (c0, c1), kind, place, t) in enumerate(groups()):
                    if i != at:
                        at = i
                        if i in nth:
                            hi, lo = (b[:, i % 2, :, :] for b in bufs)
                            pe.wait_ge(self.lo_ready.sem, self.lo_ready.at(nth[i]))
                            if i == 0:
                                pe.wait_ge(self.xlo_ready.sem, self.xlo_ready.at(4))
                        else:
                            w, landed = self.slot(n + i)
                            pe.wait_ge(self.landed[(n + i) % SLOTS], landed)
                    if g >= 8:
                        pe.wait_ge(self.sums_taken.sem, self.sums_taken.at(g - 7))
                    if kind == "tok":
                        out = self.bank[g % 8][:, 0:c1 - c0]
                    else:
                        out = self.bank[g % 8][0:c1 - c0, 0:width]
                    for k in range(KC):
                        if i not in nth:
                            mm = nc.tensor.matmul(out, w[:, k, c0:c1], self.h[:, k, 0:width],
                                                  start=(k == 0), stop=(k == KC - 1))
                            continue
                        for term, (wp, xp) in enumerate(((hi, x[0]), (lo, x[0]), (hi, x[1]))):
                            wk, xk = wp[:, k, c0:c1], xp[:, k, P * t:P * t + P] if kind == "tok" else xp[:, k, :]
                            a, b = (xk, wk) if kind == "tok" else (wk, xk)
                            mm = nc.tensor.matmul(out, a, b, start=(k == 0 and term == 0),
                                                  stop=(k == KC - 1 and term == 2))
                    mm.then_inc(self.sums_ready.sem, self.sums_ready.one())

            @block.scalar
            def _(act):
                self.input_high(act, x, width)
                self.split_high(act, bufs, n, 0)
                at = -1
                for g, (i, (c0, c1), kind, place, t) in enumerate(groups()):
                    if i != at:
                        at = i
                        if i + 1 in nth:
                            self.split_high(act, bufs, n, i + 1)
                    act.wait_ge(self.sums_ready.sem, self.sums_ready.at(g + 1))
                    if kind == "tok":
                        cp = nc.scalar.copy(tok[:, t, place:place + c1 - c0], self.bank[g % 8][:, 0:c1 - c0])
                    else:
                        cp = nc.scalar.copy(feat[place], self.bank[g % 8][0:c1 - c0, 0:width])
                    cp.then_inc(self.sums_taken.sem, self.sums_taken.one())

            @block.vector
            def _(dve):
                self.input_low(dve, x, width)
                for i in nth:
                    self.split_low(dve, bufs, n, i, nth[i])

            @block.sync
            def _(sp):
                self.refill(sp, chunks)

    def transposes(self, jobs):
        nc = self.nc
        with self.stage() as block:
            @block.tensor
            def _(pe):
                for g, (sources, rows, _) in enumerate(jobs):
                    if g >= 8:
                        before = self.act_ready if g % 2 == 0 else self.dve_ready
                        pe.wait_ge(before.sem, before.at((g - 8) // 2 + 1))
                    for b, src in enumerate(sources):
                        mm = nc.tensor.transpose(self.bank[g % 8][0:rows, P * b:P * b + P], src, self.tab("ident"))
                    mm.then_inc(self.pe_ready.sem, self.pe_ready.one())

            @block.scalar
            def _(act):
                for g in range(0, len(jobs), 2):
                    sources, rows, dst = jobs[g]
                    act.wait_ge(self.pe_ready.sem, self.pe_ready.at(g + 1))
                    nc.scalar.copy(dst, self.bank[g % 8][0:rows, 0:P * len(sources)])\
                        .then_inc(self.act_ready.sem, self.act_ready.one())

            @block.vector
            def _(dve):
                for g in range(1, len(jobs), 2):
                    sources, rows, dst = jobs[g]
                    dve.wait_ge(self.pe_ready.sem, self.pe_ready.at(g + 1))
                    nc.vector.tensor_copy(dst, self.bank[g % 8][0:rows, 0:P * len(sources)])\
                        .then_inc(self.dve_ready.sem, self.dve_ready.one())

    def attention(self, units, name):
        nc = self.nc
        count = len(units)
        ident = self.tab("ident")
        S_, T_, O_ = self.bank[0:2], self.bank[2:4], self.bank[4:6]
        with ExitStack() as ctx, self.stage() as block:
            logits = self.sb(name + "_logits", [P, 2, S], ctx=ctx)
            soft = self.sb(name + "_soft", [P, 2, S], ctx=ctx)
            probs = self.sb(name + "_probs", [P, 2, 2 * S], ctx=ctx)
            turned = self.sb(name + "_turned", [P, 2, 2 * S], ctx=ctx)
            peak = self.sb(name + "_peak", [P, 2], ctx=ctx)
            mass = self.sb(name + "_mass", [P, 4], ctx=ctx)
            part = self.sb(name + "_part", [P, 2], ctx=ctx)
            sizes = [u["key"].shape[1] for u in units]

            @block.tensor
            def _(pe):
                for i in range(count + 2):
                    if i < count:
                        u = units[i]
                        mm = nc.tensor.matmul(S_[i % 2][:, 0:sizes[i]], u["q"], u["key"], start=True,
                                              stop=not u["add"], skip_group_check=True)
                        for x, (add, c0) in enumerate(u["add"]):
                            mm = nc.tensor.matmul(S_[i % 2][:, c0:c0 + add.shape[1]], ident, add, start=False,
                                                  stop=True, skip_group_check=True)
                        mm.then_inc(self.scores_ready.sem, self.scores_ready.one())
                    if 1 <= i <= count:
                        j = i - 1
                        pe.wait_ge(self.probs_ready.sem, self.probs_ready.at(j + 1))
                        if j >= 2:
                            pe.wait_ge(self.turned_copied.sem, self.turned_copied.at(j - 1))
                        for b in range(sizes[j] // P):
                            mm = nc.tensor.transpose(T_[j % 2][:, P * b:P * b + P],
                                                     probs[:, j % 2, P * b:P * b + P], ident)
                        mm.then_inc(self.turned.sem, self.turned.one())
                    if i >= 2:
                        j = i - 2
                        nb = sizes[j] // P
                        pe.wait_ge(self.turned_copied.sem, self.turned_copied.at(j + 1))
                        if j >= 2:
                            pe.wait_ge(self.mixed_taken.sem, self.mixed_taken.at(j - 1))
                        for b in range(nb):
                            mm = nc.tensor.matmul(O_[j % 2][:, 0:HD], turned[:, j % 2, P * b:P * b + P],
                                                  units[j]["values"][b], start=(b == 0), stop=(b == nb - 1))
                        mm.then_inc(self.mixed.sem, self.mixed.one())

            @block.vector
            def _(dve):
                for i in range(count + 2):
                    if i < count:
                        u, b, n = units[i], i % 2, sizes[i]
                        sc = S_[b][:, 0:n]
                        if i >= 2:
                            dve.wait_ge(self.probs_ready.sem, self.probs_ready.at(i - 1))
                        if u["hide"] is None:
                            dve.wait_ge(self.scores_ready.sem, self.scores_ready.at(i + 1))
                            nc.vector.reduce_max(peak[:, b:b + 1], sc, AX_X, negate=True)\
                                .then_inc(self.logits_ready.sem, self.logits_ready.one())
                        else:
                            sf, lg = soft[:, b, 0:n], logits[:, b, 0:n]
                            dve.wait_ge(self.mass_ready.sem, self.mass_ready.at(i + 1))
                            nc.vector.scalar_tensor_tensor(
                                sf, sc, 0.0, sf, ALU.max, ALU.add).then_inc(self.dve_step.sem, self.dve_step.one())
                            dve.wait_ge(self.dve_step.sem, self.dve_step.count)
                            nc.vector.tensor_tensor(sf, sf, u["hide"][0], ALU.mult)\
                                .then_inc(self.dve_step.sem, self.dve_step.one())
                            dve.wait_ge(self.dve_step.sem, self.dve_step.count)
                            nc.vector.tensor_tensor_scan(
                                lg[:, ::-1], self.tab("ones")[:, 0:n], sf[:, ::-1], 0.0, ALU.mult, ALU.add)\
                                    .then_inc(self.dve_step.sem, self.dve_step.one())
                            dve.wait_ge(self.dve_step.sem, self.dve_step.count)
                            nc.vector.tensor_tensor(lg, sc, lg, ALU.subtract)\
                                .then_inc(self.dve_step.sem, self.dve_step.one())
                            dve.wait_ge(self.dve_step.sem, self.dve_step.count)
                            nc.vector.tensor_tensor(lg, lg, u["hide"][1], ALU.add)\
                                .then_inc(self.logits_ready.sem, self.logits_ready.one())
                    if i >= 2:
                        j = i - 2
                        u, b = units[j], j % 2
                        o = O_[b][:, 0:HD]
                        dve.wait_ge(self.mixed.sem, self.mixed.at(j + 1))
                        if u["hide"] is None:
                            nc.vector.reciprocal(part[:, b:b + 1], mass[:, j % 4:j % 4 + 1])\
                                .then_inc(self.dve_step.sem, self.dve_step.one())
                            dve.wait_ge(self.dve_step.sem, self.dve_step.count)
                            nc.vector.tensor_scalar(u["out"], o, part[:, b:b + 1], None, ALU.mult)\
                                .then_inc(self.mixed_taken.sem, self.mixed_taken.one())
                        else:
                            nc.vector.tensor_copy(u["out"], o)\
                                .then_inc(self.mixed_taken.sem, self.mixed_taken.one())

            @block.scalar
            def _(act):
                for i in range(count + 1):
                    if i < count:
                        u, b, n = units[i], i % 2, sizes[i]
                        sc, pr = S_[b][:, 0:n], probs[:, b, 0:n]
                        if u["hide"] is not None:
                            sf = soft[:, b, 0:n]
                            act.wait_ge(self.scores_ready.sem, self.scores_ready.at(i + 1))
                            nc.scalar.activation(sf, sc, ACT.Abs).then_inc(self.act_step.sem, self.act_step.one())
                            act.wait_ge(self.act_step.sem, self.act_step.count)
                            nc.scalar.activation(sf, sf, ACT.Exp, scale=-1.0)\
                                .then_inc(self.act_step.sem, self.act_step.one())
                            act.wait_ge(self.act_step.sem, self.act_step.count)
                            nc.scalar.activation(sf, sf, ACT.Ln, bias=1.0)\
                                .then_inc(self.mass_ready.sem, self.mass_ready.one())
                        act.wait_ge(self.logits_ready.sem, self.logits_ready.at(i + 1))
                        if i >= 2:
                            act.wait_ge(self.turned.sem, self.turned.at(i - 1))
                        if u["hide"] is None:
                            if i >= 4:
                                act.wait_ge(self.mixed_taken.sem, self.mixed_taken.at(i - 3))
                            nc.scalar.activation(
                                pr, sc, ACT.Exp, bias=peak[:, b:b + 1], accum_out=mass[:, i % 4:i % 4 + 1])\
                                    .then_inc(self.probs_ready.sem, self.probs_ready.one())
                        else:
                            nc.scalar.activation(pr, logits[:, b, 0:n], ACT.Exp)\
                                .then_inc(self.probs_ready.sem, self.probs_ready.one())
                    if i >= 1:
                        j = i - 1
                        act.wait_ge(self.turned.sem, self.turned.at(j + 1))
                        if j >= 2:
                            act.wait_ge(self.mixed.sem, self.mixed.at(j - 1))
                        nc.scalar.copy(turned[:, j % 2, 0:sizes[j]], T_[j % 2][:, 0:sizes[j]])\
                            .then_inc(self.turned_copied.sem, self.turned_copied.one())

    def out_project(self, width, vectors, scaled):
        nc = self.nc
        n = self.plan_use([2] * 4)
        with ExitStack() as ctx, self.stage() as block:
            bufs = self.split_buffers("op", 3, ctx)
            x = self.split_input("op", ctx, width)

            @block.tensor
            def _(pe):
                pe.wait_ge(self.xlo_ready.sem, self.xlo_ready.at(4))
                for g in range(KC):
                    i, c0 = g // 2, P * (g % 2)
                    hi, lo = (b[:, i % 3, :, c0:c0 + P] for b in bufs)
                    pe.wait_ge(self.lo_ready.sem, self.lo_ready.at(i + 1))
                    for k in range(KC):
                        for term, (wp, xp) in enumerate(((hi, x[0]), (lo, x[0]), (hi, x[1]))):
                            mm = nc.tensor.matmul(self.bank[g][:, 0:width], wp[:, k, :], xp[:, k, :],
                                                  start=(k == 0 and term == 0), stop=(k == KC - 1 and term == 2))
                    mm.then_inc(self.sums_ready.sem, self.sums_ready.one())

            @block.scalar
            def _(act):
                self.input_high(act, x, width)
                for i in range(4):
                    self.split_high(act, bufs, n, i)

            @block.vector
            def _(dve):
                self.input_low(dve, x, width)
                for i in range(3):
                    self.split_low(dve, bufs, n, i, i + 1)
                if scaled:
                    nc.vector.tensor_scalar(self.res[:, :, 0:width], self.res[:, :, 0:width], ALPHA, None, ALU.mult)\
                        .then_inc(self.dve_step.sem, self.dve_step.one())
                    dve.wait_ge(self.dve_step.sem, self.dve_step.count)
                for g in range(KC):
                    dve.wait_ge(self.sums_ready.sem, self.sums_ready.at(g + 1))
                    for v in range(vectors):
                        r = self.res[:, g, S * v:S * v + S]
                        nc.vector.scalar_tensor_tensor(r, self.bank[g][:, S * v:S * v + S],
                                                       self.mod[:, 2, g, v:v + 1], r, ALU.mult, ALU.add)
                    if g == 1:
                        self.split_low(dve, bufs, n, 3, 4)

            @block.sync
            def _(sp):
                self.refill(sp, 4)

    def first_block(self):
        nc = self.nc
        self.modulation("c", "b_ada", 1)
        self.rms_modulate("norm1_g", 0, 1)
        with ExitStack() as ctx:
            tok = self.sb("b1_tok", [P, 2, 2310], ctx=ctx)
            conv = self.sb("b1_conv", [P, 6, S], ctx=ctx)
            vpad = self.sb("b1_vpad", [P, 2, S + 2], ctx=ctx)
            ytok = self.sb("b1_y", [P, 2, 2 * HEADS * HD], ctx=ctx)
            qk = self.sb("b1_qk", [66, 4 * HEADS, S], ctx=ctx)
            layout = [[((0, P), "feat", 2 * i), ((P, CW), "feat", 2 * i + 1)] for i in range(3)]
            layout += [[((0, CW), "tok", i * CW)] for i in range(9)]
            self.project(layout, S, tok, [conv[:, i, :] for i in range(6)])
            self.conv_and_gates(tok, conv, vpad, ctx)
            fox = self.fox
            self.transposes([([tok[:, t, HD * h:HD * h + HD] for h in (2 * i, 2 * i + 1) for t in range(2)], HD,
                              qk[0:HD, 2 * i:2 * i + 2, :]) for i in range(6)]
                            + [([fox[:, t, h, :] for h in (2 * i, 2 * i + 1) for t in range(2)], 66,
                                qk[0:66, 12 + 2 * i:14 + 2 * i, :]) for i in range(6)])
            tok_v = lambda off, h, b: tok[:, b, off + HD * h:off + HD * h + HD]
            units = []
            for kind in range(2):
                for h in range(HEADS):
                    for t in range(2):
                        n, c0 = P * (t + 1), P * (1 - t)
                        d = HD if kind == 0 else HD + 2
                        units.append(dict(
                            q=qk[0:d, 12 * kind + h, P * t:P * t + P], key=qk[0:d, 12 * kind + 6 + h, 0:n],
                            add=[] if kind == 0 else [(self.tab("causal")[:, P:2 * P], P * t)],
                            hide=None if kind else (self.tab("strict01")[:, c0:2 * P],
                                                    self.tab("strictneg")[:, c0:2 * P]),
                            values=[tok_v(768 + 1152 * kind, h, b) for b in range(t + 1)],
                            out=ytok[:, t, 384 * kind + HD * h:384 * kind + HD * h + HD]))
            self.attention(units, "b1")
            self.transposes([([ytok[:, t, P * (2 * i + c):P * (2 * i + c) + P] for c in range(2) for t in range(2)], P,
                              self.h[:, 2 + 2 * i:4 + 2 * i, 0:S]) for i in range(3)])
            self.group_norm()
        self.out_project(S, 1, False)
        self.rms_modulate("norm2_g", 3, 4)
        self.experts()

    def conv_and_gates(self, tok, conv, vpad, ctx):
        nc = self.nc
        sq = self.sb("b1_sq", [P, 768], ctx=ctx)
        ms = self.sb("b1_ms", [P, 2, 2, 12], ctx=ctx)
        fox = self.sb("b1_fox", [P, 2, 12, 66], ctx=ctx)
        lf = self.sb("b1_lf", [P, 3, 2, 6], ctx=ctx)
        tmp = self.sb("b1_ctmp", [P, 2, 3, S], ctx=ctx)
        flog = self.bank[7][:, 0:12].rearrange("p (t h) -> p t h", h=HEADS)
        cum = self.bank[6][:, 0:12].rearrange("p (t h) -> p t h", h=HEADS)
        w = self.vec("conv_w").rearrange("p (c j) -> p c j", j=3)
        heads = lambda t, kind: tok[:, t, 1152 * kind:1152 * kind + 768].rearrange("p (h d) -> p h d", d=HD)
        with self.stage() as block:
            @block.gpsimd
            def _(pool):
                step = self.pool_step
                nc.gpsimd.memset(vpad[:, :, 0:2], 0.0).then_inc(step.sem, step.one())
                pool.wait_ge(step.sem, step.count)
                nc.gpsimd.tensor_tensor(vpad[:, :, 2:S + 2], conv[:, 2:4, :], conv[:, 4:6, :], ALU.mult)\
                    .then_inc(step.sem, step.one())
                pool.wait_ge(step.sem, step.count)
                for c in range(2):
                    for j in range(3):
                        nc.gpsimd.tensor_scalar(tmp[:, c, j, :], vpad[:, c, j:j + S], w[:, c, j:j + 1],
                                                         None, ALU.mult).then_inc(step.sem, step.one())
                pool.wait_ge(step.sem, step.count)
                nc.gpsimd.tensor_tensor(tmp[:, :, 0, :], tmp[:, :, 0, :], tmp[:, :, 1, :], ALU.add)\
                    .then_inc(step.sem, step.one())
                pool.wait_ge(step.sem, step.count)
                nc.gpsimd.tensor_tensor(tmp[:, :, 0, :], tmp[:, :, 0, :], tmp[:, :, 2, :], ALU.add)\
                    .then_inc(step.sem, step.one())
                pool.wait_ge(step.sem, step.count)
                pool.wait_ge(self.pe_ready.sem, self.pe_ready.at(1))
                nc.gpsimd.tensor_tensor(self.h[:, 0:2, 0:S], tmp[:, :, 0, :], conv[:, 0:2, :], ALU.mult)\
                    .then_inc(step.sem, step.one())
                pool.wait_ge(step.sem, step.count)

            @block.tensor
            def _(pe):
                wf = self.vec("w_f").rearrange("p (k n) -> p k n", n=HEADS)
                for t in range(2):
                    for k in range(KC):
                        mm = nc.tensor.matmul(flog[:, t, :], self.h[:, k, P * t:P * t + P], wf[:, k, :],
                                              start=(k == 0), stop=(k == KC - 1))
                mm.then_inc(self.pe_ready.sem, self.pe_ready.one())
                pe.wait_ge(self.dve_ready.sem, self.dve_ready.at(3))
                for t in range(2):
                    for s in range(t + 1):
                        mm = nc.tensor.matmul(cum[:, t, :], self.tab("upto") if s == t else self.tab("ones")[:, 0:P],
                                              lf[:, 2, s, :], start=(s == 0), stop=(s == t))
                mm.then_inc(self.pe_ready.sem, self.pe_ready.one())

            @block.scalar
            def _(act):
                act.wait_ge(self.dve_ready.sem, self.dve_ready.at(1))
                nc.scalar.activation(lf[:, 1, :, :], lf[:, 1, :, :], ACT.Exp, scale=-1.0)\
                    .then_inc(self.act_step.sem, self.act_step.one())
                act.wait_ge(self.act_step.sem, self.act_step.count)
                nc.scalar.activation(lf[:, 1, :, :], lf[:, 1, :, :], ACT.Ln, bias=1.0)\
                    .then_inc(self.act_ready.sem, self.act_ready.one())
                act.wait_ge(self.dve_ready.sem, self.dve_ready.at(2))
                nc.scalar.activation(ms[:, :, :, :], ms[:, :, :, :], ACT.Ln)\
                    .then_inc(self.act_step.sem, self.act_step.one())
                act.wait_ge(self.act_step.sem, self.act_step.count)
                nc.scalar.activation(ms[:, :, :, :], ms[:, :, :, :], ACT.Exp, scale=-0.5)\
                    .then_inc(self.act_ready.sem, self.act_ready.one())

            @block.vector
            def _(dve):
                step = self.dve_step
                dve.wait_ge(self.pe_ready.sem, self.pe_ready.at(1))
                nc.vector.tensor_tensor(lf[:, 0, :, :], flog,
                                                       self.vec("f_b").unsqueeze(1).to_broadcast([P, 2, HEADS]), ALU.add)\
                                                           .then_inc(step.sem, step.one())
                dve.wait_ge(step.sem, step.count)
                nc.vector.scalar_tensor_tensor(lf[:, 1, :, :], lf[:, 0, :, :], -1.0,
                                                                  lf[:, 0, :, :], ALU.mult, ALU.max)\
                                                                      .then_inc(self.dve_ready.sem, self.dve_ready.one())
                for t in range(2):
                    for kind in range(2):
                        v = sq[:, :].rearrange("p (h d) -> p h d", d=HD)
                        nc.vector.tensor_tensor(v, heads(t, kind), heads(t, kind), ALU.mult)\
                            .then_inc(step.sem, step.one())
                        dve.wait_ge(step.sem, step.count)
                        nc.vector.reduce_sum(ms[:, t, kind, :], v, AX_X).then_inc(step.sem, step.one())
                        dve.wait_ge(step.sem, step.count)
                nc.vector.tensor_scalar(ms[:, :, :, :], ms[:, :, :, :], 1.0 / HD, EPS_RMS,
                                                           ALU.mult, ALU.add)\
                                                               .then_inc(self.dve_ready.sem, self.dve_ready.one())
                dve.wait_ge(self.act_ready.sem, self.act_ready.at(1))
                nc.vector.scalar_tensor_tensor(
                    lf[:, 2, :, :].rearrange("p t h -> p (t h)"), lf[:, 0, :, :].rearrange("p t h -> p (t h)"), 0.0,
                    lf[:, 1, :, :].rearrange("p t h -> p (t h)"), ALU.min, ALU.subtract)\
                        .then_inc(self.dve_ready.sem, self.dve_ready.one())
                dve.wait_ge(self.act_ready.sem, self.act_ready.at(2))
                nc.vector.tensor_scalar(ms[:, :, :, 0:6], ms[:, :, :, 0:6], HD ** -0.5, None, ALU.mult)\
                    .then_inc(step.sem, step.one())
                dve.wait_ge(step.sem, step.count)
                for t in range(2):
                    for kind in range(2):
                        v, r = heads(t, kind), ms[:, t, kind, :]
                        s = sq[:, :].rearrange("p (h d) -> p h d", d=HD)
                        nc.vector.tensor_tensor(s, v, r.unsqueeze(2).to_broadcast([P, 12, HD]), ALU.mult)\
                            .then_inc(step.sem, step.one())
                        dve.wait_ge(step.sem, step.count)
                        for q in range(2):
                            g = self.vec(("sb_" if kind == 0 else "fox_") + ("q_g" if q == 0 else "k_g"))
                            dst = v[:, 6 * q:6 * q + 6, :] if kind == 0 else fox[:, t, 6 * q:6 * q + 6, 0:HD]
                            nc.vector.tensor_tensor(dst, s[:, 6 * q:6 * q + 6, :],
                                                             g.unsqueeze(1).to_broadcast([P, 6, HD]), ALU.mult)\
                                                                 .then_inc(step.sem, step.one())
                        dve.wait_ge(step.sem, step.count)
                dve.wait_ge(self.pe_ready.sem, self.pe_ready.at(2))
                nc.vector.tensor_copy(fox[:, :, 0:6, 64], cum).then_inc(step.sem, step.one())
                nc.vector.memset(fox[:, :, 0:6, 65], 1.0).then_inc(step.sem, step.one())
                nc.vector.memset(fox[:, :, 6:12, 64], 1.0).then_inc(step.sem, step.one())
                nc.vector.tensor_scalar(fox[:, :, 6:12, 65], cum, -1.0, None, ALU.mult)\
                    .then_inc(step.sem, step.one())

        self.fox = fox

    def group_norm(self):
        nc = self.nc
        with ExitStack() as ctx, self.stage() as block:
            sq = self.sb("gn_sq", [P, KC, S], ctx=ctx)

            @block.vector
            def _(dve):
                for c in range(4):
                    y = self.h[:, 2 * c:2 * c + 2, 0:S]
                    nc.vector.tensor_tensor(sq[:, 2 * c:2 * c + 2, :], y, y, ALU.mult)\
                        .then_inc(self.dve_ready.sem, self.dve_ready.one())
                for c in range(4):
                    dve.wait_ge(self.pe_ready.sem, self.pe_ready.at(c + 1))
                    nc.vector.tensor_scalar(
                        sq[:, 2 * c:2 * c + 2, :], self.bank[c][:, :].rearrange("p (c t) -> p c t", t=S),
                        1.0 / HD, EPS_RMS, ALU.mult, ALU.add).then_inc(self.dve_ready.sem, self.dve_ready.one())
                for c in range(4):
                    dve.wait_ge(self.act_ready.sem, self.act_ready.at(c + 1))
                    for k in (2 * c, 2 * c + 1):
                        nc.vector.scalar_tensor_tensor(self.h[:, k, 0:S], self.h[:, k, 0:S],
                                                       self.vec("out_norm_g")[:, k:k + 1], sq[:, k, :],
                                                       ALU.mult, ALU.mult)

            @block.tensor
            def _(pe):
                for c in range(4):
                    pe.wait_ge(self.dve_ready.sem, self.dve_ready.at(c + 1))
                    nc.tensor.matmul(self.bank[c][:, :], self.tab("halves"),
                                                       sq[:, 2 * c:2 * c + 2, :], start=True, stop=True)\
                                                           .then_inc(self.pe_ready.sem, self.pe_ready.one())

            @block.scalar
            def _(act):
                for c in range(4):
                    v = sq[:, 2 * c:2 * c + 2, :]
                    act.wait_ge(self.dve_ready.sem, self.dve_ready.at(4 + c + 1))
                    nc.scalar.activation(v, v, ACT.Ln).then_inc(self.act_step.sem, self.act_step.one())
                    act.wait_ge(self.act_step.sem, self.act_step.count)
                    nc.scalar.activation(v, v, ACT.Exp, scale=-0.5)\
                        .then_inc(self.act_ready.sem, self.act_ready.one())

    def experts(self):
        nc = self.nc
        with ExitStack() as ctx:
            comb = self.sb("moe_comb", [P, 2, EXPERTS], ctx=ctx)
            comb_t = self.sb("moe_comb_t", [EXPERTS, S], ctx=ctx)
            gates = self.sb("moe_gates", [P, EXPERTS, S], ctx=ctx)
            b2 = self.sb("moe_b2", [EXPERTS, D], ctx=ctx)
            self.route(comb, comb_t, gates, b2, ctx)
            self.mixture(comb_t, gates, b2, ctx)

    def route(self, comb, comb_t, gates, b2, ctx):
        nc = self.nc
        lg = self.sb("rt_lg", [P, 2, EXPERTS], ctx=ctx)
        top = self.sb("rt_top", [P, 2, 8], ctx=ctx)
        idx = self.sb("rt_idx", [P, 2, 8], U32, ctx=ctx)
        idf = self.sb("rt_idf", [P, 2, 8], ctx=ctx)
        wts = self.sb("rt_w", [P, 2, 4], ctx=ctx)
        neg = self.sb("rt_neg", [P, 2], ctx=ctx)
        mass = self.sb("rt_mass", [P, 2], ctx=ctx)
        hot = self.sb("rt_hot", [P, 2, 4, EXPERTS], ctx=ctx)
        raw = self.bank[0][:, 0:2 * EXPERTS].rearrange("p (t e) -> p t e", e=EXPERTS)
        rw = self.vec("router_w").rearrange("p (k e) -> p k e", e=EXPERTS)
        with self.stage() as block:
            @block.sync
            def _(sp):
                self.load(sp, b2[:, :], self.dram["b_mlp2"][0])
                sp.wait_ge(self.loaded, self.n_loaded)

            @block.tensor
            def _(pe):
                for t in range(2):
                    for k in range(KC):
                        mm = nc.tensor.matmul(raw[:, t, :], self.h[:, k, P * t:P * t + P], rw[:, k, :],
                                              start=(k == 0), stop=(k == KC - 1))
                mm.then_inc(self.pe_ready.sem, self.pe_ready.one())
                pe.wait_ge(self.dve_ready.sem, self.dve_ready.at(2))
                for t in range(2):
                    mm = nc.tensor.transpose(self.bank[1][0:EXPERTS, P * t:P * t + P], comb[:, t, :], self.tab("ident"))
                mm.then_inc(self.pe_ready.sem, self.pe_ready.one())
                for g in range(EXPERTS // 2):
                    if g >= 6:
                        pe.wait_ge(self.act_ready.sem, self.act_ready.at(1 + g - 5))
                    for e in (2 * g, 2 * g + 1):
                        for t in range(2):
                            c0 = S * (e % 2) + P * t
                            mm = nc.tensor.matmul(self.bank[2 + g % 6][:, c0:c0 + P],
                                                  comb[:, t, e:e + 1].to_broadcast([P, P]), self.tab("ident"),
                                                  start=True, stop=True)
                    mm.then_inc(self.pe_ready.sem, self.pe_ready.one())

            @block.vector
            def _(dve):
                step = self.dve_step
                nc.vector.tensor_scalar(self.vec("b_lin"), self.vec("b_lin"), 1.0, None, ALU.add)
                dve.wait_ge(self.pe_ready.sem, self.pe_ready.at(1))
                nc.vector.tensor_tensor(
                    lg[:, :, :], raw, self.vec("router_b").unsqueeze(1).to_broadcast([P, 2, EXPERTS]), ALU.add)\
                        .then_inc(step.sem, step.one())
                dve.wait_ge(step.sem, step.count)
                for t in range(2):
                    nc.vector.max(top[:, t, :], lg[:, t, :]).then_inc(step.sem, step.one())
                    dve.wait_ge(step.sem, step.count)
                    nc.vector.max_index(idx[:, t, :], top[:, t, :], lg[:, t, :]).then_inc(step.sem, step.one())
                    dve.wait_ge(step.sem, step.count)
                nc.vector.tensor_copy(idf[:, :, :], idx[:, :, :]).then_inc(step.sem, step.one())
                dve.wait_ge(step.sem, step.count)
                nc.vector.tensor_scalar(neg[:, :], top[:, :, 0], -1.0, None, ALU.mult)\
                    .then_inc(self.dve_ready.sem, self.dve_ready.one())
                dve.wait_ge(self.act_ready.sem, self.act_ready.at(1))
                nc.vector.reciprocal(mass[:, :], mass[:, :]).then_inc(step.sem, step.one())
                dve.wait_ge(step.sem, step.count)
                for t in range(2):
                    nc.vector.tensor_scalar(wts[:, t, :], wts[:, t, :], mass[:, t:t + 1], None, ALU.mult)\
                        .then_inc(step.sem, step.one())
                    dve.wait_ge(step.sem, step.count)
                    for k in range(TOPK):
                        nc.vector.tensor_scalar(hot[:, t, k, :], self.tab("iota"), idf[:, t, k:k + 1],
                                                         wts[:, t, k:k + 1], ALU.is_equal, ALU.mult)\
                                                             .then_inc(step.sem, step.one())
                dve.wait_ge(step.sem, step.count)
                nc.vector.tensor_tensor(hot[:, :, 0:2, :], hot[:, :, 0:2, :], hot[:, :, 2:4, :], ALU.add)\
                    .then_inc(step.sem, step.one())
                dve.wait_ge(step.sem, step.count)
                nc.vector.tensor_tensor(comb[:, :, :], hot[:, :, 0, :], hot[:, :, 1, :], ALU.add)\
                    .then_inc(self.dve_ready.sem, self.dve_ready.one())
                dve.wait_ge(self.pe_ready.sem, self.pe_ready.at(2))
                nc.vector.tensor_copy(comb_t[:, :], self.bank[1][0:EXPERTS, 0:S])

            @block.scalar
            def _(act):
                act.wait_ge(self.dve_ready.sem, self.dve_ready.at(1))
                for t in range(2):
                    e = nc.scalar.activation(wts[:, t, :], top[:, t, 0:4], ACT.Exp, bias=neg[:, t:t + 1],
                                             accum_out=mass[:, t:t + 1])
                e.then_inc(self.act_ready.sem, self.act_ready.one())
                for g in range(EXPERTS // 2):
                    act.wait_ge(self.pe_ready.sem, self.pe_ready.at(3 + g))
                    nc.scalar.copy(gates[:, 2 * g:2 * g + 2, :],
                                                      self.bank[2 + g % 6][:, :].rearrange("p (e t) -> p e t", t=S))\
                                                          .then_inc(self.act_ready.sem, self.act_ready.one())

    def mixture(self, comb_t, gates, b2, ctx):
        nc = self.nc
        depth = 3
        bufs = self.split_buffers("moe", depth, ctx)
        x = self.split_input("moe", ctx, S)
        hid = [self.sb(f"moe_hid_{part}", [P, KC, S], F32R, ctx=ctx) for part in ("hi", "lo")]
        glu, lin, sig = (self.h[:, 2 * i:2 * i + 2, S:2 * S] for i in range(3))
        gate = self.h[:, 6, S:2 * S]
        pair = self.bank[0:4]
        acc = lambda d: self.bank[4 + d // 2][:, S * (d % 2):S * (d % 2) + S]
        per = 12
        assert per % SLOTS == 0 and per % depth == 0 and self.n_moe == self.next_use
        first = self.plan_use([1] * (per * EXPERTS))
        visit = lambda j: ((self.n_moe + j) % SLOTS, (self.n_moe + j) // SLOTS + 1)
        loads = per // SLOTS
        sums, taken, lows = self.sums_ready.count, self.sums_taken.count, self.lo_ready.count
        highs, glus, gated = self.hi_ready.count, self.glu_ready.count, self.gate_ready.count
        weighted, done, step = self.pool_ready.count, self.hidden_ready.count, self.dve_step.count
        copied = self.pool_step.count
        lag = 2
        with self.stage() as block:
            @block.tensor
            def _(pe):
                for d in range(KC):
                    nc.tensor.matmul(acc(d), b2[:, P * d:P * d + P], comb_t[:, :], start=(d % 2 == 0), stop=False,
                                     skip_group_check=True)
                pe.wait_ge(self.xlo_ready.sem, self.xlo_ready.at(4))
                with pe.Fori(0, EXPERTS) as e:
                    for j in range(per):
                        hi, lo = (b[:, j % depth, :, :] for b in bufs)
                        pe.wait_ge(self.lo_ready.sem, e * per + (lows + j + 1))
                        if j < KC:
                            pe.wait_ge(self.sums_taken.sem, e * KC + (taken + j + 1))
                            for half in range(2):
                                for k in range(KC):
                                    for term, (w, xp) in enumerate(((hi, x[0]), (lo, x[0]), (hi, x[1]))):
                                        mm = nc.tensor.matmul(pair[j % 4][:, S * half:S * half + S],
                                                              w[:, k, P * half:P * half + P], xp[:, k, :],
                                                              start=(k == 0 and term == 0),
                                                              stop=(k == KC - 1 and term == 2))
                        else:
                            for k in range(KC):
                                if j == KC:
                                    pe.wait_ge(self.hidden_ready.sem, e * KC + (done + k + 1))
                                for d in (2 * (j - KC), 2 * (j - KC) + 1):
                                    c0 = P * (d % 2)
                                    for w, hp in ((hi, hid[0]), (lo, hid[0]), (hi, hid[1])):
                                        mm = nc.tensor.matmul(acc(d), w[:, k, c0:c0 + P], hp[:, k, :],
                                                              start=False, stop=False, skip_group_check=True)
                        mm.then_inc(self.sums_ready.sem, 1)

            @block.scalar
            def _(act):
                self.input_high(act, x, S)
                with act.Fori(0, EXPERTS) as e:
                    for j in range(per):
                        slot, v = visit(j)
                        act.wait_ge(self.landed[slot], e * (32 * loads) + 32 * v)
                        act.wait_ge(self.sums_ready.sem, e * per + (sums + j - depth + 1))
                        w, out = self.ring[:, slot, :, :], bufs[0][:, j % depth, :, :]
                        if j < KC:
                            w = w.rearrange("p k (c two) -> p k two c", two=2)
                            out = out.rearrange("p k (two c) -> p k two c", two=2)
                        nc.scalar.copy(out, w).then_inc(self.hi_ready.sem, 1)
                        if lag <= j < KC + lag:
                            act.wait_ge(self.glu_ready.sem, e * KC + (glus + j - lag + 1))
                            nc.scalar.activation(sig[:, j % 2, :], glu[:, j % 2, :], ACT.Sigmoid, scale=SWIGLU_ALPHA)\
                                .then_inc(self.gate_ready.sem, 1)

            @block.gpsimd
            def _(pool):
                with pool.Fori(0, EXPERTS) as e:
                    nc.gpsimd.tensor_copy(gate, gates[:, bass.ds(e, 1), :].rearrange("p e t -> p (e t)"))\
                        .then_inc(self.pool_step.sem, 1)
                    pool.wait_ge(self.pool_step.sem, e + (copied + 1))
                    for j in range(KC):
                        s = sig[:, j % 2, :]
                        pool.wait_ge(self.gate_ready.sem, e * KC + (gated + j + 1))
                        nc.gpsimd.tensor_tensor(s, s, gate, ALU.mult).then_inc(self.pool_ready.sem, 1)
                    pool.wait_ge(self.pool_ready.sem, e * KC + (weighted + KC))

            @block.vector
            def _(dve):
                for i in range(4):
                    nc.vector.memset(lin[:, 0, i:i + 1], 0.0).then_inc(self.sums_taken.sem, 1)
                dve.wait_ge(self.sums_taken.sem, taken + 4)
                self.input_low(dve, x, S)
                with dve.Fori(0, EXPERTS) as e:
                    for j in range(per):
                        slot, _ = visit(j)
                        dve.wait_ge(self.hi_ready.sem, e * per + (highs + j + 1))
                        w, hi, lo = self.ring[:, slot, :, :], bufs[0][:, j % depth, :, :], bufs[1][:, j % depth, :, :]
                        if j < KC:
                            w = w.rearrange("p k (c two) -> p k two c", two=2)
                            hi = hi.rearrange("p k (two c) -> p k two c", two=2)
                            lo = lo.rearrange("p k (two c) -> p k two c", two=2)
                        nc.vector.tensor_tensor(lo, w, hi.bitcast(F32), ALU.subtract).then_inc(self.lo_ready.sem, 1)
                        if not lag <= j < KC + lag:
                            continue
                        i = j - lag
                        g, l, s = glu[:, i % 2, :], lin[:, i % 2, :], sig[:, i % 2, :]
                        bg = self.vec("b_glu")[:, bass.ds(e * KC + i, 1)]
                        bl = self.vec("b_lin")[:, bass.ds(e * KC + i, 1)]
                        dve.wait_ge(self.sums_ready.sem, e * per + (sums + i + 1))
                        nc.vector.tensor_scalar(g, pair[i % 4][:, 0:S], bg, SWIGLU_LIMIT, ALU.add, ALU.min)\
                            .then_inc(self.glu_ready.sem, 1)
                        nc.vector.tensor_scalar(l, pair[i % 4][:, S:2 * S], bl, SWIGLU_LIMIT + 1, ALU.add, ALU.min)\
                            .then_inc(self.sums_taken.sem, 1)
                        dve.wait_ge(self.sums_taken.sem, e * KC + (taken + 4 + i + 1))
                        nc.vector.scalar_tensor_tensor(l, l, 1 - SWIGLU_LIMIT, g, ALU.max, ALU.mult)\
                            .then_inc(self.dve_step.sem, 1)
                        dve.wait_ge(self.dve_step.sem, e * (3 * KC) + (step + 3 * i + 1))
                        dve.wait_ge(self.pool_ready.sem, e * KC + (weighted + i + 1))
                        nc.vector.tensor_tensor(l, l, s, ALU.mult).then_inc(self.dve_step.sem, 1)
                        dve.wait_ge(self.dve_step.sem, e * (3 * KC) + (step + 3 * i + 2))
                        nc.vector.tensor_copy(hid[0][:, i, :], l).then_inc(self.dve_step.sem, 1)
                        dve.wait_ge(self.dve_step.sem, e * (3 * KC) + (step + 3 * i + 3))
                        nc.vector.tensor_tensor(hid[1][:, i, :], l, hid[0][:, i, :].bitcast(F32), ALU.subtract)\
                            .then_inc(self.hidden_ready.sem, 1)

            @block.sync
            def _(sp):
                w1 = self.dram["w_mlp1"][0].rearrange("e (c p) n -> e p c n", p=P)
                w2 = self.dram["w_mlp2"][0].rearrange("e (c p) n -> e p c n", p=P)
                with sp.Fori(0, EXPERTS - 1) as e:
                    for jj in range(per):
                        m = SLOTS + jj
                        ahead, j = m // per, m % per
                        slot, _ = visit(m)
                        w, c = (w1, j) if j < KC else (w2, j - KC)
                        sp.wait_ge(self.lo_ready.sem, e * per + (lows + jj + 1))
                        for half in range(2):
                            src = w[bass.ds(e + ahead, 1), :, 4 * half:4 * half + 4, c * CW:(c + 1) * CW]
                            sp.dma_start(self.ring[:, slot, 4 * half:4 * half + 4, :],
                                         src.rearrange("e p c n -> (e p) c n")).then_inc(self.landed[slot], 16)
                self.next_issue += per * (EXPERTS - 1)
                self.refill(sp, per)
            self.sums_ready.count += per * EXPERTS
            self.hi_ready.count += per * EXPERTS
            self.lo_ready.count += per * EXPERTS
            self.sums_taken.count += 4 + KC * EXPERTS
            self.hidden_ready.count += KC * EXPERTS
            self.dve_step.count += 3 * KC * EXPERTS
            self.glu_ready.count += KC * EXPERTS
            self.gate_ready.count += KC * EXPERTS
            self.pool_ready.count += KC * EXPERTS
            self.pool_step.count += EXPERTS
        with self.stage() as block:
            @block.vector
            def _(dve):
                for d in range(KC):
                    nc.vector.scalar_tensor_tensor(self.res[:, d, 0:S], acc(d), self.mod[:, 5, d, 0:1],
                                                   self.res[:, d, 0:S], ALU.mult, ALU.add)

    def modulate(self, width, vectors, shift, scale):
        nc = self.nc
        with self.stage() as block:
            @block.vector
            def _(dve):
                for v in range(vectors):
                    nc.vector.tensor_scalar(self.amp[:, :], self.mod[:, scale, :, v], 1.0, None,
                                                                    ALU.add)\
                                                                        .then_inc(self.dve_step.sem, self.dve_step.one())
                    dve.wait_ge(self.dve_step.sem, self.dve_step.count)
                    for k in range(KC):
                        c = slice(S * v, S * v + S)
                        o = nc.vector.tensor_scalar(self.h[:, k, c], self.res[:, k, c], self.amp[:, k:k + 1],
                                                    self.mod[:, shift, k, v:v + 1], ALU.mult, ALU.add)
                    o.then_inc(self.dve_step.sem, self.dve_step.one())
                    dve.wait_ge(self.dve_step.sem, self.dve_step.count)

    def layer_norm(self, width, gain, bias, l):
        nc = self.nc
        total, spread = self.bank[0][:, 0:width], self.bank[1][:, 0:width]
        mean, rstd = self.stat[:, 0, 0:width], self.stat[:, 1, 0:width]
        g, b = self.vec(f"{gain}{l}"), self.vec(f"{bias}{l}")
        with self.stage() as block:
            @block.tensor
            def _(pe):
                for k in range(KC):
                    mm = nc.tensor.matmul(total, self.tab("ones")[:, 0:P], self.res[:, k, 0:width],
                                          start=(k == 0), stop=(k == KC - 1))
                mm.then_inc(self.pe_ready.sem, self.pe_ready.one())
                for k in range(KC):
                    pe.wait_ge(self.act_ready.sem, self.act_ready.at(k + 1))
                    mm = nc.tensor.matmul(spread, self.tab("ones")[:, 0:P], self.h[:, k, 0:width],
                                          start=(k == 0), stop=(k == KC - 1))
                mm.then_inc(self.pe_ready.sem, self.pe_ready.one())

            @block.vector
            def _(dve):
                dve.wait_ge(self.pe_ready.sem, self.pe_ready.at(1))
                nc.vector.tensor_scalar(mean, total, 1.0 / D, None, ALU.mult)\
                    .then_inc(self.dve_step.sem, self.dve_step.one())
                dve.wait_ge(self.dve_step.sem, self.dve_step.count)
                for k in range(KC):
                    r = self.res[:, k, 0:width]
                    nc.vector.tensor_tensor(r, r, mean, ALU.subtract)\
                        .then_inc(self.dve_ready.sem, self.dve_ready.one())
                dve.wait_ge(self.pe_ready.sem, self.pe_ready.at(2))
                nc.vector.tensor_scalar(rstd, spread, 1.0 / D, EPS_LN, ALU.mult, ALU.add)\
                    .then_inc(self.dve_ready.sem, self.dve_ready.one())
                dve.wait_ge(self.act_ready.sem, self.act_ready.at(KC + 1))
                for k in range(KC):
                    r = self.res[:, k, 0:width]
                    nc.vector.tensor_tensor(r, r, rstd, ALU.mult).then_inc(self.dve_ready.sem, self.dve_ready.one())

            @block.scalar
            def _(act):
                for k in range(KC):
                    act.wait_ge(self.dve_ready.sem, self.dve_ready.at(k + 1))
                    nc.scalar.activation(self.h[:, k, 0:width], self.res[:, k, 0:width], ACT.Square)\
                        .then_inc(self.act_ready.sem, self.act_ready.one())
                act.wait_ge(self.dve_ready.sem, self.dve_ready.at(KC + 1))
                nc.scalar.activation(rstd, rstd, ACT.Ln).then_inc(self.act_step.sem, self.act_step.one())
                act.wait_ge(self.act_step.sem, self.act_step.count)
                nc.scalar.activation(rstd, rstd, ACT.Exp, scale=-0.5)\
                    .then_inc(self.act_ready.sem, self.act_ready.one())
                for k in range(KC):
                    act.wait_ge(self.dve_ready.sem, self.dve_ready.at(KC + 2 + k))
                    nc.scalar.activation(self.res[:, k, 0:width], self.res[:, k, 0:width], ACT.Identity,
                                         bias=b[:, k:k + 1], scale=g[:, k:k + 1])

    def feed_forward(self, width, vectors):
        nc = self.nc
        fp = FC // PARTS
        with ExitStack() as ctx:
            hid = [self.sb(f"ff_hid_{part}", [P, fp, width], F32R, ctx=ctx) for part in ("hi", "lo")]
            sig = self.sb("ff_sig", [P, 2, width], ctx=ctx)
            bufs = self.split_buffers("ff", 2, ctx)
            x = self.split_input("ff", ctx, width)
            for part in range(PARTS):
                n = self.plan_use([1] * fp)
                with self.stage() as block:
                    @block.tensor
                    def _(pe):
                        if part == 0:
                            pe.wait_ge(self.xlo_ready.sem, self.xlo_ready.at(4))
                        for f in range(fp):
                            pe.wait_ge(self.lo_ready.sem, self.lo_ready.at(f + 1))
                            if f >= 4:
                                pe.wait_ge(self.sums_taken.sem, self.sums_taken.at(f - 3))
                            for side in range(2):
                                hi, lo = (b[:, f % 2, :, P * side:P * side + P] for b in bufs)
                                for k in range(KC):
                                    for term, (w, xp) in enumerate(((hi, x[0]), (lo, x[0]), (hi, x[1]))):
                                        mm = nc.tensor.matmul(self.bank[2 * (f % 4) + side][:, 0:width],
                                                              w[:, k, :], xp[:, k, :], start=(k == 0 and term == 0),
                                                              stop=(k == KC - 1 and term == 2))
                            mm.then_inc(self.sums_ready.sem, self.sums_ready.one())

                    @block.scalar
                    def _(act):
                        if part == 0:
                            self.input_high(act, x, width)
                        self.split_high(act, bufs, n, 0)
                        for f in range(fp):
                            if f + 1 < fp:
                                self.split_high(act, bufs, n, f + 1)
                            act.wait_ge(self.sums_ready.sem, self.sums_ready.at(f + 1))
                            if f >= 2:
                                act.wait_ge(self.sums_taken.sem, self.sums_taken.at(f - 1))
                            nc.scalar.activation(sig[:, f % 2, :], self.bank[2 * (f % 4)][:, 0:width], ACT.Sigmoid)\
                                .then_inc(self.gate_ready.sem, self.gate_ready.one())

                    @block.vector
                    def _(dve):
                        step = self.dve_step
                        if part == 0:
                            self.input_low(dve, x, width)
                        self.split_low(dve, bufs, n, 0, 1)
                        if part == 0:
                            nc.vector.tensor_scalar(self.res[:, :, 0:width], self.res[:, :, 0:width], ALPHA, None,
                                                    ALU.mult).then_inc(step.sem, step.one())
                        for f in range(fp):
                            if f + 1 < fp:
                                self.split_low(dve, bufs, n, f + 1, f + 2)
                            s = sig[:, f % 2, :]
                            dve.wait_ge(self.gate_ready.sem, self.gate_ready.at(f + 1))
                            nc.vector.tensor_tensor(s, self.bank[2 * (f % 4)][:, 0:width], s, ALU.mult)\
                                .then_inc(step.sem, step.one())
                            dve.wait_ge(step.sem, step.count)
                            nc.vector.tensor_tensor(s, self.bank[2 * (f % 4) + 1][:, 0:width], s, ALU.mult)\
                                .then_inc(step.sem, step.one())
                            dve.wait_ge(step.sem, step.count)
                            nc.vector.tensor_copy(hid[0][:, f, :], s).then_inc(step.sem, step.one())
                            dve.wait_ge(step.sem, step.count)
                            nc.vector.tensor_tensor(hid[1][:, f, :], s, hid[0][:, f, :].bitcast(F32), ALU.subtract)\
                                .then_inc(self.sums_taken.sem, self.sums_taken.one())

                    @block.sync
                    def _(sp):
                        self.refill(sp, fp)

                chunks = 4 * len(PIECES)
                n = self.plan_use([1] * chunks)
                with self.stage() as block:
                    @block.tensor
                    def _(pe):
                        for i in range(chunks):
                            k0, k1 = PIECES[i % len(PIECES)]
                            pe.wait_ge(self.lo_ready.sem, self.lo_ready.at(i + 1))
                            for d in (2 * (i // len(PIECES)), 2 * (i // len(PIECES)) + 1):
                                hi, lo = (b[:, i % 2, :, P * (d % 2):P * (d % 2) + P] for b in bufs)
                                for k in range(k0, k1):
                                    for term, (w, hp) in enumerate(((hi, hid[0]), (lo, hid[0]), (hi, hid[1]))):
                                        mm = nc.tensor.matmul(self.bank[d][:, 0:width], w[:, k - k0, :], hp[:, k, :],
                                                              start=(k == 0 and term == 0),
                                                              stop=(k == fp - 1 and term == 2))
                            mm.then_inc(self.sums_ready.sem, self.sums_ready.one())

                    @block.scalar
                    def _(act):
                        for i in range(chunks):
                            self.split_high(act, bufs, n, i)

                    @block.vector
                    def _(dve):
                        for i in range(chunks + 2):
                            if i < chunks:
                                self.split_low(dve, bufs, n, i, i + 1)
                            if i < 2 or (i - 2) % len(PIECES) != len(PIECES) - 1:
                                continue
                            dve.wait_ge(self.sums_ready.sem, self.sums_ready.at(i - 1))
                            for d in (2 * ((i - 2) // len(PIECES)), 2 * ((i - 2) // len(PIECES)) + 1):
                                for v in range(vectors):
                                    r = self.res[:, d, S * v:S * v + S]
                                    nc.vector.scalar_tensor_tensor(r, self.bank[d][:, S * v:S * v + S],
                                                                   self.mod[:, 5, d, v:v + 1], r, ALU.mult, ALU.add)

                    @block.sync
                    def _(sp):
                        self.refill(sp, chunks)

    def neighbour_window(self, bias, l):
        nc = self.nc
        with self.stage() as block:
            @block.sync
            def _(sp):
                self.load(sp, bias[:, :, :, :], self.dram["na_bias"][l])
                sp.wait_ge(self.loaded, self.n_loaded)

            @block.vector
            def _(dve):
                dve.wait_ge(self.loaded, self.n_loaded)
                mask = self.tab("colneg").unsqueeze(1).to_broadcast([P, HEADS * 4, 64])
                for t in range(2):
                    v = bias[:, t, :, :].rearrange("p h (r c) -> p (h r) c", c=64)
                    nc.vector.tensor_tensor(v, v, mask, ALU.add)

    def linear_and_norms(self, tok, vz, tiles, l):
        nc = self.nc
        with ExitStack() as ctx, self.stage() as block:
            sq = self.sb("nn_sq", [P, 8, HD], ctx=ctx)
            rot = self.sb("nn_rot", [P, 8, HD], ctx=ctx)
            ms = self.sb("nn_ms", [P, 4, 8], ctx=ctx)
            heads = lambda t: tok[:, t, GAQ:GAQ + 8 * HD].rearrange("p (h d) -> p h d", d=HD)

            @block.gpsimd
            def _(pool):
                nc.gpsimd.memset(vz[:, :, :, :], 0.0).then_inc(self.pool_step.sem, self.pool_step.one())
                pool.wait_ge(self.pool_step.sem, self.pool_step.count)
                for t in range(4):
                    for q in range(2):
                        v = tok[:, t, GLV:GLV + 256].rearrange("p (a b d) -> p a b d", b=2, d=GDV)[:, :, q, :]
                        nc.gpsimd.tensor_copy(vz[:, t, q:4:2, GDV * q:GDV * q + GDV], v)\
                            .then_inc(self.pool_step.sem, self.pool_step.one())
                pool.wait_ge(self.pool_step.sem, self.pool_step.count)

            @block.scalar
            def _(act):
                act.wait_ge(self.dve_ready.sem, self.dve_ready.at(1))
                m = ms[:, 0:tiles, :]
                nc.scalar.activation(m, m, ACT.Ln).then_inc(self.act_step.sem, self.act_step.one())
                act.wait_ge(self.act_step.sem, self.act_step.count)
                nc.scalar.activation(m, m, ACT.Exp, scale=-0.5).then_inc(self.act_ready.sem, self.act_ready.one())

            @block.vector
            def _(dve):
                step = self.dve_step
                for t in range(tiles):
                    nc.vector.tensor_tensor(sq[:, :, :], heads(t), heads(t), ALU.mult)\
                        .then_inc(step.sem, step.one())
                    dve.wait_ge(step.sem, step.count)
                    nc.vector.reduce_sum(ms[:, t, :], sq[:, :, :], AX_X).then_inc(step.sem, step.one())
                    dve.wait_ge(step.sem, step.count)
                m = ms[:, 0:tiles, :]
                nc.vector.tensor_scalar(m, m, 1.0 / HD, EPS_RMS, ALU.mult, ALU.add)\
                    .then_inc(self.dve_ready.sem, self.dve_ready.one())
                for t in range(tiles):
                    q = tok[:, t, NAQ:NAQ + 384]
                    nc.vector.tensor_scalar(q, q, HD ** -0.5, None, ALU.mult).then_inc(step.sem, step.one())
                dve.wait_ge(self.act_ready.sem, self.act_ready.at(1))
                nc.vector.tensor_scalar(ms[:, 0:tiles, 0:6], ms[:, 0:tiles, 0:6], HD ** -0.5, None, ALU.mult)\
                    .then_inc(step.sem, step.one())
                dve.wait_ge(step.sem, step.count)
                for t in range(tiles):
                    x = heads(t)
                    nc.vector.tensor_tensor(
                        x, x, ms[:, t, :].unsqueeze(2).to_broadcast([P, 8, HD]), ALU.mult)\
                            .then_inc(step.sem, step.one())
                    dve.wait_ge(step.sem, step.count)
                    for a, b, g in ((0, 6, "qn"), (6, 8, "kn")):
                        nc.vector.tensor_tensor(x[:, a:b, :], x[:, a:b, :],
                                                         self.vec(f"{g}{l}").unsqueeze(1).to_broadcast([P, b - a, HD]),
                                                         ALU.mult).then_inc(step.sem, step.one())
                    dve.wait_ge(step.sem, step.count)
                    if t >= 2:
                        continue
                    cos = self.tab("cos")[:, HD * t:HD * t + HD].unsqueeze(1).to_broadcast([P, 8, HD])
                    for half in range(2):
                        for axis in range(2):
                            c0, c1 = 32 * axis + 16 * half, 32 * axis + 16 * (1 - half)
                            sin = self.tab("sin")[:, HD * t + c0:HD * t + c0 + 16].unsqueeze(1).to_broadcast([P, 8, 16])
                            nc.vector.tensor_tensor(rot[:, :, c0:c0 + 16], x[:, :, c1:c1 + 16], sin, ALU.mult)\
                                .then_inc(step.sem, step.one())
                    dve.wait_ge(step.sem, step.count)
                    nc.vector.tensor_tensor(x, x, cos, ALU.mult).then_inc(step.sem, step.one())
                    dve.wait_ge(step.sem, step.count)
                    nc.vector.tensor_tensor(x, x, rot[:, :, :], ALU.add).then_inc(step.sem, step.one())
                    dve.wait_ge(step.sem, step.count)

    def linear_attention(self, l, streams, gq, gk, gg, lr, tok, vz):
        nc = self.nc
        with ExitStack() as ctx:
            cum = self.sb("gl_cum", [P, 2, 2, S + 1], ctx=ctx)
            state = self.sb("gl_state", [P, 2, 2 * P], ctx=ctx)
            levels = self.sb("gl_levels", [P, 2, 7, P], ctx=ctx)
            self.gates_and_ends(l, lr, gk, tok, cum, state, levels)
            for s in streams:
                self.linear_stream(l, s, gq, gk, gg, vz, cum, state, levels)

    def gates_and_ends(self, l, lr, gk, tok, cum, state, levels):
        nc = self.nc
        with ExitStack() as ctx:
            wa = self.sb("gl_wa", [32, 2, P], ctx=ctx)
            gate = self.sb("gl_gate", [P, 2, 2 * S], ctx=ctx)
            tmp = self.sb("gl_tmp", [P, 2, 2 * S], ctx=ctx)
            kend = self.sb("gl_kend", [P, 2, S], ctx=ctx)
            kend_t = self.sb("gl_kend_t", [P, 2, 2, P], ctx=ctx)
            with self.stage() as block:
                @block.sync
                def _(sp):
                    self.load(sp, levels[:, :, :, :].rearrange("p e m t -> p (e m t)"), self.dram["levels"])
                    sp.wait_ge(self.pool_ready.sem, self.pool_ready.at(1))
                    for e in range(2):
                        self.load(sp, wa[16 * e:16 * e + 16, e, :], self.dram["gla_wa2_2"][l, e])
                    sp.wait_ge(self.loaded, self.n_loaded)

                @block.gpsimd
                def _(pool):
                    nc.gpsimd.memset(wa[:, :, :], 0.0).then_inc(self.pool_ready.sem, self.pool_ready.one())
                    nc.gpsimd.memset(cum[:, :, :, 0:1], 0.0).then_inc(self.pool_ready.sem, self.pool_ready.one())
                    pool.wait_ge(self.pool_ready.sem, self.pool_ready.at(2))

                @block.tensor
                def _(pe):
                    pe.wait_ge(self.loaded, self.n_loaded)
                    for e in range(2):
                        mm = nc.tensor.matmul(self.bank[e][:, :], wa[:, e, :], lr, start=True, stop=True)
                    mm.then_inc(self.pe_ready.sem, self.pe_ready.one())

                @block.scalar
                def _(act):
                    act.wait_ge(self.dve_ready.sem, self.dve_ready.at(1))
                    nc.scalar.activation(tmp[:, :, :], tmp[:, :, :], ACT.Exp, scale=-1.0)\
                        .then_inc(self.act_step.sem, self.act_step.one())
                    act.wait_ge(self.act_step.sem, self.act_step.count)
                    nc.scalar.activation(tmp[:, :, :], tmp[:, :, :], ACT.Ln, bias=1.0)\
                        .then_inc(self.act_ready.sem, self.act_ready.one())

                @block.vector
                def _(dve):
                    step = self.dve_step
                    dve.wait_ge(self.pe_ready.sem, self.pe_ready.at(1))
                    for e in range(2):
                        nc.vector.tensor_scalar(gate[:, e, :], self.bank[e][:, :],
                                                         self.vec(f"gla_ba{l}")[:, e:e + 1], None, ALU.add)\
                                                             .then_inc(step.sem, step.one())
                    dve.wait_ge(step.sem, step.count)
                    nc.vector.scalar_tensor_tensor(tmp[:, :, :], gate[:, :, :], -1.0,
                                                                      gate[:, :, :], ALU.mult, ALU.max)\
                                                                          .then_inc(self.dve_ready.sem, self.dve_ready.one())
                    dve.wait_ge(self.act_ready.sem, self.act_ready.at(1))
                    flat = lambda x: x[:, :, :].rearrange("p e t -> p (e t)")
                    nc.vector.scalar_tensor_tensor(flat(gate), flat(gate), 0.0, flat(tmp), ALU.min,
                                                                  ALU.subtract).then_inc(step.sem, step.one())
                    dve.wait_ge(step.sem, step.count)
                    nc.vector.tensor_scalar(flat(gate), flat(gate), 1.0 / 16.0, None, ALU.mult)\
                        .then_inc(step.sem, step.one())
                    dve.wait_ge(step.sem, step.count)
                    dve.wait_ge(self.pool_ready.sem, self.pool_ready.at(2))
                    for e in range(2):
                        for s in range(2):
                            nc.vector.tensor_tensor_scan(cum[:, e, s, 1:S + 1], self.tab("ones"),
                                                                  gate[:, e, S * s:S * s + S], 0.0, ALU.mult, ALU.add)\
                                                                      .then_inc(step.sem, step.one())

            with self.stage() as block:
                @block.vector
                def _(dve):
                    step = self.dve_step
                    nc.vector.tensor_scalar(tmp[:, 0, 0:S], cum[:, 0, 1, 1:S + 1],
                                                           cum[:, 0, 1, S:S + 1], -1.0, ALU.subtract, ALU.mult)\
                                                               .then_inc(step.sem, step.one())
                    dve.wait_ge(step.sem, step.count)
                    nc.vector.tensor_copy(tmp[:, 1, 0:S], cum[:, 1, 1, 0:S])\
                        .then_inc(self.dve_ready.sem, self.dve_ready.one())
                    dve.wait_ge(self.act_ready.sem, self.act_ready.at(1))
                    for e in range(2):
                        nc.vector.tensor_tensor(kend[:, e, :], gk[:, S:2 * S], tmp[:, e, 0:S], ALU.mult)\
                            .then_inc(self.dve_ready.sem, self.dve_ready.one())
                    dve.wait_ge(self.pe_ready.sem, self.pe_ready.at(1))
                    nc.vector.tensor_copy(kend_t[:, :, :, :].rearrange("p e t d -> p (e t d)"),
                                                             self.bank[0][:, :])\
                                                                 .then_inc(self.dve_ready.sem, self.dve_ready.one())
                    dve.wait_ge(self.pe_ready.sem, self.pe_ready.at(2))
                    for e in range(2):
                        nc.vector.tensor_tensor(state[:, e, :], self.bank[1 + e][:, 0:2 * P], self.tab("headdiag"), ALU.mult)

                @block.scalar
                def _(act):
                    act.wait_ge(self.dve_ready.sem, self.dve_ready.at(1))
                    nc.scalar.activation(tmp[:, :, 0:S], tmp[:, :, 0:S], ACT.Exp)\
                        .then_inc(self.act_ready.sem, self.act_ready.one())

                @block.tensor
                def _(pe):
                    pe.wait_ge(self.dve_ready.sem, self.dve_ready.at(3))
                    for e in range(2):
                        for t in range(2):
                            mm = nc.tensor.transpose(self.bank[0][:, P * (2 * e + t):P * (2 * e + t) + P],
                                                     kend[:, e, P * t:P * t + P], self.tab("ident"))
                    mm.then_inc(self.pe_ready.sem, self.pe_ready.one())
                    pe.wait_ge(self.dve_ready.sem, self.dve_ready.at(4))
                    for e in range(2):
                        for t in range(2):
                            mm = nc.tensor.matmul(self.bank[1 + e][:, 0:2 * P], kend_t[:, e, t, :],
                                                  tok[:, 2 + t, GLV:GLV + 2 * P], start=(t == 0), stop=(t == 1))
                    mm.then_inc(self.pe_ready.sem, self.pe_ready.one())

    def linear_stream(self, l, s, gq, gk, gg, vz, cum, state, levels):
        nc = self.nc
        with ExitStack() as ctx:
            q4 = self.h[:, 0:2, :].rearrange("p c (a t) -> p (c a) t", t=S)
            decay = self.sb("gs_decay", [P, 2, 8, S], ctx=ctx)
            keys = self.sb("gs_keys", [P, 2, 8, S], ctx=ctx)
            moving = self.sb("gs_moving", [P, 2, GH, P], ctx=ctx)
            att = self.sb("gs_att", [P, 2, GH, S], ctx=ctx)
            carry = self.stat[:, :, 0:S]
            out = self.h[:, 5:8, :].rearrange("p x (c t) -> p x c t", t=S)
            q, k = gq[:, S * s:S * s + S], gk[:, S * s:S * s + S]
            hm = self.tab("headmask").unsqueeze(2).to_broadcast([P, GH, S])
            products = [(None, None, t, t) for t in range(2)] + [(0, 0, 1, 0), (1, 0, 0, 1)]
            products += [(e, i, t, t) for e in range(2) for i in range(1, 8) for t in range(2)]
            with self.stage() as block:
                @block.vector
                def _(dve):
                    step = self.dve_step
                    nc.vector.tensor_tensor(q4[:, :, :], q.unsqueeze(1).to_broadcast([P, GH, S]),
                                                               hm, ALU.mult)\
                                                                   .then_inc(self.dve_ready.sem, self.dve_ready.one())
                    for e in range(2):
                        b = cum[:, e, s, 1 - e:S + 1 - e]
                        for i, m in enumerate(LEVELS):
                            blocks = S // (2 * m)
                            border = cum[:, e, s, m:S:2 * m].unsqueeze(2).to_broadcast([P, blocks, 2 * m])
                            nc.vector.tensor_tensor(
                                decay[:, e, i, :].rearrange("p (b w) -> p b w", w=2 * m),
                                b.rearrange("p (b w) -> p b w", w=2 * m), border, ALU.subtract)\
                                    .then_inc(step.sem, step.one())
                        dve.wait_ge(step.sem, step.count)
                        nc.vector.scalar_tensor_tensor(decay[:, e, :, :], decay[:, e, :, :], -1.0,
                                                                          decay[:, e, :, :], ALU.mult, ALU.max)\
                                                                              .then_inc(self.dve_ready.sem, self.dve_ready.one())
                    for e in range(2):
                        dve.wait_ge(self.act_ready.sem, self.act_ready.at(e + 1))
                        nc.vector.tensor_tensor(
                            keys[:, e, :, :], k.unsqueeze(1).to_broadcast([P, 8, S]), decay[:, e, :, :], ALU.mult)\
                                .then_inc(self.dve_ready.sem, self.dve_ready.one())
                    for g, (e, i, t, sp) in enumerate(products):
                        dst = att[:, sp, :, P * t:P * t + P]
                        src = self.bank[g % 4][:, :].rearrange("p (h t) -> p h t", t=P)
                        dve.wait_ge(self.sums_ready.sem, self.sums_ready.at(g + 1))
                        if e is None:
                            mask = self.tab("ident2").unsqueeze(1).to_broadcast([P, GH, P])
                            o = nc.vector.tensor_tensor(dst, src, mask, ALU.mult)
                        elif i == 0:
                            o = nc.vector.tensor_copy(dst, src)
                        else:
                            mask = levels[:, e, i - 1, :].bitcast(I32).unsqueeze(1).to_broadcast([P, GH, P])
                            if g >= 2:
                                dve.wait_ge(self.sums_taken.sem, self.sums_taken.at(g))
                            o = nc.vector.copy_predicated(dst, mask, src)
                        o.then_inc(self.sums_taken.sem, self.sums_taken.one())
                    if s == 0:
                        dve.wait_ge(self.act_ready.sem, self.act_ready.at(4))
                        for e in range(2):
                            nc.vector.tensor_tensor(carry[:, e, :], carry[:, e, :], q, ALU.mult)\
                                .then_inc(step.sem, step.one())
                        dve.wait_ge(step.sem, step.count)
                        nc.vector.tensor_scalar(carry[:, :, :], carry[:, :, :], GDK ** -0.5, None,
                                                                   ALU.mult)\
                                                                       .then_inc(self.dve_ready.sem, self.dve_ready.one())
                    else:
                        nc.vector.tensor_copy(carry[:, 0, 0:1], q[:, 0:1])\
                            .then_inc(self.dve_ready.sem, self.dve_ready.one())
                    dve.wait_ge(self.pe_ready.sem, self.pe_ready.at(1))
                    o = self.bank[4][:, :].rearrange("p (c t) -> p c t", t=S)
                    nc.vector.tensor_copy(out[:, 0, :, :], o).then_inc(step.sem, step.one())
                    dve.wait_ge(step.sem, step.count)
                    nc.vector.tensor_tensor(out[:, 1, :, :], out[:, 0, :, :], out[:, 0, :, :], ALU.mult)\
                        .then_inc(self.dve_ready.sem, self.dve_ready.one())
                    dve.wait_ge(self.pe_ready.sem, self.pe_ready.at(2))
                    nc.vector.tensor_scalar(
                        out[:, 1, :, :], self.bank[5][:, :].rearrange("p (c t) -> p c t", t=S), 1.0 / GDV, EPS_RMS,
                        ALU.mult, ALU.add).then_inc(self.dve_ready.sem, self.dve_ready.one())
                    flat = lambda x: out[:, x, :, :].rearrange("p c t -> p (c t)")
                    dve.wait_ge(self.act_ready.sem, self.act_ready.at(6 if s == 0 else 4))
                    nc.vector.scalar_tensor_tensor(flat(0), flat(0), self.vec(f"gla_nw{l}"), flat(1),
                                                                  ALU.mult, ALU.mult).then_inc(step.sem, step.one())
                    dve.wait_ge(step.sem, step.count)
                    g = gg[:, :, S * s:S * s + S]
                    nc.vector.tensor_tensor(out[:, 2, :, :], out[:, 2, :, :], g, ALU.mult)\
                        .then_inc(step.sem, step.one())
                    dve.wait_ge(step.sem, step.count)
                    nc.vector.tensor_tensor(self.h[:, 3:5, S * s:S * s + S], out[:, 0, :, :], out[:, 2, :, :], ALU.mult)

                @block.scalar
                def _(act):
                    for e in range(2):
                        act.wait_ge(self.dve_ready.sem, self.dve_ready.at(2 + e))
                        nc.scalar.activation(decay[:, e, :, :], decay[:, e, :, :], ACT.Exp, scale=-1.0)\
                            .then_inc(self.act_ready.sem, self.act_ready.one())
                    if s == 0:
                        nc.scalar.activation(carry[:, 0, :], cum[:, 0, s, 1:S + 1], ACT.Exp)\
                            .then_inc(self.act_ready.sem, self.act_ready.one())
                        nc.scalar.activation(carry[:, 1, :], cum[:, 1, s, 0:S], ACT.Exp, scale=-1.0,
                                                                bias=cum[:, 1, s, S:S + 1])\
                                                                    .then_inc(self.act_ready.sem, self.act_ready.one())
                    act.wait_ge(self.dve_ready.sem, self.dve_ready.at(8))
                    nc.scalar.activation(out[:, 1, :, :], out[:, 1, :, :], ACT.Ln)\
                        .then_inc(self.act_step.sem, self.act_step.one())
                    act.wait_ge(self.act_step.sem, self.act_step.count)
                    nc.scalar.activation(out[:, 1, :, :], out[:, 1, :, :], ACT.Exp, scale=-0.5)\
                        .then_inc(self.act_ready.sem, self.act_ready.one())
                    nc.scalar.activation(out[:, 2, :, :], gg[:, :, S * s:S * s + S], ACT.Sigmoid)\
                        .then_inc(self.act_ready.sem, self.act_ready.one())

                @block.gpsimd
                def _(pool):
                    pool.wait_ge(self.dve_ready.sem, self.dve_ready.at(1))
                    for g, (e, i, t, sp) in enumerate(products[2:]):
                        if i == 0 or (g >= 2 and i == 1 and t == 0):
                            pool.wait_ge(self.dve_ready.sem, self.dve_ready.at(4 + e))
                        if g >= 2:
                            pool.wait_ge(self.sums_ready.sem, self.sums_ready.at(g + 1))
                        nc.gpsimd.tensor_tensor(
                            moving[:, g % 2, :, :], q4[:, :, P * t:P * t + P],
                            decay[:, e, i, P * t:P * t + P].unsqueeze(1).to_broadcast([P, GH, P]), ALU.mult)\
                                .then_inc(self.pool_ready.sem, self.pool_ready.one())
                    pool.wait_ge(self.pool_ready.sem, self.pool_ready.count)

                @block.tensor
                def _(pe):
                    pe.wait_ge(self.dve_ready.sem, self.dve_ready.at(1))
                    for g, (e, i, t, sp) in enumerate(products):
                        if g >= 4:
                            pe.wait_ge(self.sums_taken.sem, self.sums_taken.at(g - 3))
                        if e is None:
                            lhs, rhs = k[:, P * sp:P * sp + P], q4[:, :, P * t:P * t + P]
                        else:
                            pe.wait_ge(self.pool_ready.sem, self.pool_ready.at(g - 1))
                            if i == 0:
                                pe.wait_ge(self.dve_ready.sem, self.dve_ready.at(4 + e))
                            lhs, rhs = keys[:, e, i, P * sp:P * sp + P], moving[:, g % 2, :, :]
                        nc.tensor.matmul(self.bank[g % 4][:, :].rearrange("p (h t) -> p h t", t=P),
                                                             lhs, rhs, start=True, stop=True)\
                                                                 .then_inc(self.sums_ready.sem, self.sums_ready.one())
                    pe.wait_ge(self.sums_taken.sem, self.sums_taken.at(len(products)))
                    pe.wait_ge(self.dve_ready.sem, self.dve_ready.at(6))
                    for c in range(2):
                        o = self.bank[4][:, S * c:S * c + S]
                        last = None
                        terms = [(vz[:, 2 * s + sp, h, :], att[:, sp, h, :]) for sp in range(2) for h in (2 * c, 2 * c + 1)]
                        if s == 0:
                            terms += [(state[:, e, P * c:P * c + P], carry[:, e, :]) for e in range(2)]
                        for x, (lhs, rhs) in enumerate(terms):
                            mm = nc.tensor.matmul(o, lhs, rhs, start=(x == 0), stop=(x == len(terms) - 1))
                    mm.then_inc(self.pe_ready.sem, self.pe_ready.one())
                    pe.wait_ge(self.dve_ready.sem, self.dve_ready.at(7))
                    nc.tensor.matmul(self.bank[5][:, :], self.tab("halves"), out[:, 1, :, :],
                                                       start=True, stop=True)\
                                                           .then_inc(self.pe_ready.sem, self.pe_ready.one())

    def second_block(self):
        nc = self.nc
        for l in range(LAYERS):
            context_out = l < LAYERS - 1
            v = 2 if context_out else 1
            width = S * v
            self.modulation("cc", f"b_ada{l}", 2)
            self.modulate(2 * S, 2, 0, 1)
            with ExitStack() as ctx:
                tok = self.sb(f"b2_tok{l}", [P, 4, TOKW], ctx=ctx)
                gq = self.sb(f"b2_gq{l}", [P, 2 * S], ctx=ctx)
                gk = self.sb(f"b2_gk{l}", [P, 2 * S], ctx=ctx)
                gg = self.sb(f"b2_gg{l}", [P, 2, 2 * S], ctx=ctx)
                lr = self.sb(f"b2_lr{l}", [32, 2 * S], ctx=ctx)
                feat = [gq[:, :], gk[:, :], gg[:, 0, :], gg[:, 1, :], lr[:, :]]
                layout = [[((0, w), "tok", c0)] for c0, w in IN2[:5]]
                layout += [[((0, P), "feat", 0), ((P, CW), "feat", 1)], [((0, CW), "tok", GLV)],
                           [((0, P), "feat", 2), ((P, CW), "feat", 3)], [((0, 32), "feat", 4)]]
                layout += [[((0, w), "tok", c0 - 1952 + GAQ)] for c0, w in IN2[9:]]
                self.project(layout, 2 * S, tok, feat)
                with ExitStack() as inner:
                    vz = self.sb(f"b2_vz{l}", [P, 4, GH, P], ctx=inner)
                    self.linear_and_norms(tok, vz, 4, l)
                    self.linear_attention(l, (1, 0) if context_out else (0,), gq[:, :], gk[:, :], gg, lr[:, :], tok, vz)
                ytok = self.sb(f"b2_y{l}", [P, 4, HEADS * HD], ctx=ctx)
                bias = self.sb(f"b2_bias{l}", [P, 2, HEADS, S], ctx=ctx)
                self.neighbour_window(bias, l)
                for kind in range(2):
                    with ExitStack() as inner:
                        nk = HEADS if kind == 0 else KV_HEADS
                        qk = self.sb(f"b2_qk{l}{kind}", [HD, HEADS + nk, 2 * S], ctx=inner)
                        q0 = NAQ if kind == 0 else GAQ
                        v0 = NAV if kind == 0 else GAV
                        self.transposes([([tok[:, t, q0 + HD * h:q0 + HD * h + HD] for t in range(4)], HD, qk[:, h, :])
                                         for h in range(HEADS + nk)])
                        units = []
                        for h in range(HEADS):
                            kv = h if kind == 0 else h // (HEADS // KV_HEADS)
                            for t in range(2 * v):
                                k0 = 0 if t < 2 else 2
                                units.append(dict(
                                    q=qk[:, h, P * t:P * t + P], key=qk[:, HEADS + kv, P * k0:2 * S],
                                    add=[(bias[:, t, h, :], 0)] if kind == 0 and t < 2 else [], hide=None,
                                    values=[tok[:, b, v0 + HD * kv:v0 + HD * kv + HD] for b in range(k0, 4)],
                                    out=ytok[:, t, HD * h:HD * h + HD]))
                        self.attention(units, f"b2a{l}{kind}")
                        self.transposes([([ytok[:, t, P * c:P * c + P] for t in range(2 * v)], P,
                                          self.h[:, 5 * kind + c, 0:width]) for c in range(3)])
            self.out_project(width, v, True)
            self.layer_norm(width, "ln1_g", "ln1_b", l)
            self.modulate(width, v, 3, 4)
            self.feed_forward(width, v)
            self.layer_norm(width, "ln2_g", "ln2_b", l)

    def finish(self):
        nc = self.nc
        with self.stage() as block:
            @block.sync
            def _(sp):
                self.load(sp, self.dram["out"], self.res[:, :, 0:S])
                sp.wait_ge(self.loaded, self.n_loaded)


def hybrid_then_latent_kernel(nc, dram, where, twhere):
    b = Builder(nc, dram, where)
    b.twhere = twhere
    with b.ctx:
        b.allocate()
        b.plan_chunks()
        b.start()
        b.first_block()
        b.second_block()
        b.finish()


_WHOLE = ["w_ada", "w_in", "w_out", "w_mlp1", "w_mlp2", "b_mlp2", "w_ada_2", "w_in_2", "gla_wa2_2", "w_out_2",
          "w_ffn_in_2", "w_ffn_out_2"]


def kernel(**inputs):
    import concourse.bacc as bacc
    from concourse.bass_utils import run_bass_kernel_spmd as run

    inputs = {k: np.asarray(v) for k, v in inputs.items()}
    tokens = lambda a: np.ascontiguousarray(a[0].T.reshape(KC, P, S).transpose(1, 0, 2))
    arrays = {n: np.ascontiguousarray(inputs[n]) for n in _WHOLE}
    arrays["x"], arrays["ctx"] = tokens(inputs["x"]), tokens(inputs["ctx_2"])
    arrays["vecs"], where = pack(packed_vectors(inputs))
    arrays["tables"], twhere = pack(shape_tables())
    arrays["levels"] = level_masks()
    arrays["na_bias"] = neighbour_bias(inputs["na_rpb_2"])
    nc = bacc.Bacc("TRN2", target_bir_lowering=False, num_devices=1)
    dram = {n: nc.dram_tensor(f"in_{n}", a.shape, mybir.dt.from_np(a.dtype), kind="ExternalInput").ap()
            for n, a in arrays.items()}
    dram["out"] = nc.dram_tensor("out_0", (P, KC, S), F32, kind="ExternalOutput").ap()
    hybrid_then_latent_kernel(nc, dram, where, twhere)
    r = run(nc, [{f"in_{n}": a for n, a in arrays.items()}], core_ids=[0])
    out = r.results[0]["out_0"]
    return np.ascontiguousarray(out.transpose(1, 0, 2).reshape(D, S).T)[None]
```

```python
from contextlib import ExitStack, contextmanager

import numpy as np
import concourse.bass as bass
from concourse import mybir

F32 = mybir.dt.float32
F32R = mybir.dt.float32r
U32 = mybir.dt.uint32
I32 = mybir.dt.int32
ALU = mybir.AluOpType
ACT = mybir.ActivationFunctionType
AX_X = mybir.AxisListType.X

P = 128
D = 1024
KC = D // P
S = 256
HD = 64
HEADS = 6
CONV = 256
EXPERTS = 32
TOPK = 4
HIDDEN = 2816
FC = HIDDEN // P
LAYERS = 2
GH, GDK, GDV = 4, 32, 64
KV_HEADS = 2
PLACES = P
ITEMS = EXPERTS + TOPK * S // PLACES
ITEMW = ITEMS + ITEMS % 2 + 2
LEVELS = (128, 64, 32, 16, 8, 4, 2, 1)
EPS_RMS = 1e-6
EPS_LN = 1e-5
ALPHA = (2.0 * LAYERS) ** 0.25
NEG = -1e30
SWIGLU_LIMIT = 7.0
SWIGLU_ALPHA = 1.702
PARTS = 2
PIECES = ((0, 6), (6, 11))
SLOTS = 4
CW = 256
MODS = 6 * D // CW
FRONT1, FRONT2 = 8, 8
SIDES = [{"norms": (8, 13), "stream1": (13, 19), "stream0": (19, 24)},
         {"norms": (8, 13), "ends": (13, 17), "stream0": (17, 24)}]
SIDES1 = {"conv": (8, 12), "attention": (12, 24)}

NAQ, NAK, NAV, GLV, GAQ, GAK, GAV, TOKW = 0, 384, 768, 1152, 1408, 1792, 1920, 2048
IN2 = [(0, 256), (256, 256), (512, 256), (768, 256), (1024, 128), (1152, 256), (1408, 256), (1664, 256),
       (1920, 32), (1952, 256), (2208, 256), (2464, 128)]


def shape_tables():
    i = np.arange(P)
    f = np.float32
    t = {
        "ident": np.eye(P, dtype=f),
        "ident2": 2 * np.eye(P, dtype=f),
        "upto": (i[:, None] <= i[None, :]).astype(f),
        "ones": np.ones((P, 256), f),
        "halves": (i[:, None] // 64 == i[None, :] // 64).astype(f),
        "headmask": ((i[:, None] // GDK == np.arange(GH)[None, :]) * GDK ** -0.5).astype(f),
        "headdiag": (i[:, None] // GDK == np.arange(GH * GDV)[None, :] // GDV).astype(f),
        "iota": np.tile(np.arange(ITEMW, dtype=f), (P, 1)),
        "places": np.tile(np.arange(1, PLACES + 1, dtype=f), (P, 1)),
        "line": i.astype(f)[:, None],
        "line1": (i + 1).astype(f)[:, None],
    }
    z = np.zeros((P, P), f)
    causal = i[None, :] <= i[:, None]
    strict = i[None, :] < i[:, None]
    t["causal"] = np.concatenate([z, np.where(causal, 0, NEG)], 1).astype(f)
    t["strictneg"] = np.concatenate([z, np.where(strict, 0, NEG)], 1).astype(f)
    t["strict01"] = np.concatenate([z + 1, strict], 1).astype(f)
    c, k = i % 64, np.arange(64)
    lo = np.clip(c - 8, 0, 48)
    t["colneg"] = np.where((k >= lo[:, None]) & (k < lo[:, None] + 16), 0, NEG).astype(f)
    cosr, sinr = [], []
    inv = 10000.0 ** (-np.arange(16, dtype=f) / 16)
    for tile in range(2):
        tok = tile * P + i
        r, cc = (tok // 64).astype(f)[:, None] * inv, (tok % 64).astype(f)[:, None] * inv
        ang = np.concatenate([r, r, cc, cc], 1).astype(f)
        sign = np.where((np.arange(64) // 16) % 2 == 0, -1, 1).astype(f)
        cosr.append(np.cos(ang))
        sinr.append(np.sin(ang) * sign)
    t["cos"] = np.concatenate(cosr, 1).astype(f)
    t["sin"] = np.concatenate(sinr, 1).astype(f)
    return t


def level_masks():
    i, t = np.arange(P), {}
    for direction in range(2):
        for m in LEVELS[1:]:
            s_even = (i[:, None] // m) % 2 == 0
            t_odd = (i[None, :] // m) % 2 == 1
            mask = s_even & t_odd & (i[:, None] // (2 * m) == i[None, :] // (2 * m))
            t[f"level{direction}_{m}"] = (mask if direction == 0 else mask.T).astype(np.float32)
    return np.concatenate(list(t.values()), axis=1)


def pack(parts):
    at, where = 0, {}
    for name, a in parts.items():
        where[name] = (at, a.shape[1])
        at += a.shape[1]
    return np.ascontiguousarray(np.concatenate(list(parts.values()), axis=1)), where


def feature_columns(v):
    return np.asarray(v).reshape(-1, P).T


def row(v):
    return np.tile(np.asarray(v).reshape(1, -1), (P, 1))


def packed_vectors(a):
    v = {
        "c": feature_columns(a["c"][0]),
        "cc": np.stack([feature_columns(a["c_2"][0]), feature_columns(a["c_ctx_2"])], 2).reshape(P, -1),
        "norm1_g": feature_columns(a["norm1_g"][0]),
        "norm2_g": feature_columns(a["norm2_g"][0]),
        "out_norm_g": feature_columns(a["out_norm_g"][0]),
        "b_ada": feature_columns(a["b_ada"][0]),
        "conv_w": a["conv_w"][0].reshape(3, 2, P).transpose(2, 1, 0).reshape(P, 6),
        "b_glu": a["b_mlp1"][0][:, ::2].reshape(EXPERTS * KC, P).T,
        "b_lin": a["b_mlp1"][0][:, 1::2].reshape(EXPERTS * KC, P).T,
        "router_b": row(a["router_b"][0]),
        "router_w": a["router_w"][0].reshape(KC, P, EXPERTS).transpose(1, 0, 2).reshape(P, -1),
        "w_f": a["w_in"][0][:, 3072:3078].reshape(KC, P, 6).transpose(1, 0, 2).reshape(P, -1),
        "f_b": row(a["fox_f_b"][0]),
        "sb_q_g": row(a["sb_q_g"][0]), "sb_k_g": row(a["sb_k_g"][0]),
        "fox_q_g": row(a["fox_q_g"][0]), "fox_k_g": row(a["fox_k_g"][0]),
    }
    for l in range(LAYERS):
        v[f"b_ada{l}"] = feature_columns(a["b_ada_2"][l])
        v[f"gla_ba{l}"] = a["gla_ba_2"][l].T
        v[f"gla_nw{l}"] = np.tile(a["gla_norm_w_2"][l], 2).reshape(P, 1)
        v[f"qn{l}"] = row(a["gqa_qnorm_w_2"][l])
        v[f"kn{l}"] = row(a["gqa_knorm_w_2"][l])
        for n in ("ln1_g", "ln1_b", "ln2_g", "ln2_b"):
            v[f"{n}{l}"] = feature_columns(a[n + "_2"][l])
    return v


def neighbour_bias(rpb):
    q, k = np.arange(S)[:, None], np.arange(S)[None, :]
    dr = k // 64 - q // 64 + 7
    dc = np.clip(k % 64 - q % 64, -15, 15) + 15
    b = np.asarray(rpb)[:, :, dr, dc]
    return np.ascontiguousarray(b.reshape(LAYERS, HEADS, 2, P, S).transpose(0, 3, 2, 1, 4))


def rows(w):
    return w.rearrange("(c p) n -> p c n", p=P)


class Counter:

    def __init__(self, sem):
        self.sem, self.base, self.count = sem, 0, 0

    def one(self):
        self.count += 1
        return 1

    def at(self, n):
        return self.base + n


class Builder:
    def __init__(self, nc, dram, where):
        self.nc, self.dram, self.where = nc, dram, where
        self.ctx = ExitStack()
        self.counters = []
        self.names = {}

    def sb(self, name, shape, dt=F32, ctx=None):
        self.names[name] = self.names.get(name, 0) + 1
        if self.names[name] > 1:
            name += f"_{self.names[name]}"
        return (ctx or self.ctx).enter_context(self.nc.sbuf_tensor(name, shape, dt))

    def counter(self, name):
        s = Counter(self.ctx.enter_context(self.nc.semaphore(name)))
        self.counters.append(s)
        return s

    @contextmanager
    def stage(self):
        with self.nc.Block(no_gpsimd_drain=True) as block:
            yield block
        for s in self.counters:
            s.base = s.count

    def vec(self, name):
        at, n = self.where[name]
        return self.vecs[:, at:at + n]

    def tab(self, name):
        at, n = self.twhere[name]
        return self.tables[:, at:at + n]

    def allocate(self):
        nc = self.nc
        self.bank = [self.ctx.enter_context(nc.psum_tensor(f"bank{i}", [P, 512], F32)) for i in range(8)]
        self.ring = self.sb("ring", [P, SLOTS, KC, CW])
        self.landed = [self.ctx.enter_context(nc.semaphore(f"landed{i}")) for i in range(SLOTS)]
        self.loaded = self.ctx.enter_context(nc.semaphore("loaded"))
        self.n_loaded = 0
        self.sums_ready = self.counter("sums_ready")
        self.hi_ready = self.counter("hi_ready")
        self.lo_ready = self.counter("lo_ready")
        self.xhi_ready = self.counter("xhi_ready")
        self.xlo_ready = self.counter("xlo_ready")
        self.sums_taken = self.counter("sums_taken")
        self.pe_ready = self.counter("pe_ready")
        self.dve_ready = self.counter("dve_ready")
        self.act_ready = self.counter("act_ready")
        self.pool_ready = self.counter("pool_ready")
        self.dve_step = self.counter("dve_step")
        self.act_step = self.counter("act_step")
        self.pool_step = self.counter("pool_step")
        self.scores_ready = self.counter("scores_ready")
        self.logits_ready = self.counter("logits_ready")
        self.mass_ready = self.counter("mass_ready")
        self.probs_ready = self.counter("probs_ready")
        self.turned = self.counter("turned")
        self.turned_copied = self.counter("turned_copied")
        self.mixed = self.counter("mixed")
        self.mixed_taken = self.counter("mixed_taken")
        self.glu_ready = self.counter("glu_ready")
        self.gate_ready = self.counter("gate_ready")
        self.hidden_ready = self.counter("hidden_ready")
        self.rows_summed = self.counter("rows_summed")
        self.rows_taken = self.counter("rows_taken")
        self.rows_turned = self.counter("rows_turned")
        self.line = self.sb("line", [2, 2, CW])
        self.vecs = self.sb("vecs", [P, self.dram["vecs"].shape[1]])
        self.tables = self.sb("tables", [P, self.dram["tables"].shape[1]])
        self.res = self.sb("res", [P, KC, 2 * S])
        self.h = self.sb("h", [P, KC, 2 * S])
        self.mod = self.sb("mod", [P, 6, KC, 2])
        self.cond = self.sb("cond", [P, KC, 1])
        self.cond_pair = self.sb("cond_pair", [P, KC, 2])
        self.amp = self.sb("amp", [P, KC])
        self.stat = self.sb("stat", [P, 2, 512])

    def plan_chunks(self):
        d, plan, shape = self.dram, [], []

        def add(a, k0, kn, c0, width):
            half = (kn + 1) // 2
            plan.append([((slice(0, half), slice(0, width)), a[:, k0:k0 + half, c0:c0 + width]),
                         ((slice(half, kn), slice(0, width)), a[:, k0 + half:k0 + kn, c0:c0 + width])])
            shape.append((kn, width))

        for i in range(FRONT1):
            add(rows(d["w_ada"][0]), 0, KC, i * CW, CW)
        for i in range(12):
            add(rows(d["w_in"][0]), 0, KC, i * CW, CW)
        for i in range(FRONT1, MODS):
            add(rows(d["w_ada"][0]), 0, KC, i * CW, CW)
        for i in range(4):
            add(rows(d["w_out"][0]), 0, KC, i * CW, CW)
        for i in range(FRONT2):
            add(rows(d["w_ada_2"][0]), 0, KC, i * CW, CW)
        self.n_moe = len(plan)
        for l in range(LAYERS):
            for c0, w in IN2:
                add(rows(d["w_in_2"][l]), 0, KC, c0, w)
            for i in range(FRONT2, MODS):
                add(rows(d["w_ada_2"][l]), 0, KC, i * CW, CW)
            for i in range(FRONT2 if l + 1 < LAYERS else 0):
                add(rows(d["w_ada_2"][l + 1]), 0, KC, i * CW, CW)
            for i in range(4):
                add(rows(d["w_out_2"][l]), 0, KC, i * CW, CW)
            a, b = rows(d["w_ffn_in_2"][l]), rows(d["w_ffn_out_2"][l])
            for part in range(PARTS):
                for f in range(FC // PARTS * part, FC // PARTS * (part + 1)):
                    plan.append([((slice(0, 8), slice(P * s, P * s + P)),
                                  a[:, :, s * HIDDEN + f * P:s * HIDDEN + f * P + P]) for s in range(2)])
                    shape.append((KC, CW))
                for i in range(4):
                    for k0, k1 in PIECES:
                        add(b, FC // PARTS * part + k0, k1 - k0, i * CW, CW)
        self.plan, self.shape = plan, shape
        self.issue_end = self.n_moe
        self.free_at = []
        self.done_at = []
        self.next_issue = 0
        self.next_use = 0

    def refill(self, sp, chunks):
        end = min(self.next_issue + chunks, self.issue_end)
        for n in range(self.next_issue, end):
            if n >= SLOTS:
                counter, value = self.free_at[n - SLOTS]
                sp.wait_ge(counter.sem, value)
            for (kk, cc), src in self.plan[n]:
                sp.dma_start(self.ring[:, n % SLOTS, kk, cc], src).then_inc(self.landed[n % SLOTS], 16)
        self.next_issue = end

    def plan_use(self, groups, whole=()):
        v, split, first = self.sums_ready.count, self.lo_ready.count, self.next_use
        for x, g in enumerate(groups):
            v += g
            self.done_at.append(v)
            if x in whole:
                self.free_at.append((self.sums_ready, v))
            else:
                split += 1
                self.free_at.append((self.lo_ready, split))
        self.next_use += len(groups)
        return first

    def plan_side(self, sides, bias, nv):
        if sides is None:
            return None
        x0, x1 = sides
        first = self.next_use
        for x in range(x1 - x0):
            self.done_at.append(0)
            self.free_at.append((self.rows_summed, self.rows_summed.count + x + 1))
        self.next_use += x1 - x0
        return dict(first=first, x0=x0, chunks=x1 - x0, bias=bias, nv=nv)

    def side_turn(self, side, x):
        nv = side["nv"]
        out = self.bank[7][:, 0:2 * MODS * nv].rearrange("p (i v) -> p i v", v=nv)
        for j in range(2):
            mm = self.nc.tensor.transpose(out[:, 2 * (side["x0"] + x) + j, :], self.line[0:nv, x % 2, P * j:P * j + P],
                                          self.tab("ident")[0:nv, 0:nv])
        return mm

    def side_step(self, pe, side, step):
        x, quarter = step // 4, step % 4
        nv, n = side["nv"], side["first"] + x
        w, landed = self.slot(n)
        cond = self.cond if nv == 1 else self.cond_pair
        if quarter == 0:
            if x > 0:
                pe.wait_ge(self.rows_taken.sem, self.rows_taken.at(x))
                self.side_turn(side, x - 1)
            pe.wait_ge(self.landed[n % SLOTS], landed)
        for k in (2 * quarter, 2 * quarter + 1):
            mm = self.nc.tensor.matmul(self.bank[6][0:nv, 0:CW], cond[:, k, :], w[:, k, :],
                                       start=(k == 0), stop=(k == KC - 1))
        if quarter == 3:
            mm.then_inc(self.rows_summed.sem, self.rows_summed.one())

    def side_last(self, pe, side):
        pe.wait_ge(self.rows_taken.sem, self.rows_taken.at(side["chunks"]))
        self.side_turn(side, side["chunks"] - 1).then_inc(self.rows_turned.sem, self.rows_turned.one())

    def side_copy(self, eng, copy, side, x):
        eng.wait_ge(self.rows_summed.sem, self.rows_summed.at(x + 1))
        copy(self.line[0:side["nv"], x % 2, :], self.bank[6][0:side["nv"], 0:CW])\
            .then_inc(self.rows_taken.sem, self.rows_taken.one())

    def side_bias(self, dve, side):
        nv, c0, c1 = side["nv"], 2 * side["x0"], 2 * (side["x0"] + side["chunks"])
        dve.wait_ge(self.rows_turned.sem, self.rows_turned.at(1))
        self.nc.vector.tensor_tensor(
            self.mod[:, :, :, 0:nv].rearrange("p i c v -> p (i c) v")[:, c0:c1, :],
            self.bank[7][:, 0:2 * MODS * nv].rearrange("p (i v) -> p i v", v=nv)[:, c0:c1, :],
            self.vec(side["bias"])[:, c0:c1].unsqueeze(2).to_broadcast([P, c1 - c0, nv]), ALU.add)

    def slot(self, n):
        kn, width = self.shape[n]
        return self.ring[:, n % SLOTS, 0:kn, 0:width], 32 * (n // SLOTS + 1)

    def split_buffers(self, name, depth, ctx):
        return [self.sb(f"{name}_{part}", [P, depth, KC, CW], F32R, ctx=ctx) for part in ("whi", "wlo")]

    def split_high(self, act, bufs, first, x):
        depth = bufs[0].shape[1]
        kn, width = self.shape[first + x]
        src, landed = self.slot(first + x)
        act.wait_ge(self.landed[(first + x) % SLOTS], landed)
        if x >= depth:
            act.wait_ge(self.sums_ready.sem, self.done_at[first + x - depth])
        self.nc.scalar.copy(bufs[0][:, x % depth, 0:kn, 0:width], src)\
            .then_inc(self.hi_ready.sem, self.hi_ready.one())

    def split_low(self, dve, bufs, first, x, nth):
        depth = bufs[0].shape[1]
        kn, width = self.shape[first + x]
        src, _ = self.slot(first + x)
        dve.wait_ge(self.hi_ready.sem, self.hi_ready.at(nth))
        self.nc.vector.tensor_tensor(bufs[1][:, x % depth, 0:kn, 0:width], src,
                                     bufs[0][:, x % depth, 0:kn, 0:width].bitcast(F32), ALU.subtract)\
            .then_inc(self.lo_ready.sem, self.lo_ready.one())

    def load(self, eng, dst, src):
        eng.dma_start(dst, src).then_inc(self.loaded, 16)
        self.n_loaded += 16

    def start(self):
        nc = self.nc
        with self.stage() as block:
            @block.sync
            def _(sp):
                self.load(sp, self.vecs[:, :], self.dram["vecs"])
                self.load(sp, self.tables[:, :], self.dram["tables"])
                self.load(sp, self.res[:, :, 0:S], self.dram["x"])
                self.load(sp, self.res[:, :, S:2 * S], self.dram["ctx"])
                self.refill(sp, SLOTS)
                sp.wait_ge(self.loaded, self.n_loaded)

    def modulation(self, bias, chunks):
        nc = self.nc
        nv, c, pair = 1, self.cond[:, :, :], self.cond_pair[:, :, :]
        src, src_pair = (self.vec(x).rearrange("p (k v) -> p k v", k=KC) for x in ("c", "cc"))
        out = self.bank[7][:, 0:48 * nv].rearrange("p (i v) -> p i v", v=nv)
        n = self.plan_use([1] * chunks, whole=range(chunks))
        with ExitStack() as ctx, self.stage() as block:
            line = self.sb("mod_line", [nv, chunks * CW], ctx=ctx)

            @block.scalar
            def _(act):
                nc.scalar.activation(c, src, ACT.Sigmoid).then_inc(self.act_ready.sem, self.act_ready.one())
                nc.scalar.activation(pair, src_pair, ACT.Sigmoid).then_inc(self.act_ready.sem, self.act_ready.one())
                for i in range(chunks):
                    act.wait_ge(self.sums_ready.sem, self.sums_ready.at(i + 1))
                    nc.scalar.copy(line[:, i * CW:(i + 1) * CW], self.bank[i % 4][0:nv, 0:CW])\
                        .then_inc(self.sums_taken.sem, self.sums_taken.one())

            @block.vector
            def _(dve):
                dve.wait_ge(self.act_ready.sem, self.act_ready.at(1))
                nc.vector.tensor_tensor(c, c, src, ALU.mult).then_inc(self.dve_ready.sem, self.dve_ready.one())
                dve.wait_ge(self.act_ready.sem, self.act_ready.at(2))
                nc.vector.tensor_tensor(pair, pair, src_pair, ALU.mult)
                dve.wait_ge(self.pe_ready.sem, self.pe_ready.at(1))
                b = self.vec(bias)[:, 0:2 * chunks].unsqueeze(2).to_broadcast([P, 2 * chunks, nv])
                m = self.mod[:, :, :, 0:nv].rearrange("p i c v -> p (i c) v")[:, 0:2 * chunks, :]
                nc.vector.tensor_tensor(m, out[:, 0:2 * chunks, :], b, ALU.add)

            @block.tensor
            def _(pe):
                pe.wait_ge(self.dve_ready.sem, self.dve_ready.at(1))
                for i in range(chunks + 1):
                    if i < chunks:
                        w, landed = self.slot(n + i)
                        pe.wait_ge(self.landed[(n + i) % SLOTS], landed)
                        if i >= 4:
                            pe.wait_ge(self.sums_taken.sem, self.sums_taken.at(i - 3))
                        for k in range(KC):
                            mm = nc.tensor.matmul(self.bank[i % 4][0:nv, 0:CW], c[:, k, :], w[:, k, :],
                                                  start=(k == 0), stop=(k == KC - 1))
                        mm.then_inc(self.sums_ready.sem, self.sums_ready.one())
                    if i >= 1:
                        pe.wait_ge(self.sums_taken.sem, self.sums_taken.at(i))
                        for j in (2 * i - 2, 2 * i - 1):
                            mm = nc.tensor.transpose(out[:, j, :], line[:, P * j:P * j + P],
                                                     self.tab("ident")[0:nv, 0:nv])
                mm.then_inc(self.pe_ready.sem, self.pe_ready.one())

            @block.sync
            def _(sp):
                self.refill(sp, chunks)

    def rms_modulate(self, gain, shift, scale):
        nc = self.nc
        total = self.bank[0][:, 0:S]
        rstd = self.stat[:, 0, 0:S]
        with self.stage() as block:
            @block.vector
            def _(dve):
                for k in range(KC):
                    nc.vector.tensor_tensor(self.h[:, k, S:2 * S], self.res[:, k, 0:S],
                                                               self.res[:, k, 0:S], ALU.mult)\
                                                                   .then_inc(self.dve_ready.sem, self.dve_ready.one())
                nc.vector.scalar_tensor_tensor(
                    self.amp[:, :], self.mod[:, scale, :, 0], 1.0, self.vec(gain), ALU.add, ALU.mult)\
                        .then_inc(self.dve_ready.sem, self.dve_ready.one())
                dve.wait_ge(self.pe_ready.sem, self.pe_ready.at(1))
                nc.vector.tensor_scalar(rstd, total, 1.0 / D, EPS_RMS, ALU.mult, ALU.add)\
                    .then_inc(self.dve_ready.sem, self.dve_ready.one())
                dve.wait_ge(self.act_ready.sem, self.act_ready.at(1))
                for k in range(KC):
                    nc.vector.tensor_tensor(self.h[:, k, 0:S], self.res[:, k, 0:S], rstd,
                                                               ALU.mult)\
                                                                   .then_inc(self.dve_ready.sem, self.dve_ready.one())

            @block.tensor
            def _(pe):
                for k in range(KC):
                    pe.wait_ge(self.dve_ready.sem, self.dve_ready.at(k + 1))
                    mm = nc.tensor.matmul(total, self.tab("ones")[:, 0:P], self.h[:, k, S:2 * S],
                                          start=(k == 0), stop=(k == KC - 1))
                mm.then_inc(self.pe_ready.sem, self.pe_ready.one())

            @block.scalar
            def _(act):
                act.wait_ge(self.dve_ready.sem, self.dve_ready.at(KC + 2))
                nc.scalar.activation(rstd, rstd, ACT.Ln).then_inc(self.act_step.sem, self.act_step.one())
                act.wait_ge(self.act_step.sem, self.act_step.count)
                nc.scalar.activation(rstd, rstd, ACT.Exp, scale=-0.5)\
                    .then_inc(self.act_ready.sem, self.act_ready.one())
                for k in range(KC):
                    act.wait_ge(self.dve_ready.sem, self.dve_ready.at(KC + 3 + k))
                    nc.scalar.activation(self.h[:, k, 0:S], self.h[:, k, 0:S], ACT.Identity,
                                         bias=self.mod[:, shift, k, 0:1], scale=self.amp[:, k:k + 1])

    def split_input(self, name, ctx, width):
        return [self.sb(f"{name}_{part}", [P, KC, width], F32R, ctx=ctx) for part in ("xhi", "xlo")]

    def input_high(self, act, x, width):
        for k in range(0, KC, 2):
            self.nc.scalar.copy(x[0][:, k:k + 2, :], self.h[:, k:k + 2, 0:width])\
                .then_inc(self.xhi_ready.sem, self.xhi_ready.one())

    def input_low(self, dve, x, width):
        for k in range(0, KC, 2):
            dve.wait_ge(self.xhi_ready.sem, self.xhi_ready.at(k // 2 + 1))
            self.nc.vector.tensor_tensor(x[1][:, k:k + 2, :], self.h[:, k:k + 2, 0:width],
                                         x[0][:, k:k + 2, :].bitcast(F32), ALU.subtract)\
                .then_inc(self.xlo_ready.sem, self.xlo_ready.one())

    def project(self, layout, width, tok, feat):
        nc = self.nc
        tokens = lambda part: part[3] if len(part) > 3 else width
        tiles = lambda part: tokens(part) // P if part[1] == "tok" else 1
        chunks = len(layout)
        narrow = [i for i in range(chunks) if self.shape[self.next_use + i][1] < P]
        n = self.plan_use([sum(tiles(part) for part in parts) for parts in layout],
                          whole=narrow)
        nth = {}
        for i in range(chunks):
            if i not in narrow:
                nth[i] = len(nth) + 1

        def groups():
            for i, parts in enumerate(layout):
                for part in parts:
                    for t in range(tiles(part)):
                        yield i, *part[0:3], t, tokens(part)

        with ExitStack() as ctx, self.stage() as block:
            bufs = self.split_buffers("pr", 2, ctx)
            x = self.split_input("pr", ctx, width)

            @block.tensor
            def _(pe):
                at = -1
                for g, (i, (c0, c1), kind, place, t, n_tok) in enumerate(groups()):
                    if i != at:
                        at = i
                        if i in nth:
                            hi, lo = (b[:, i % 2, :, :] for b in bufs)
                            pe.wait_ge(self.lo_ready.sem, self.lo_ready.at(nth[i]))
                        else:
                            w, landed = self.slot(n + i)
                            pe.wait_ge(self.landed[(n + i) % SLOTS], landed)
                    if g >= 8:
                        pe.wait_ge(self.sums_taken.sem, self.sums_taken.at(g - 7))
                    if kind == "tok":
                        out = self.bank[g % 8][:, 0:c1 - c0]
                    else:
                        out = self.bank[g % 8][0:c1 - c0, 0:n_tok]
                    for k in range(KC):
                        if i not in nth:
                            mm = nc.tensor.matmul(out, w[:, k, c0:c1], self.h[:, k, 0:n_tok],
                                                  start=(k == 0), stop=(k == KC - 1))
                            continue
                        if g == 0 and k % 2 == 0:
                            pe.wait_ge(self.xlo_ready.sem, self.xlo_ready.at(k // 2 + 1))
                        for term, (wp, xp) in enumerate(((hi, x[0]), (lo, x[0]), (hi, x[1]))):
                            wk, xk = wp[:, k, c0:c1], xp[:, k, P * t:P * t + P] if kind == "tok" else xp[:, k, 0:n_tok]
                            a, b = (xk, wk) if kind == "tok" else (wk, xk)
                            mm = nc.tensor.matmul(out, a, b, start=(k == 0 and term == 0),
                                                  stop=(k == KC - 1 and term == 2))
                    mm.then_inc(self.sums_ready.sem, self.sums_ready.one())

            @block.scalar
            def _(act):
                self.split_high(act, bufs, n, 0)
                self.input_high(act, x, width)
                at = -1
                for g, (i, (c0, c1), kind, place, t, n_tok) in enumerate(groups()):
                    if i != at:
                        at = i
                        if i + 1 in nth:
                            self.split_high(act, bufs, n, i + 1)
                    act.wait_ge(self.sums_ready.sem, self.sums_ready.at(g + 1))
                    if kind == "tok":
                        cp = nc.scalar.copy(tok[:, t, place:place + c1 - c0], self.bank[g % 8][:, 0:c1 - c0])
                    else:
                        cp = nc.scalar.copy(feat[place][:, 0:n_tok], self.bank[g % 8][0:c1 - c0, 0:n_tok])
                    cp.then_inc(self.sums_taken.sem, self.sums_taken.one())

            @block.vector
            def _(dve):
                for i in nth:
                    self.split_low(dve, bufs, n, i, nth[i])
                    if i == 0:
                        self.input_low(dve, x, width)

            @block.sync
            def _(sp):
                self.refill(sp, chunks)

    def transposes(self, jobs):
        nc = self.nc
        with self.stage() as block:
            @block.tensor
            def _(pe):
                for g, (sources, rows, _) in enumerate(jobs):
                    if g >= 8:
                        before = self.act_ready if g % 2 == 0 else self.dve_ready
                        pe.wait_ge(before.sem, before.at((g - 8) // 2 + 1))
                    for b, src in enumerate(sources):
                        mm = nc.tensor.transpose(self.bank[g % 8][0:rows, P * b:P * b + P], src, self.tab("ident"))
                    mm.then_inc(self.pe_ready.sem, self.pe_ready.one())

            @block.scalar
            def _(act):
                for g in range(0, len(jobs), 2):
                    sources, rows, dst = jobs[g]
                    act.wait_ge(self.pe_ready.sem, self.pe_ready.at(g + 1))
                    nc.scalar.copy(dst, self.bank[g % 8][0:rows, 0:P * len(sources)])\
                        .then_inc(self.act_ready.sem, self.act_ready.one())

            @block.vector
            def _(dve):
                for g in range(1, len(jobs), 2):
                    sources, rows, dst = jobs[g]
                    dve.wait_ge(self.pe_ready.sem, self.pe_ready.at(g + 1))
                    nc.vector.tensor_copy(dst, self.bank[g % 8][0:rows, 0:P * len(sources)])\
                        .then_inc(self.dve_ready.sem, self.dve_ready.one())

    def attention(self, units, name, side=None):
        nc = self.nc
        count = len(units)
        ident = self.tab("ident")
        S_, T_, O_ = self.bank[0:2], self.bank[2:4], self.bank[4:6]
        steps = 4 * side["chunks"] if side else 0
        with ExitStack() as ctx, self.stage() as block:
            logits = self.sb(name + "_logits", [P, 2, S], ctx=ctx)
            soft = self.sb(name + "_soft", [P, 2, S], ctx=ctx)
            probs = self.sb(name + "_probs", [P, 2, 2 * S], ctx=ctx)
            turned = self.sb(name + "_turned", [P, 2, 2 * S], ctx=ctx)
            peak = self.sb(name + "_peak", [P, 2], ctx=ctx)
            mass = self.sb(name + "_mass", [P, 4], ctx=ctx)
            part = self.sb(name + "_part", [P, 2], ctx=ctx)
            sizes = [u["key"].shape[1] for u in units]

            @block.tensor
            def _(pe):
                for i in range(count + 2):
                    if i < count:
                        u = units[i]
                        mm = nc.tensor.matmul(S_[i % 2][:, 0:sizes[i]], u["q"], u["key"], start=True,
                                              stop=not u["add"], skip_group_check=True)
                        for x, (add, c0) in enumerate(u["add"]):
                            mm = nc.tensor.matmul(S_[i % 2][:, c0:c0 + add.shape[1]], ident, add, start=False,
                                                  stop=True, skip_group_check=True)
                        mm.then_inc(self.scores_ready.sem, self.scores_ready.one())
                    if 1 <= i <= count:
                        j = i - 1
                        pe.wait_ge(self.probs_ready.sem, self.probs_ready.at(j + 1))
                        if j >= 2:
                            pe.wait_ge(self.turned_copied.sem, self.turned_copied.at(j - 1))
                        for b in range(sizes[j] // P):
                            mm = nc.tensor.transpose(T_[j % 2][:, P * b:P * b + P],
                                                     probs[:, j % 2, P * b:P * b + P], ident)
                        mm.then_inc(self.turned.sem, self.turned.one())
                    if i >= 2:
                        j = i - 2
                        nb = sizes[j] // P
                        pe.wait_ge(self.turned_copied.sem, self.turned_copied.at(j + 1))
                        if j >= 2:
                            pe.wait_ge(self.mixed_taken.sem, self.mixed_taken.at(j - 1))
                        for b in range(nb):
                            mm = nc.tensor.matmul(O_[j % 2][:, 0:HD], turned[:, j % 2, P * b:P * b + P],
                                                  units[j]["values"][b], start=(b == 0), stop=(b == nb - 1))
                        mm.then_inc(self.mixed.sem, self.mixed.one())
                    if i < count:
                        for step in range(steps * i // count, steps * (i + 1) // count):
                            self.side_step(pe, side, step)
                if side:
                    self.side_last(pe, side)

            if side:
                @block.sync
                def _(sp):
                    self.refill(sp, side["chunks"])

            @block.vector
            def _(dve):
                for i in range(count + 2):
                    if i < count:
                        u, b, n = units[i], i % 2, sizes[i]
                        sc = S_[b][:, 0:n]
                        if i >= 2:
                            dve.wait_ge(self.probs_ready.sem, self.probs_ready.at(i - 1))
                        if u["hide"] is None:
                            dve.wait_ge(self.scores_ready.sem, self.scores_ready.at(i + 1))
                            nc.vector.reduce_max(peak[:, b:b + 1], sc, AX_X, negate=True)\
                                .then_inc(self.logits_ready.sem, self.logits_ready.one())
                        else:
                            sf, lg = soft[:, b, 0:n], logits[:, b, 0:n]
                            dve.wait_ge(self.mass_ready.sem, self.mass_ready.at(i + 1))
                            nc.vector.scalar_tensor_tensor(
                                sf, sc, 0.0, sf, ALU.max, ALU.add).then_inc(self.dve_step.sem, self.dve_step.one())
                            dve.wait_ge(self.dve_step.sem, self.dve_step.count)
                            nc.vector.tensor_tensor(sf, sf, u["hide"][0], ALU.mult)\
                                .then_inc(self.dve_step.sem, self.dve_step.one())
                            dve.wait_ge(self.dve_step.sem, self.dve_step.count)
                            nc.vector.tensor_tensor_scan(
                                lg[:, ::-1], self.tab("ones")[:, 0:n], sf[:, ::-1], 0.0, ALU.mult, ALU.add)\
                                    .then_inc(self.dve_step.sem, self.dve_step.one())
                            dve.wait_ge(self.dve_step.sem, self.dve_step.count)
                            nc.vector.tensor_tensor(lg, sc, lg, ALU.subtract)\
                                .then_inc(self.dve_step.sem, self.dve_step.one())
                            dve.wait_ge(self.dve_step.sem, self.dve_step.count)
                            nc.vector.tensor_tensor(lg, lg, u["hide"][1], ALU.add)\
                                .then_inc(self.logits_ready.sem, self.logits_ready.one())
                    if i >= 2:
                        j = i - 2
                        u, b = units[j], j % 2
                        o = O_[b][:, 0:HD]
                        dve.wait_ge(self.mixed.sem, self.mixed.at(j + 1))
                        if u["hide"] is None:
                            nc.vector.reciprocal(part[:, b:b + 1], mass[:, j % 4:j % 4 + 1])\
                                .then_inc(self.dve_step.sem, self.dve_step.one())
                            dve.wait_ge(self.dve_step.sem, self.dve_step.count)
                            nc.vector.tensor_scalar(u["out"], o, part[:, b:b + 1], None, ALU.mult)\
                                .then_inc(self.mixed_taken.sem, self.mixed_taken.one())
                        else:
                            nc.vector.tensor_copy(u["out"], o)\
                                .then_inc(self.mixed_taken.sem, self.mixed_taken.one())
                if side:
                    self.side_bias(dve, side)

            @block.scalar
            def _(act):
                for i in range(count + 1):
                    for x in range(steps * (i - 1) // count // 4 if i else 0, steps * i // count // 4):
                        self.side_copy(act, nc.scalar.copy, side, x)
                    if i < count:
                        u, b, n = units[i], i % 2, sizes[i]
                        sc, pr = S_[b][:, 0:n], probs[:, b, 0:n]
                        if u["hide"] is not None:
                            sf = soft[:, b, 0:n]
                            act.wait_ge(self.scores_ready.sem, self.scores_ready.at(i + 1))
                            nc.scalar.activation(sf, sc, ACT.Abs).then_inc(self.act_step.sem, self.act_step.one())
                            act.wait_ge(self.act_step.sem, self.act_step.count)
                            nc.scalar.activation(sf, sf, ACT.Exp, scale=-1.0)\
                                .then_inc(self.act_step.sem, self.act_step.one())
                            act.wait_ge(self.act_step.sem, self.act_step.count)
                            nc.scalar.activation(sf, sf, ACT.Ln, bias=1.0)\
                                .then_inc(self.mass_ready.sem, self.mass_ready.one())
                        act.wait_ge(self.logits_ready.sem, self.logits_ready.at(i + 1))
                        if i >= 2:
                            act.wait_ge(self.turned.sem, self.turned.at(i - 1))
                        if u["hide"] is None:
                            if i >= 4:
                                act.wait_ge(self.mixed_taken.sem, self.mixed_taken.at(i - 3))
                            nc.scalar.activation(
                                pr, sc, ACT.Exp, bias=peak[:, b:b + 1], accum_out=mass[:, i % 4:i % 4 + 1])\
                                    .then_inc(self.probs_ready.sem, self.probs_ready.one())
                        else:
                            nc.scalar.activation(pr, logits[:, b, 0:n], ACT.Exp)\
                                .then_inc(self.probs_ready.sem, self.probs_ready.one())
                    if i >= 1:
                        j = i - 1
                        act.wait_ge(self.turned.sem, self.turned.at(j + 1))
                        if j >= 2:
                            act.wait_ge(self.mixed.sem, self.mixed.at(j - 1))
                        nc.scalar.copy(turned[:, j % 2, 0:sizes[j]], T_[j % 2][:, 0:sizes[j]])\
                            .then_inc(self.turned_copied.sem, self.turned_copied.one())

    def out_project(self, width, vectors, scaled):
        nc = self.nc
        n = self.plan_use([2] * 4)
        with ExitStack() as ctx, self.stage() as block:
            bufs = self.split_buffers("op", 3, ctx)
            x = self.split_input("op", ctx, width)

            @block.tensor
            def _(pe):
                for g in range(KC):
                    i, c0 = g // 2, P * (g % 2)
                    hi, lo = (b[:, i % 3, :, c0:c0 + P] for b in bufs)
                    pe.wait_ge(self.lo_ready.sem, self.lo_ready.at(i + 1))
                    for k in range(KC):
                        if g == 0 and k % 2 == 0:
                            pe.wait_ge(self.xlo_ready.sem, self.xlo_ready.at(k // 2 + 1))
                        for term, (wp, xp) in enumerate(((hi, x[0]), (lo, x[0]), (hi, x[1]))):
                            mm = nc.tensor.matmul(self.bank[g][:, 0:width], wp[:, k, :], xp[:, k, :],
                                                  start=(k == 0 and term == 0), stop=(k == KC - 1 and term == 2))
                    mm.then_inc(self.sums_ready.sem, self.sums_ready.one())

            @block.scalar
            def _(act):
                for i in range(4):
                    self.split_high(act, bufs, n, i)
                    if i == 0:
                        self.input_high(act, x, width)

            @block.vector
            def _(dve):
                for i in range(3):
                    self.split_low(dve, bufs, n, i, i + 1)
                    if i == 0:
                        self.input_low(dve, x, width)
                if scaled:
                    nc.vector.tensor_scalar(self.res[:, :, 0:width], self.res[:, :, 0:width], ALPHA, None, ALU.mult)\
                        .then_inc(self.dve_step.sem, self.dve_step.one())
                    dve.wait_ge(self.dve_step.sem, self.dve_step.count)
                for g in range(KC):
                    dve.wait_ge(self.sums_ready.sem, self.sums_ready.at(g + 1))
                    for v in range(vectors):
                        r = self.res[:, g, S * v:S * v + S]
                        nc.vector.scalar_tensor_tensor(r, self.bank[g][:, S * v:S * v + S],
                                                       self.mod[:, 2, g, v:v + 1], r, ALU.mult, ALU.add)
                    if g == 1:
                        self.split_low(dve, bufs, n, 3, 4)

            @block.sync
            def _(sp):
                self.refill(sp, 4)

    def first_block(self):
        nc = self.nc
        self.modulation("b_ada", FRONT1)
        self.rms_modulate("norm1_g", 0, 1)
        with ExitStack() as ctx:
            tok = self.sb("b1_tok", [P, 2, 2310], ctx=ctx)
            conv = self.sb("b1_conv", [P, 6, S], ctx=ctx)
            vpad = self.sb("b1_vpad", [P, 2, S + 2], ctx=ctx)
            ytok = self.sb("b1_y", [P, 2, 2 * HEADS * HD], ctx=ctx)
            qk = self.sb("b1_qk", [66, 4 * HEADS, S], ctx=ctx)
            layout = [[((0, P), "feat", 2 * i), ((P, CW), "feat", 2 * i + 1)] for i in range(3)]
            layout += [[((0, CW), "tok", i * CW)] for i in range(9)]
            self.project(layout, S, tok, [conv[:, i, :] for i in range(6)])
            self.conv_and_gates(tok, conv, vpad, ctx)
            fox = self.fox
            self.transposes([([tok[:, t, HD * h:HD * h + HD] for h in (2 * i, 2 * i + 1) for t in range(2)], HD,
                              qk[0:HD, 2 * i:2 * i + 2, :]) for i in range(6)]
                            + [([fox[:, t, h, :] for h in (2 * i, 2 * i + 1) for t in range(2)], 66,
                                qk[0:66, 12 + 2 * i:14 + 2 * i, :]) for i in range(6)])
            tok_v = lambda off, h, b: tok[:, b, off + HD * h:off + HD * h + HD]
            units = []
            for kind in range(2):
                for h in range(HEADS):
                    for t in range(2):
                        n, c0 = P * (t + 1), P * (1 - t)
                        d = HD if kind == 0 else HD + 2
                        units.append(dict(
                            q=qk[0:d, 12 * kind + h, P * t:P * t + P], key=qk[0:d, 12 * kind + 6 + h, 0:n],
                            add=[] if kind == 0 else [(self.tab("causal")[:, P:2 * P], P * t)],
                            hide=None if kind else (self.tab("strict01")[:, c0:2 * P],
                                                    self.tab("strictneg")[:, c0:2 * P]),
                            values=[tok_v(768 + 1152 * kind, h, b) for b in range(t + 1)],
                            out=ytok[:, t, 384 * kind + HD * h:384 * kind + HD * h + HD]))
            self.attention(units, "b1", self.plan_side(SIDES1["attention"], "b_ada", 1))
            self.transposes([([ytok[:, t, P * (2 * i + c):P * (2 * i + c) + P] for c in range(2) for t in range(2)], P,
                              self.h[:, 2 + 2 * i:4 + 2 * i, 0:S]) for i in range(3)])
            self.group_norm()
        self.out_project(S, 1, False)
        self.rms_modulate("norm2_g", 3, 4)
        self.experts()

    def conv_and_gates(self, tok, conv, vpad, ctx):
        nc = self.nc
        sq = self.sb("b1_sq", [P, 768], ctx=ctx)
        ms = self.sb("b1_ms", [P, 2, 2, 12], ctx=ctx)
        fox = self.sb("b1_fox", [P, 2, 12, 66], ctx=ctx)
        lf = self.sb("b1_lf", [P, 3, 2, 6], ctx=ctx)
        tmp = self.sb("b1_ctmp", [P, 2, 3, S], ctx=ctx)
        side = self.plan_side(SIDES1["conv"], "b_ada", 1)
        flog = self.bank[5][:, 0:12].rearrange("p (t h) -> p t h", h=HEADS)
        cum = self.bank[4][:, 0:12].rearrange("p (t h) -> p t h", h=HEADS)
        w = self.vec("conv_w").rearrange("p (c j) -> p c j", j=3)
        heads = lambda t, kind: tok[:, t, 1152 * kind:1152 * kind + 768].rearrange("p (h d) -> p h d", d=HD)
        with self.stage() as block:
            @block.gpsimd
            def _(pool):
                step = self.pool_step
                nc.gpsimd.memset(vpad[:, :, 0:2], 0.0).then_inc(step.sem, step.one())
                pool.wait_ge(step.sem, step.count)
                nc.gpsimd.tensor_tensor(vpad[:, :, 2:S + 2], conv[:, 2:4, :], conv[:, 4:6, :], ALU.mult)\
                    .then_inc(step.sem, step.one())
                pool.wait_ge(step.sem, step.count)
                for c in range(2):
                    for j in range(3):
                        nc.gpsimd.tensor_scalar(tmp[:, c, j, :], vpad[:, c, j:j + S], w[:, c, j:j + 1],
                                                         None, ALU.mult).then_inc(step.sem, step.one())
                pool.wait_ge(step.sem, step.count)
                nc.gpsimd.tensor_tensor(tmp[:, :, 0, :], tmp[:, :, 0, :], tmp[:, :, 1, :], ALU.add)\
                    .then_inc(step.sem, step.one())
                pool.wait_ge(step.sem, step.count)
                nc.gpsimd.tensor_tensor(tmp[:, :, 0, :], tmp[:, :, 0, :], tmp[:, :, 2, :], ALU.add)\
                    .then_inc(step.sem, step.one())
                pool.wait_ge(step.sem, step.count)
                pool.wait_ge(self.pe_ready.sem, self.pe_ready.at(1))
                nc.gpsimd.tensor_tensor(self.h[:, 0:2, 0:S], tmp[:, :, 0, :], conv[:, 0:2, :], ALU.mult)\
                    .then_inc(step.sem, step.one())
                pool.wait_ge(step.sem, step.count)

            @block.sync
            def _(sp):
                self.refill(sp, side["chunks"])

            @block.tensor
            def _(pe):
                wf = self.vec("w_f").rearrange("p (k n) -> p k n", n=HEADS)
                for t in range(2):
                    for k in range(KC):
                        mm = nc.tensor.matmul(flog[:, t, :], self.h[:, k, P * t:P * t + P], wf[:, k, :],
                                              start=(k == 0), stop=(k == KC - 1))
                mm.then_inc(self.pe_ready.sem, self.pe_ready.one())
                for step in range(8):
                    self.side_step(pe, side, step)
                pe.wait_ge(self.dve_ready.sem, self.dve_ready.at(3))
                for t in range(2):
                    for s in range(t + 1):
                        mm = nc.tensor.matmul(cum[:, t, :], self.tab("upto") if s == t else self.tab("ones")[:, 0:P],
                                              lf[:, 2, s, :], start=(s == 0), stop=(s == t))
                mm.then_inc(self.pe_ready.sem, self.pe_ready.one())
                for step in range(8, 4 * side["chunks"]):
                    self.side_step(pe, side, step)
                self.side_last(pe, side)

            @block.scalar
            def _(act):
                act.wait_ge(self.dve_ready.sem, self.dve_ready.at(1))
                nc.scalar.activation(lf[:, 1, :, :], lf[:, 1, :, :], ACT.Exp, scale=-1.0)\
                    .then_inc(self.act_step.sem, self.act_step.one())
                act.wait_ge(self.act_step.sem, self.act_step.count)
                nc.scalar.activation(lf[:, 1, :, :], lf[:, 1, :, :], ACT.Ln, bias=1.0)\
                    .then_inc(self.act_ready.sem, self.act_ready.one())
                self.side_copy(act, nc.scalar.copy, side, 0)
                act.wait_ge(self.dve_ready.sem, self.dve_ready.at(2))
                nc.scalar.activation(ms[:, :, :, :], ms[:, :, :, :], ACT.Ln)\
                    .then_inc(self.act_step.sem, self.act_step.one())
                act.wait_ge(self.act_step.sem, self.act_step.count)
                nc.scalar.activation(ms[:, :, :, :], ms[:, :, :, :], ACT.Exp, scale=-0.5)\
                    .then_inc(self.act_ready.sem, self.act_ready.one())
                for x in range(1, side["chunks"]):
                    self.side_copy(act, nc.scalar.copy, side, x)

            @block.vector
            def _(dve):
                step = self.dve_step
                dve.wait_ge(self.pe_ready.sem, self.pe_ready.at(1))
                nc.vector.tensor_tensor(lf[:, 0, :, :], flog,
                                                       self.vec("f_b").unsqueeze(1).to_broadcast([P, 2, HEADS]), ALU.add)\
                                                           .then_inc(step.sem, step.one())
                dve.wait_ge(step.sem, step.count)
                nc.vector.scalar_tensor_tensor(lf[:, 1, :, :], lf[:, 0, :, :], -1.0,
                                                                  lf[:, 0, :, :], ALU.mult, ALU.max)\
                                                                      .then_inc(self.dve_ready.sem, self.dve_ready.one())
                for t in range(2):
                    for kind in range(2):
                        v = sq[:, :].rearrange("p (h d) -> p h d", d=HD)
                        nc.vector.tensor_tensor(v, heads(t, kind), heads(t, kind), ALU.mult)\
                            .then_inc(step.sem, step.one())
                        dve.wait_ge(step.sem, step.count)
                        nc.vector.reduce_sum(ms[:, t, kind, :], v, AX_X).then_inc(step.sem, step.one())
                        dve.wait_ge(step.sem, step.count)
                nc.vector.tensor_scalar(ms[:, :, :, :], ms[:, :, :, :], 1.0 / HD, EPS_RMS,
                                                           ALU.mult, ALU.add)\
                                                               .then_inc(self.dve_ready.sem, self.dve_ready.one())
                dve.wait_ge(self.act_ready.sem, self.act_ready.at(1))
                nc.vector.scalar_tensor_tensor(
                    lf[:, 2, :, :].rearrange("p t h -> p (t h)"), lf[:, 0, :, :].rearrange("p t h -> p (t h)"), 0.0,
                    lf[:, 1, :, :].rearrange("p t h -> p (t h)"), ALU.min, ALU.subtract)\
                        .then_inc(self.dve_ready.sem, self.dve_ready.one())
                dve.wait_ge(self.act_ready.sem, self.act_ready.at(2))
                nc.vector.tensor_scalar(ms[:, :, :, 0:6], ms[:, :, :, 0:6], HD ** -0.5, None, ALU.mult)\
                    .then_inc(step.sem, step.one())
                dve.wait_ge(step.sem, step.count)
                for t in range(2):
                    for kind in range(2):
                        v, r = heads(t, kind), ms[:, t, kind, :]
                        s = sq[:, :].rearrange("p (h d) -> p h d", d=HD)
                        nc.vector.tensor_tensor(s, v, r.unsqueeze(2).to_broadcast([P, 12, HD]), ALU.mult)\
                            .then_inc(step.sem, step.one())
                        dve.wait_ge(step.sem, step.count)
                        for q in range(2):
                            g = self.vec(("sb_" if kind == 0 else "fox_") + ("q_g" if q == 0 else "k_g"))
                            dst = v[:, 6 * q:6 * q + 6, :] if kind == 0 else fox[:, t, 6 * q:6 * q + 6, 0:HD]
                            nc.vector.tensor_tensor(dst, s[:, 6 * q:6 * q + 6, :],
                                                             g.unsqueeze(1).to_broadcast([P, 6, HD]), ALU.mult)\
                                                                 .then_inc(step.sem, step.one())
                        dve.wait_ge(step.sem, step.count)
                dve.wait_ge(self.pe_ready.sem, self.pe_ready.at(2))
                nc.vector.tensor_copy(fox[:, :, 0:6, 64], cum).then_inc(step.sem, step.one())
                nc.vector.memset(fox[:, :, 0:6, 65], 1.0).then_inc(step.sem, step.one())
                nc.vector.memset(fox[:, :, 6:12, 64], 1.0).then_inc(step.sem, step.one())
                nc.vector.tensor_scalar(fox[:, :, 6:12, 65], cum, -1.0, None, ALU.mult)\
                    .then_inc(step.sem, step.one())
                self.side_bias(dve, side)

        self.fox = fox

    def group_norm(self):
        nc = self.nc
        with ExitStack() as ctx, self.stage() as block:
            sq = self.sb("gn_sq", [P, KC, S], ctx=ctx)

            @block.vector
            def _(dve):
                for c in range(4):
                    y = self.h[:, 2 * c:2 * c + 2, 0:S]
                    nc.vector.tensor_tensor(sq[:, 2 * c:2 * c + 2, :], y, y, ALU.mult)\
                        .then_inc(self.dve_ready.sem, self.dve_ready.one())
                for c in range(4):
                    dve.wait_ge(self.pe_ready.sem, self.pe_ready.at(c + 1))
                    nc.vector.tensor_scalar(
                        sq[:, 2 * c:2 * c + 2, :], self.bank[c][:, :].rearrange("p (c t) -> p c t", t=S),
                        1.0 / HD, EPS_RMS, ALU.mult, ALU.add).then_inc(self.dve_ready.sem, self.dve_ready.one())
                for c in range(4):
                    dve.wait_ge(self.act_ready.sem, self.act_ready.at(c + 1))
                    for k in (2 * c, 2 * c + 1):
                        nc.vector.scalar_tensor_tensor(self.h[:, k, 0:S], self.h[:, k, 0:S],
                                                       self.vec("out_norm_g")[:, k:k + 1], sq[:, k, :],
                                                       ALU.mult, ALU.mult)

            @block.tensor
            def _(pe):
                for c in range(4):
                    pe.wait_ge(self.dve_ready.sem, self.dve_ready.at(c + 1))
                    nc.tensor.matmul(self.bank[c][:, :], self.tab("halves"),
                                                       sq[:, 2 * c:2 * c + 2, :], start=True, stop=True)\
                                                           .then_inc(self.pe_ready.sem, self.pe_ready.one())

            @block.scalar
            def _(act):
                for c in range(4):
                    v = sq[:, 2 * c:2 * c + 2, :]
                    act.wait_ge(self.dve_ready.sem, self.dve_ready.at(4 + c + 1))
                    nc.scalar.activation(v, v, ACT.Ln).then_inc(self.act_step.sem, self.act_step.one())
                    act.wait_ge(self.act_step.sem, self.act_step.count)
                    nc.scalar.activation(v, v, ACT.Exp, scale=-0.5)\
                        .then_inc(self.act_ready.sem, self.act_ready.one())

    def experts(self):
        with ExitStack() as ctx:
            comb = self.sb("moe_comb", [P, 2, EXPERTS], ctx=ctx)
            comb_t = self.sb("moe_comb_t", [EXPERTS, S], ctx=ctx)
            b2 = self.sb("moe_b2", [EXPERTS, D], ctx=ctx)
            self.item_place = self.sb("moe_item_place", [P, 2, ITEMW], ctx=ctx)
            self.item_gate = self.sb("moe_item_gate", [P, 2, ITEMW], ctx=ctx)
            self.item_expert = self.sb("moe_item_expert", [1, ITEMW], I32, ctx=ctx)
            self.n_items = self.sb("moe_n_items", [1, 1], I32, ctx=ctx)
            self.put_back = self.sb("moe_put_back", [P, ITEMS, S], mybir.dt.bfloat16, ctx=ctx)
            self.turned_h = self.sb("moe_turned_h", [P, 2, D], ctx=ctx)
            with ExitStack() as inner:
                self.route(comb, comb_t, b2, inner)
            self.mixture(comb_t, b2, ctx)

    def route(self, comb, comb_t, b2, ctx):
        nc = self.nc
        lg = self.sb("rt_lg", [P, 2, EXPERTS], ctx=ctx)
        top = self.sb("rt_top", [P, 2, 8], ctx=ctx)
        idx = self.sb("rt_idx", [P, 2, 8], U32, ctx=ctx)
        idf = self.sb("rt_idf", [P, 2, 8], ctx=ctx)
        wts = self.sb("rt_w", [P, 2, 4], ctx=ctx)
        neg = self.sb("rt_neg", [P, 2], ctx=ctx)
        mass = self.sb("rt_mass", [P, 2], ctx=ctx)
        hot = self.sb("rt_hot", [P, 2, 4, EXPERTS], ctx=ctx)
        chosen = self.sb("rt_chosen", [P, 2, EXPERTS], ctx=ctx)
        chosen_t = self.sb("rt_chosen_t", [EXPERTS, S], ctx=ctx)
        place_t = self.sb("rt_place_t", [EXPERTS, S], ctx=ctx)
        n_own = self.sb("rt_n_own", [EXPERTS, 1], ctx=ctx)
        after = self.sb("rt_after", [EXPERTS, 1], ctx=ctx)
        begin = self.sb("rt_begin", [EXPERTS, 1], ctx=ctx)
        owns = self.sb("rt_owns", [EXPERTS, ITEMW], ctx=ctx)
        less = self.sb("rt_less", [EXPERTS, ITEMW], ctx=ctx)
        raw = self.bank[0][:, 0:2 * EXPERTS].rearrange("p (t e) -> p t e", e=EXPERTS)
        rw = self.vec("router_w").rearrange("p (k e) -> p k e", e=EXPERTS)
        among = self.bank[2][0:EXPERTS, 0:S]
        ends = self.bank[2][0:EXPERTS, S:S + 1]
        tables = self.bank[3][:, 0:256].rearrange("p (a t i) -> p a t i", a=2, t=2)
        ids, total = self.bank[3][0:1, 256:256 + ITEMW], self.bank[3][0:1, 320:321]
        items = self.tab("iota")[0:EXPERTS, :]
        upto, ones = self.tab("upto"), self.tab("ones")
        pieces = [(t, half) for t in range(2) for half in range(2)]
        side = self.plan_side((0, FRONT2), "b_ada0", 2)
        with self.stage() as block:
            @block.sync
            def _(sp):
                self.load(sp, b2[:, :], self.dram["b_mlp2"][0])
                self.refill(sp, side["chunks"])
                sp.wait_ge(self.loaded, self.n_loaded)

            @block.tensor
            def _(pe):
                for t in range(2):
                    for k in range(KC):
                        mm = nc.tensor.matmul(raw[:, t, :], self.h[:, k, P * t:P * t + P], rw[:, k, :],
                                              start=(k == 0), stop=(k == KC - 1))
                mm.then_inc(self.pe_ready.sem, self.pe_ready.one())
                for x, (t, half) in enumerate(pieces):
                    for k in range(4):
                        mm = nc.tensor.transpose(self.bank[4 + x][:, P * k:P * k + P],
                                                 self.h[:, 4 * half + k, P * t:P * t + P], self.tab("ident"))
                    mm.then_inc(self.turned.sem, self.turned.one())
                pe.wait_ge(self.xhi_ready.sem, self.xhi_ready.at(4))
                for step in range(12):
                    self.side_step(pe, side, step)
                pe.wait_ge(self.dve_ready.sem, self.dve_ready.at(2))
                for t in range(2):
                    mm = nc.tensor.transpose(self.bank[1][0:EXPERTS, P * t:P * t + P], comb[:, t, :], self.tab("ident"))
                mm.then_inc(self.pe_ready.sem, self.pe_ready.one())
                pe.wait_ge(self.dve_ready.sem, self.dve_ready.at(3))
                nc.tensor.matmul(among[:, 0:P], chosen[:, 0, :], upto, start=True, stop=True)
                nc.tensor.matmul(among[:, P:S], chosen[:, 0, :], ones[:, 0:P], start=True, stop=False)
                nc.tensor.matmul(among[:, P:S], chosen[:, 1, :], upto, start=False, stop=True)\
                    .then_inc(self.pe_ready.sem, self.pe_ready.one())
                for step in range(12, 15):
                    self.side_step(pe, side, step)
                pe.wait_ge(self.dve_ready.sem, self.dve_ready.at(4))
                nc.tensor.matmul(ends, upto[0:EXPERTS, 0:EXPERTS], n_own[:, :], start=True, stop=True)\
                    .then_inc(self.pe_ready.sem, self.pe_ready.one())
                for step in range(15, 18):
                    self.side_step(pe, side, step)
                pe.wait_ge(self.dve_ready.sem, self.dve_ready.at(5))
                for t in range(2):
                    c = slice(P * t, P * t + P)
                    nc.tensor.matmul(tables[:, 0, t, 0:ITEMW], place_t[:, c], owns[:, :], start=True, stop=False)
                    nc.tensor.matmul(tables[:, 0, t, 0:ITEMW], ones[0:EXPERTS, 0:P], less[:, :], start=False, stop=True)
                    nc.tensor.matmul(tables[:, 1, t, 0:ITEMW], comb_t[:, c], owns[:, :], start=True, stop=True)
                nc.tensor.matmul(ids, self.tab("line")[0:EXPERTS, :], owns[:, :], start=True, stop=True)
                nc.tensor.matmul(total, n_own[:, :], ones[0:EXPERTS, 0:1], start=True, stop=True)\
                    .then_inc(self.pe_ready.sem, self.pe_ready.one())
                pe.wait_ge(self.dve_ready.sem, self.dve_ready.at(6))
                for g in range(ITEMS // 2):
                    if g >= 3:
                        pe.wait_ge(self.dve_ready.sem, self.dve_ready.at(6 + g - 2))
                    for i in (2 * g, 2 * g + 1):
                        for t in range(2):
                            c0 = S * (i % 2) + P * t
                            mm = nc.tensor.matmul(self.bank[g % 3][:, c0:c0 + P],
                                                  self.item_place[:, t, i:i + 1].to_broadcast([P, P]),
                                                  self.tab("ident"), start=True, stop=True)
                    mm.then_inc(self.pe_ready.sem, self.pe_ready.one())
                    if 18 + g < 4 * side["chunks"]:
                        self.side_step(pe, side, 18 + g)
                self.side_last(pe, side)

            @block.vector
            def _(dve):
                step = self.dve_step
                nc.vector.tensor_scalar(self.vec("b_lin"), self.vec("b_lin"), 1.0, None, ALU.add)
                dve.wait_ge(self.pe_ready.sem, self.pe_ready.at(1))
                nc.vector.tensor_tensor(
                    lg[:, :, :], raw, self.vec("router_b").unsqueeze(1).to_broadcast([P, 2, EXPERTS]), ALU.add)\
                        .then_inc(step.sem, step.one())
                dve.wait_ge(step.sem, step.count)
                for t in range(2):
                    nc.vector.max(top[:, t, :], lg[:, t, :]).then_inc(step.sem, step.one())
                    dve.wait_ge(step.sem, step.count)
                    nc.vector.max_index(idx[:, t, :], top[:, t, :], lg[:, t, :]).then_inc(step.sem, step.one())
                    dve.wait_ge(step.sem, step.count)
                nc.vector.tensor_copy(idf[:, :, :], idx[:, :, :]).then_inc(step.sem, step.one())
                dve.wait_ge(step.sem, step.count)
                nc.vector.tensor_scalar(neg[:, :], top[:, :, 0], -1.0, None, ALU.mult)\
                    .then_inc(self.dve_ready.sem, self.dve_ready.one())
                dve.wait_ge(self.act_ready.sem, self.act_ready.at(1))
                nc.vector.reciprocal(mass[:, :], mass[:, :]).then_inc(step.sem, step.one())
                dve.wait_ge(step.sem, step.count)
                for t in range(2):
                    nc.vector.tensor_scalar(wts[:, t, :], wts[:, t, :], mass[:, t:t + 1], None, ALU.mult)\
                        .then_inc(step.sem, step.one())
                    dve.wait_ge(step.sem, step.count)
                    for k in range(TOPK):
                        nc.vector.tensor_scalar(hot[:, t, k, :], self.tab("iota")[:, 0:EXPERTS], idf[:, t, k:k + 1],
                                                         wts[:, t, k:k + 1], ALU.is_equal, ALU.mult)\
                                                             .then_inc(step.sem, step.one())
                dve.wait_ge(step.sem, step.count)
                nc.vector.tensor_tensor(hot[:, :, 0:2, :], hot[:, :, 0:2, :], hot[:, :, 2:4, :], ALU.add)\
                    .then_inc(step.sem, step.one())
                dve.wait_ge(step.sem, step.count)
                nc.vector.tensor_tensor(comb[:, :, :], hot[:, :, 0, :], hot[:, :, 1, :], ALU.add)\
                    .then_inc(self.dve_ready.sem, self.dve_ready.one())
                dve.wait_ge(self.dve_ready.sem, self.dve_ready.at(2))
                nc.vector.tensor_scalar(chosen[:, :, :], comb[:, :, :], 0.0, None, ALU.is_gt)\
                    .then_inc(self.dve_ready.sem, self.dve_ready.one())
                dve.wait_ge(self.pe_ready.sem, self.pe_ready.at(2))
                nc.vector.tensor_scalar(chosen_t[:, :], self.bank[1][0:EXPERTS, 0:S], 0.0, None, ALU.is_gt)\
                    .then_inc(step.sem, step.one())
                nc.vector.tensor_copy(comb_t[:, :], self.bank[1][0:EXPERTS, 0:S]).then_inc(step.sem, step.one())
                dve.wait_ge(self.pe_ready.sem, self.pe_ready.at(3))
                nc.vector.tensor_scalar(n_own[:, :], among[:, S - 1:S], 0.5, None, ALU.is_gt).then_inc(step.sem, step.one())
                dve.wait_ge(step.sem, step.count)
                for full in range(PLACES, S, PLACES):
                    nc.vector.scalar_tensor_tensor(n_own[:, :], among[:, S - 1:S], full + 0.5, n_own[:, :],
                                                   ALU.is_gt, ALU.add).then_inc(step.sem, step.one())
                    dve.wait_ge(step.sem, step.count)
                nc.vector.tensor_tensor(place_t[:, :], among, chosen_t[:, :], ALU.mult)\
                    .then_inc(self.dve_ready.sem, self.dve_ready.one())
                dve.wait_ge(self.pe_ready.sem, self.pe_ready.at(4))
                nc.vector.tensor_copy(after[:, :], ends).then_inc(step.sem, step.one())
                nc.vector.tensor_tensor(begin[:, :], ends, n_own[:, :], ALU.subtract).then_inc(step.sem, step.one())
                dve.wait_ge(step.sem, step.count)
                nc.vector.tensor_scalar(owns[:, :], items, begin[:, :], None, ALU.is_ge).then_inc(step.sem, step.one())
                nc.vector.tensor_scalar(less[:, :], items, begin[:, :], -float(PLACES), ALU.subtract, ALU.mult)\
                    .then_inc(step.sem, step.one())
                dve.wait_ge(step.sem, step.count)
                nc.vector.scalar_tensor_tensor(owns[:, :], items, after[:, :], owns[:, :], ALU.is_lt, ALU.mult)\
                    .then_inc(step.sem, step.one())
                dve.wait_ge(step.sem, step.count)
                nc.vector.tensor_tensor(less[:, :], less[:, :], owns[:, :], ALU.mult)\
                    .then_inc(self.dve_ready.sem, self.dve_ready.one())
                dve.wait_ge(self.pe_ready.sem, self.pe_ready.at(5))
                nc.vector.tensor_copy(self.item_gate[:, :, :], tables[:, 1, :, 0:ITEMW])
                nc.vector.tensor_copy(self.item_expert[:, :], ids)
                nc.vector.tensor_copy(self.n_items[:, :], total)
                nc.vector.tensor_copy(self.item_place[:, :, :], tables[:, 0, :, 0:ITEMW])\
                    .then_inc(self.dve_ready.sem, self.dve_ready.one())
                for g in range(ITEMS // 2):
                    dve.wait_ge(self.pe_ready.sem, self.pe_ready.at(6 + g))
                    nc.vector.tensor_scalar(self.put_back[:, 2 * g:2 * g + 2, :],
                                            self.bank[g % 3][:, :].rearrange("p (i t) -> p i t", t=S),
                                            self.tab("line1"), None, ALU.is_equal)\
                                                .then_inc(self.dve_ready.sem, self.dve_ready.one())
                self.side_bias(dve, side)

            @block.scalar
            def _(act):
                for x, (t, half) in enumerate(pieces):
                    act.wait_ge(self.turned.sem, self.turned.at(x + 1))
                    nc.scalar.copy(self.turned_h[:, t, 512 * half:512 * half + 512], self.bank[4 + x][:, :])\
                        .then_inc(self.xhi_ready.sem, self.xhi_ready.one())
                act.wait_ge(self.dve_ready.sem, self.dve_ready.at(1))
                for t in range(2):
                    e = nc.scalar.activation(wts[:, t, :], top[:, t, 0:4], ACT.Exp, bias=neg[:, t:t + 1],
                                             accum_out=mass[:, t:t + 1])
                e.then_inc(self.act_ready.sem, self.act_ready.one())
                for x in range(side["chunks"]):
                    self.side_copy(act, nc.scalar.copy, side, x)

    def mixture(self, comb_t, b2, ctx):
        nc = self.nc
        per, n2 = 12, 4
        assert per % SLOTS == 0 and n2 == SLOTS and self.n_moe % SLOTS == 0 and self.n_moe == self.next_use
        w2hi, w2lo = self.split_buffers("moe", n2, ctx)
        hid = [self.sb(f"moe_hid_{part}", [P, KC, PLACES], F32R, ctx=ctx) for part in ("hi", "lo")]
        y = [self.sb(f"moe_y_{part}", [PLACES, n2, CW], F32R, ctx=ctx) for part in ("hi", "lo")]
        back = self.sb("moe_back", [PLACES, S], F32R, ctx=ctx)
        gate = self.sb("moe_gate", [PLACES, 2], ctx=ctx)
        mark = self.sb("moe_mark", [P, 1], ctx=ctx)
        x = self.h[:, :, 2 * P:3 * P]
        glu, lin, sig = (self.h[:, 2 * m:2 * m + 2, 3 * P:4 * P] for m in range(3))
        sel = self.h[:, 0:2, 0:PLACES]
        acc = lambda d: self.bank[4 + d // 2][:, S * (d % 2):S * (d % 2) + S]
        gates = self.bank[1][0:PLACES, 500:501]
        sums, highs = self.counter("moe_sums"), self.counter("moe_highs")
        dve_low, pool_low = self.counter("moe_dve_low"), self.counter("moe_pool_low")
        glus, sigs, pairs = self.counter("moe_glus"), self.counter("moe_sigs"), self.counter("moe_pairs_read")
        hidden, step = self.counter("moe_hidden"), self.counter("moe_dve_step")
        y_high, y_low = self.counter("moe_y_high"), self.counter("moe_y_low")
        sel_ready, back_ready = self.counter("moe_sel_ready"), self.counter("moe_back_ready")
        gathered, x_ready = self.counter("moe_gathered"), self.counter("moe_x_ready")
        next_gate, gate_ready = self.counter("moe_next_gate"), self.counter("moe_gate_ready")
        gates_summed, put = self.counter("moe_gates_summed"), self.counter("moe_put")
        landed = [self.counter(f"moe_landed{i}").sem for i in range(SLOTS)]
        trips = lambda eng: eng.value_load(self.n_items[0:1, 0:1], min_val=1, max_val=ITEMS)
        expert_of = lambda eng, i: eng.value_load(self.item_expert[0:1, bass.ds(i, 1)], min_val=0, max_val=EXPERTS - 1)

        def gather():
            for k in range(KC):
                for t in range(2):
                    mm = nc.tensor.matmul(self.bank[2 + k // 4][:, PLACES * (k % 4):PLACES * (k % 4 + 1)],
                                          self.turned_h[:, t, P * k:P * k + P], sel[:, t, :],
                                          start=(t == 0), stop=(t == 1))
            return mm

        def gather_gates(i):
            for t in range(2):
                mm = nc.tensor.matmul(gates, sel[:, t, :], self.item_gate[:, t, bass.ds(i, 1)],
                                      start=(t == 0), stop=(t == 1))
            return mm

        with self.stage() as block:
            @block.tensor
            def _(pe):
                n = trips(pe)
                for d in range(KC):
                    mm = nc.tensor.matmul(acc(d), b2[:, P * d:P * d + P], comb_t[:, :], start=(d % 2 == 0), stop=False,
                                          skip_group_check=True)
                mm.then_inc(put.sem, 1)
                pe.wait_ge(sel_ready.sem, 2)
                gather_gates(0).then_inc(gates_summed.sem, 1)
                gather().then_inc(gathered.sem, 1)
                pe.wait_ge(next_gate.sem, 1)

                def put_back(i, c):
                    pe.wait_ge(y_low.sem, i * n2 + (c + 1))
                    for d in (2 * c, 2 * c + 1):
                        for part in range(2):
                            mm = nc.tensor.matmul(acc(d), y[part][:, c, P * (d % 2):P * (d % 2) + P], back[:, :],
                                                  start=False, stop=False, skip_group_check=True)
                    return mm

                with pe.Fori(0, n) as i:
                    pe.wait_ge(x_ready.sem, i * 2 + 2)
                    for j in range(KC):
                        pe.wait_ge(landed[j % SLOTS], i * 96 + 32 * (j // SLOTS + 1))
                        if j >= 2:
                            pe.wait_ge(pairs.sem, i * KC + (j - 1))
                        w = self.ring[:, j % SLOTS, :, :].rearrange("p k (c two) -> p k two c", two=2)
                        for half in range(2):
                            for k in range(KC):
                                mm = nc.tensor.matmul(self.bank[j % 2][:, S * half:S * half + PLACES],
                                                      w[:, k, half, :], x[:, k, :], start=(k == 0), stop=(k == KC - 1))
                        mm.then_inc(sums.sem, 1)
                    pe.wait_ge(sel_ready.sem, i * 2 + 4)
                    gather().then_inc(gathered.sem, 1)
                    pe.wait_ge(back_ready.sem, i + 1)
                    for c in range(n2):
                        if c < 3:
                            pe.wait_ge(dve_low.sem, i * 3 + (3 + c + 1))
                        else:
                            pe.wait_ge(pool_low.sem, i + 2)
                        for k in range(KC):
                            if c == 0:
                                pe.wait_ge(hidden.sem, i * KC + (k + 1))
                            if c == 1 and k == 0:
                                gather_gates(i + 1)
                            for term, (w, hp) in enumerate(((w2hi, hid[0]), (w2lo, hid[0]), (w2hi, hid[1]))):
                                mm = nc.tensor.matmul(self.bank[c % 2][:, 0:CW], hp[:, k, :], w[:, c, k, :],
                                                      start=(k == 0 and term == 0), stop=(k == KC - 1 and term == 2))
                        mm.then_inc(sums.sem, 1)
                        if c >= 1:
                            put_back(i, c - 1)
                    put_back(i, n2 - 1).then_inc(put.sem, 1)

            @block.scalar
            def _(act):
                n = trips(act)

                def take_x(i):
                    act.wait_ge(gathered.sem, i + 1)
                    for half in range(2):
                        nc.scalar.copy(x[:, 4 * half:4 * half + 4, :],
                                       self.bank[2 + half][:, :].rearrange("p (k s) -> p k s", s=PLACES))\
                                           .then_inc(x_ready.sem, 1)

                def high(i, c):
                    act.wait_ge(landed[c], i * 96 + 96)
                    nc.scalar.copy(w2hi[:, c, :, :], self.ring[:, c, :, :]).then_inc(highs.sem, 1)

                take_x(0)
                with act.Fori(0, n) as i:
                    for p in range(KC):
                        act.wait_ge(glus.sem, i * KC + (p + 1))
                        nc.scalar.activation(sig[:, p % 2, :], glu[:, p % 2, :], ACT.Sigmoid, scale=SWIGLU_ALPHA)\
                            .then_inc(sigs.sem, 1)
                        if p >= 6:
                            high(i, p - 6)
                    high(i, 2)
                    take_x(i + 1)
                    high(i, 3)
                    act.wait_ge(gate_ready.sem, i + 1)
                    for c in range(n2):
                        act.wait_ge(sums.sem, i * per + (KC + c + 1))
                        nc.scalar.activation(y[0][:, c, :], self.bank[c % 2][:, 0:CW], ACT.Identity,
                                             scale=gate[:, 0:1]).then_inc(y_high.sem, 1)

            @block.gpsimd
            def _(pool):
                n = trips(pool)
                nc.gpsimd.memset(mark[:, :], 0.0).then_inc(pool_low.sem, 1)
                with pool.Fori(0, n) as i:
                    pool.wait_ge(put.sem, i + 1)
                    nc.gpsimd.tensor_copy(back[:, :],
                                          self.put_back[0:PLACES, bass.ds(i, 1), :].rearrange("p i t -> p (i t)"))\
                                              .then_inc(back_ready.sem, 1)
                    pool.wait_ge(highs.sem, i * n2 + n2)
                    nc.gpsimd.tensor_tensor(w2lo[:, 3, :, :], self.ring[:, 3, :, :], w2hi[:, 3, :, :].bitcast(F32),
                                            ALU.subtract).then_inc(pool_low.sem, 1)
                    pool.wait_ge(pool_low.sem, i + 2)
                    pool.wait_ge(back_ready.sem, i + 1)

            @block.vector
            def _(dve):
                n = trips(dve)

                def low(i, c):
                    dve.wait_ge(highs.sem, i * n2 + (c + 1))
                    nc.vector.tensor_tensor(w2lo[:, c, :, :], self.ring[:, c, :, :], w2hi[:, c, :, :].bitcast(F32),
                                            ALU.subtract).then_inc(dve_low.sem, 1)

                def select(i):
                    for t in range(2):
                        nc.vector.tensor_scalar(sel[:, t, :], self.tab("places"), self.item_place[:, t, bass.ds(i, 1)],
                                                None, ALU.is_equal).then_inc(sel_ready.sem, 1)

                for m in range(3):
                    nc.vector.memset(lin[:, 0, m:m + 1], 0.0).then_inc(dve_low.sem, 1)
                select(0)
                dve.wait_ge(gates_summed.sem, 1)
                nc.vector.tensor_copy(gate[:, 1:2], gates).then_inc(next_gate.sem, 1)
                with dve.Fori(0, n) as i:
                    dve.wait_ge(next_gate.sem, i + 1)
                    nc.vector.tensor_copy(gate[:, 0:1], gate[:, 1:2]).then_inc(gate_ready.sem, 1)
                    dve.wait_ge(gathered.sem, i + 1)
                    select(i + 1)
                    e = expert_of(dve, i)
                    for p in range(KC):
                        g, l, s = glu[:, p % 2, :], lin[:, p % 2, :], sig[:, p % 2, :]
                        bg = self.vec("b_glu")[:, bass.ds(e * KC + p, 1)]
                        bl = self.vec("b_lin")[:, bass.ds(e * KC + p, 1)]
                        pair = self.bank[p % 2]
                        dve.wait_ge(sums.sem, i * per + (p + 1))
                        nc.vector.tensor_scalar(g, pair[:, 0:PLACES], bg, SWIGLU_LIMIT, ALU.add, ALU.min)\
                            .then_inc(glus.sem, 1)
                        nc.vector.tensor_scalar(l, pair[:, S:S + PLACES], bl, SWIGLU_LIMIT + 1, ALU.add, ALU.min)\
                            .then_inc(pairs.sem, 1)
                        dve.wait_ge(pairs.sem, i * KC + (p + 1))
                        nc.vector.scalar_tensor_tensor(l, l, 1 - SWIGLU_LIMIT, g, ALU.max, ALU.mult)\
                            .then_inc(step.sem, 1)
                        dve.wait_ge(step.sem, i * (3 * KC) + (3 * p + 1))
                        dve.wait_ge(sigs.sem, i * KC + (p + 1))
                        nc.vector.tensor_tensor(l, l, s, ALU.mult).then_inc(step.sem, 1)
                        dve.wait_ge(step.sem, i * (3 * KC) + (3 * p + 2))
                        nc.vector.tensor_copy(hid[0][:, p, :], l).then_inc(step.sem, 1)
                        dve.wait_ge(step.sem, i * (3 * KC) + (3 * p + 3))
                        nc.vector.tensor_tensor(hid[1][:, p, :], l, hid[0][:, p, :].bitcast(F32),
                                                ALU.subtract).then_inc(hidden.sem, 1)
                        if p == 6:
                            low(i, 0)
                    low(i, 1)
                    low(i, 2)
                    for c in range(n2):
                        dve.wait_ge(y_high.sem, i * n2 + (c + 1))
                        if c == 1:
                            nc.vector.tensor_copy(gate[:, 1:2], gates).then_inc(next_gate.sem, 1)
                        nc.vector.scalar_tensor_tensor(y[1][:, c, :], self.bank[c % 2][:, 0:CW], gate[:, 0:1],
                                                       y[0][:, c, :].bitcast(F32), ALU.mult, ALU.subtract)\
                                                           .then_inc(y_low.sem, 1)
                    dve.wait_ge(y_low.sem, i * n2 + n2)

            @block.sync
            def _(sp):
                w1 = self.dram["w_mlp1"][0].rearrange("e (c p) n -> e p c n", p=P)
                w2 = self.dram["w_mlp2"][0].rearrange("e (c p) n -> e p c n", p=P)
                n = trips(sp)
                with sp.Fori(0, n) as i:
                    e = expert_of(sp, i)
                    for j in range(per):
                        if j < 3:
                            sp.wait_ge(dve_low.sem, i * 3 + (j + 1))
                        elif j == 3:
                            sp.wait_ge(pool_low.sem, i + 1)
                        else:
                            sp.wait_ge(sums.sem, i * per + (j - 3))
                        w, c = (w1, j) if j < KC else (w2, j - KC)
                        for half in range(2):
                            src = w[bass.ds(e, 1), :, 4 * half:4 * half + 4, c * CW:(c + 1) * CW]
                            sp.dma_start(self.ring[:, j % SLOTS, 4 * half:4 * half + 4, :],
                                         src.rearrange("e p c n -> (e p) c n")).then_inc(landed[j % SLOTS], 16)
        self.issue_end = len(self.plan)
        with self.stage() as block:
            @block.vector
            def _(dve):
                for d in range(KC):
                    nc.vector.scalar_tensor_tensor(self.res[:, d, 0:S], acc(d), self.mod[:, 5, d, 0:1],
                                                   self.res[:, d, 0:S], ALU.mult, ALU.add)

            @block.sync
            def _(sp):
                self.refill(sp, SLOTS)

    def modulate(self, width, vectors, shift, scale):
        nc = self.nc
        with self.stage() as block:
            @block.vector
            def _(dve):
                for v in range(vectors):
                    nc.vector.tensor_scalar(self.amp[:, :], self.mod[:, scale, :, v], 1.0, None,
                                                                    ALU.add)\
                                                                        .then_inc(self.dve_step.sem, self.dve_step.one())
                    dve.wait_ge(self.dve_step.sem, self.dve_step.count)
                    for k in range(KC):
                        c = slice(S * v, S * v + S)
                        o = nc.vector.tensor_scalar(self.h[:, k, c], self.res[:, k, c], self.amp[:, k:k + 1],
                                                    self.mod[:, shift, k, v:v + 1], ALU.mult, ALU.add)
                    o.then_inc(self.dve_step.sem, self.dve_step.one())
                    dve.wait_ge(self.dve_step.sem, self.dve_step.count)

    def layer_norm(self, width, gain, bias, l):
        nc = self.nc
        total, spread = self.bank[0][:, 0:width], self.bank[1][:, 0:width]
        mean, rstd = self.stat[:, 0, 0:width], self.stat[:, 1, 0:width]
        g, b = self.vec(f"{gain}{l}"), self.vec(f"{bias}{l}")
        with self.stage() as block:
            @block.tensor
            def _(pe):
                for k in range(KC):
                    mm = nc.tensor.matmul(total, self.tab("ones")[:, 0:P], self.res[:, k, 0:width],
                                          start=(k == 0), stop=(k == KC - 1))
                mm.then_inc(self.pe_ready.sem, self.pe_ready.one())
                for k in range(KC):
                    pe.wait_ge(self.act_ready.sem, self.act_ready.at(k + 1))
                    mm = nc.tensor.matmul(spread, self.tab("ones")[:, 0:P], self.h[:, k, 0:width],
                                          start=(k == 0), stop=(k == KC - 1))
                mm.then_inc(self.pe_ready.sem, self.pe_ready.one())

            @block.vector
            def _(dve):
                dve.wait_ge(self.pe_ready.sem, self.pe_ready.at(1))
                nc.vector.tensor_scalar(mean, total, 1.0 / D, None, ALU.mult)\
                    .then_inc(self.dve_step.sem, self.dve_step.one())
                dve.wait_ge(self.dve_step.sem, self.dve_step.count)
                for k in range(KC):
                    r = self.res[:, k, 0:width]
                    nc.vector.tensor_tensor(r, r, mean, ALU.subtract)\
                        .then_inc(self.dve_ready.sem, self.dve_ready.one())
                dve.wait_ge(self.pe_ready.sem, self.pe_ready.at(2))
                nc.vector.tensor_scalar(rstd, spread, 1.0 / D, EPS_LN, ALU.mult, ALU.add)\
                    .then_inc(self.dve_ready.sem, self.dve_ready.one())
                dve.wait_ge(self.act_ready.sem, self.act_ready.at(KC + 1))
                for k in range(KC):
                    r = self.res[:, k, 0:width]
                    nc.vector.tensor_tensor(r, r, rstd, ALU.mult).then_inc(self.dve_ready.sem, self.dve_ready.one())

            @block.scalar
            def _(act):
                for k in range(KC):
                    act.wait_ge(self.dve_ready.sem, self.dve_ready.at(k + 1))
                    nc.scalar.activation(self.h[:, k, 0:width], self.res[:, k, 0:width], ACT.Square)\
                        .then_inc(self.act_ready.sem, self.act_ready.one())
                act.wait_ge(self.dve_ready.sem, self.dve_ready.at(KC + 1))
                nc.scalar.activation(rstd, rstd, ACT.Ln).then_inc(self.act_step.sem, self.act_step.one())
                act.wait_ge(self.act_step.sem, self.act_step.count)
                nc.scalar.activation(rstd, rstd, ACT.Exp, scale=-0.5)\
                    .then_inc(self.act_ready.sem, self.act_ready.one())
                for k in range(KC):
                    act.wait_ge(self.dve_ready.sem, self.dve_ready.at(KC + 2 + k))
                    nc.scalar.activation(self.res[:, k, 0:width], self.res[:, k, 0:width], ACT.Identity,
                                         bias=b[:, k:k + 1], scale=g[:, k:k + 1])

    def feed_forward(self, width, vectors):
        nc = self.nc
        fp = FC // PARTS
        with ExitStack() as ctx:
            hid = [self.sb(f"ff_hid_{part}", [P, fp, width], F32R, ctx=ctx) for part in ("hi", "lo")]
            sig = self.sb("ff_sig", [P, 2, width], ctx=ctx)
            bufs = self.split_buffers("ff", 2, ctx)
            x = self.split_input("ff", ctx, width)
            outs = 4 * len(PIECES)
            total = PARTS * (fp + outs)
            lows, highs = self.lo_ready.count, self.hi_ready.count
            n = self.plan_use([1] * total)
            for part in range(PARTS):
                at = part * (fp + outs)
                with self.stage() as block:
                    @block.tensor
                    def _(pe):
                        for f in range(fp):
                            pe.wait_ge(self.lo_ready.sem, lows + at + f + 1)
                            if f >= 4:
                                pe.wait_ge(self.sums_taken.sem, self.sums_taken.at(f - 3))
                            for side in range(2):
                                hi, lo = (b[:, (at + f) % 2, :, P * side:P * side + P] for b in bufs)
                                for k in range(KC):
                                    if part == 0 and f == 0 and side == 0 and k % 2 == 0:
                                        pe.wait_ge(self.xlo_ready.sem, self.xlo_ready.at(k // 2 + 1))
                                    for term, (w, xp) in enumerate(((hi, x[0]), (lo, x[0]), (hi, x[1]))):
                                        mm = nc.tensor.matmul(self.bank[2 * (f % 4) + side][:, 0:width],
                                                              w[:, k, :], xp[:, k, :], start=(k == 0 and term == 0),
                                                              stop=(k == KC - 1 and term == 2))
                            mm.then_inc(self.sums_ready.sem, self.sums_ready.one())

                    @block.scalar
                    def _(act):
                        if part == 0:
                            self.split_high(act, bufs, n, 0)
                            self.input_high(act, x, width)
                        for f in range(fp):
                            self.split_high(act, bufs, n, at + f + 1)
                            act.wait_ge(self.sums_ready.sem, self.sums_ready.at(f + 1))
                            if f >= 2:
                                act.wait_ge(self.sums_taken.sem, self.sums_taken.at(f - 1))
                            nc.scalar.activation(sig[:, f % 2, :], self.bank[2 * (f % 4)][:, 0:width], ACT.Sigmoid)\
                                .then_inc(self.gate_ready.sem, self.gate_ready.one())

                    @block.vector
                    def _(dve):
                        step = self.dve_step
                        if part == 0:
                            self.split_low(dve, bufs, n, 0, 1)
                            self.input_low(dve, x, width)
                            nc.vector.tensor_scalar(self.res[:, :, 0:width], self.res[:, :, 0:width], ALPHA, None,
                                                    ALU.mult).then_inc(step.sem, step.one())
                        for f in range(fp):
                            self.split_low(dve, bufs, n, at + f + 1, highs + at + f + 2 - self.hi_ready.base)
                            s = sig[:, f % 2, :]
                            dve.wait_ge(self.gate_ready.sem, self.gate_ready.at(f + 1))
                            nc.vector.tensor_tensor(s, self.bank[2 * (f % 4)][:, 0:width], s, ALU.mult)\
                                .then_inc(step.sem, step.one())
                            dve.wait_ge(step.sem, step.count)
                            nc.vector.tensor_tensor(s, self.bank[2 * (f % 4) + 1][:, 0:width], s, ALU.mult)\
                                .then_inc(step.sem, step.one())
                            dve.wait_ge(step.sem, step.count)
                            nc.vector.tensor_copy(hid[0][:, f, :], s).then_inc(step.sem, step.one())
                            dve.wait_ge(step.sem, step.count)
                            nc.vector.tensor_tensor(hid[1][:, f, :], s, hid[0][:, f, :].bitcast(F32), ALU.subtract)\
                                .then_inc(self.sums_taken.sem, self.sums_taken.one())

                    @block.sync
                    def _(sp):
                        self.refill(sp, fp)

                at += fp
                with self.stage() as block:
                    @block.tensor
                    def _(pe):
                        for i in range(outs):
                            k0, k1 = PIECES[i % len(PIECES)]
                            pe.wait_ge(self.lo_ready.sem, lows + at + i + 1)
                            for d in (2 * (i // len(PIECES)), 2 * (i // len(PIECES)) + 1):
                                hi, lo = (b[:, (at + i) % 2, :, P * (d % 2):P * (d % 2) + P] for b in bufs)
                                for k in range(k0, k1):
                                    for term, (w, hp) in enumerate(((hi, hid[0]), (lo, hid[0]), (hi, hid[1]))):
                                        mm = nc.tensor.matmul(self.bank[d][:, 0:width], w[:, k - k0, :], hp[:, k, :],
                                                              start=(k == 0 and term == 0),
                                                              stop=(k == fp - 1 and term == 2))
                            mm.then_inc(self.sums_ready.sem, self.sums_ready.one())

                    @block.scalar
                    def _(act):
                        for m in range(at + 1, min(at + outs + 1, total)):
                            self.split_high(act, bufs, n, m)

                    @block.vector
                    def _(dve):
                        for i in range(1, outs + 2):
                            if i <= outs and at + i < total:
                                self.split_low(dve, bufs, n, at + i, highs + at + i + 1 - self.hi_ready.base)
                            if i < 2 or (i - 2) % len(PIECES) != len(PIECES) - 1:
                                continue
                            dve.wait_ge(self.sums_ready.sem, self.sums_ready.at(i - 1))
                            for d in (2 * ((i - 2) // len(PIECES)), 2 * ((i - 2) // len(PIECES)) + 1):
                                for v in range(vectors):
                                    r = self.res[:, d, S * v:S * v + S]
                                    nc.vector.scalar_tensor_tensor(r, self.bank[d][:, S * v:S * v + S],
                                                                   self.mod[:, 5, d, v:v + 1], r, ALU.mult, ALU.add)

                    @block.sync
                    def _(sp):
                        self.refill(sp, outs)

    def neighbour_window(self, bias, l):
        nc = self.nc
        with self.stage() as block:
            @block.sync
            def _(sp):
                self.load(sp, bias[:, :, :, :], self.dram["na_bias"][l])
                sp.wait_ge(self.loaded, self.n_loaded)

            @block.vector
            def _(dve):
                dve.wait_ge(self.loaded, self.n_loaded)
                mask = self.tab("colneg").unsqueeze(1).to_broadcast([P, HEADS * 4, 64])
                for t in range(2):
                    v = bias[:, t, :, :].rearrange("p h (r c) -> p (h r) c", c=64)
                    nc.vector.tensor_tensor(v, v, mask, ALU.add)

    def linear_and_norms(self, tok, vz, tiles, asking, l):
        nc = self.nc
        side = self.plan_side(SIDES[l]["norms"], f"b_ada{l}", 2)
        with ExitStack() as ctx, self.stage() as block:
            sq = self.sb("nn_sq", [P, 8, HD], ctx=ctx)
            rot = self.sb("nn_rot", [P, 8, HD], ctx=ctx)
            ms = self.sb("nn_ms", [P, 4, 8], ctx=ctx)
            heads = lambda t: tok[:, t, GAQ:GAQ + 8 * HD].rearrange("p (h d) -> p h d", d=HD)

            @block.gpsimd
            def _(pool):
                nc.gpsimd.memset(vz[:, :, :, :], 0.0).then_inc(self.pool_step.sem, self.pool_step.one())
                pool.wait_ge(self.pool_step.sem, self.pool_step.count)
                for t in range(4):
                    for q in range(2):
                        v = tok[:, t, GLV:GLV + 256].rearrange("p (a b d) -> p a b d", b=2, d=GDV)[:, :, q, :]
                        nc.gpsimd.tensor_copy(vz[:, t, q:4:2, GDV * q:GDV * q + GDV], v)\
                            .then_inc(self.pool_step.sem, self.pool_step.one())
                pool.wait_ge(self.pool_step.sem, self.pool_step.count)

            @block.tensor
            def _(pe):
                for step in range(4 * side["chunks"]):
                    self.side_step(pe, side, step)
                self.side_last(pe, side)

            @block.sync
            def _(sp):
                self.refill(sp, side["chunks"])

            @block.scalar
            def _(act):
                self.side_copy(act, nc.scalar.copy, side, 0)
                act.wait_ge(self.dve_ready.sem, self.dve_ready.at(1))
                m = ms[:, 0:tiles, :]
                nc.scalar.activation(m, m, ACT.Ln).then_inc(self.act_step.sem, self.act_step.one())
                act.wait_ge(self.act_step.sem, self.act_step.count)
                nc.scalar.activation(m, m, ACT.Exp, scale=-0.5).then_inc(self.act_ready.sem, self.act_ready.one())
                for x in range(1, side["chunks"]):
                    self.side_copy(act, nc.scalar.copy, side, x)

            @block.vector
            def _(dve):
                step = self.dve_step
                first = lambda t: 0 if t < asking else HEADS
                nc.vector.memset(ms[:, :, :], 0.0).then_inc(step.sem, step.one())
                dve.wait_ge(step.sem, step.count)
                for t in range(tiles):
                    own = slice(first(t), 8)
                    nc.vector.tensor_tensor(sq[:, own, :], heads(t)[:, own, :], heads(t)[:, own, :], ALU.mult)\
                        .then_inc(step.sem, step.one())
                    dve.wait_ge(step.sem, step.count)
                    nc.vector.reduce_sum(ms[:, t, own], sq[:, own, :], AX_X).then_inc(step.sem, step.one())
                    dve.wait_ge(step.sem, step.count)
                m = ms[:, 0:tiles, :]
                nc.vector.tensor_scalar(m, m, 1.0 / HD, EPS_RMS, ALU.mult, ALU.add)\
                    .then_inc(self.dve_ready.sem, self.dve_ready.one())
                for t in range(asking):
                    q = tok[:, t, NAQ:NAQ + 384]
                    nc.vector.tensor_scalar(q, q, HD ** -0.5, None, ALU.mult).then_inc(step.sem, step.one())
                dve.wait_ge(self.act_ready.sem, self.act_ready.at(1))
                nc.vector.tensor_scalar(ms[:, 0:tiles, 0:6], ms[:, 0:tiles, 0:6], HD ** -0.5, None, ALU.mult)\
                    .then_inc(step.sem, step.one())
                dve.wait_ge(step.sem, step.count)
                for t in range(tiles):
                    x, h0 = heads(t), first(t)
                    nc.vector.tensor_tensor(
                        x[:, h0:8, :], x[:, h0:8, :], ms[:, t, h0:8].unsqueeze(2).to_broadcast([P, 8 - h0, HD]), ALU.mult)\
                            .then_inc(step.sem, step.one())
                    dve.wait_ge(step.sem, step.count)
                    for a, b, g in ((0, 6, "qn"), (6, 8, "kn")):
                        if a < h0:
                            continue
                        nc.vector.tensor_tensor(x[:, a:b, :], x[:, a:b, :],
                                                         self.vec(f"{g}{l}").unsqueeze(1).to_broadcast([P, b - a, HD]),
                                                         ALU.mult).then_inc(step.sem, step.one())
                    dve.wait_ge(step.sem, step.count)
                    if t >= 2:
                        continue
                    cos = self.tab("cos")[:, HD * t:HD * t + HD].unsqueeze(1).to_broadcast([P, 8, HD])
                    for half in range(2):
                        for axis in range(2):
                            c0, c1 = 32 * axis + 16 * half, 32 * axis + 16 * (1 - half)
                            sin = self.tab("sin")[:, HD * t + c0:HD * t + c0 + 16].unsqueeze(1).to_broadcast([P, 8, 16])
                            nc.vector.tensor_tensor(rot[:, :, c0:c0 + 16], x[:, :, c1:c1 + 16], sin, ALU.mult)\
                                .then_inc(step.sem, step.one())
                    dve.wait_ge(step.sem, step.count)
                    nc.vector.tensor_tensor(x, x, cos, ALU.mult).then_inc(step.sem, step.one())
                    dve.wait_ge(step.sem, step.count)
                    nc.vector.tensor_tensor(x, x, rot[:, :, :], ALU.add).then_inc(step.sem, step.one())
                    dve.wait_ge(step.sem, step.count)
                self.side_bias(dve, side)

    def linear_attention(self, l, streams, gq, gk, gg, lr, tok, vz):
        nc = self.nc
        with ExitStack() as ctx:
            cum = self.sb("gl_cum", [P, 2, 2, S + 1], ctx=ctx)
            state = self.sb("gl_state", [P, 2, 2 * P], ctx=ctx)
            levels = self.sb("gl_levels", [P, 2, 7, P], ctx=ctx)
            self.gates_and_ends(l, lr, gk, tok, cum, state, levels)
            for s in streams:
                self.linear_stream(l, s, gq, gk, gg, vz, cum, state, levels)

    def gates_and_ends(self, l, lr, gk, tok, cum, state, levels):
        nc = self.nc
        with ExitStack() as ctx:
            wa = self.sb("gl_wa", [32, 2, P], ctx=ctx)
            gate = self.sb("gl_gate", [P, 2, 2 * S], ctx=ctx)
            tmp = self.sb("gl_tmp", [P, 2, 2 * S], ctx=ctx)
            kend = self.sb("gl_kend", [P, 2, S], ctx=ctx)
            kend_t = self.sb("gl_kend_t", [P, 2, 2, P], ctx=ctx)
            with self.stage() as block:
                @block.sync
                def _(sp):
                    self.load(sp, levels[:, :, :, :].rearrange("p e m t -> p (e m t)"), self.dram["levels"])
                    sp.wait_ge(self.pool_ready.sem, self.pool_ready.at(1))
                    for e in range(2):
                        self.load(sp, wa[16 * e:16 * e + 16, e, :], self.dram["gla_wa2_2"][l, e])
                    sp.wait_ge(self.loaded, self.n_loaded)

                @block.gpsimd
                def _(pool):
                    nc.gpsimd.memset(wa[:, :, :], 0.0).then_inc(self.pool_ready.sem, self.pool_ready.one())
                    nc.gpsimd.memset(cum[:, :, :, 0:1], 0.0).then_inc(self.pool_ready.sem, self.pool_ready.one())
                    pool.wait_ge(self.pool_ready.sem, self.pool_ready.at(2))

                @block.tensor
                def _(pe):
                    pe.wait_ge(self.loaded, self.n_loaded)
                    for e in range(2):
                        mm = nc.tensor.matmul(self.bank[e][:, :], wa[:, e, :], lr, start=True, stop=True)
                    mm.then_inc(self.pe_ready.sem, self.pe_ready.one())

                @block.scalar
                def _(act):
                    act.wait_ge(self.dve_ready.sem, self.dve_ready.at(1))
                    nc.scalar.activation(tmp[:, :, :], tmp[:, :, :], ACT.Exp, scale=-1.0)\
                        .then_inc(self.act_step.sem, self.act_step.one())
                    act.wait_ge(self.act_step.sem, self.act_step.count)
                    nc.scalar.activation(tmp[:, :, :], tmp[:, :, :], ACT.Ln, bias=1.0)\
                        .then_inc(self.act_ready.sem, self.act_ready.one())

                @block.vector
                def _(dve):
                    step = self.dve_step
                    dve.wait_ge(self.pe_ready.sem, self.pe_ready.at(1))
                    for e in range(2):
                        nc.vector.tensor_scalar(gate[:, e, :], self.bank[e][:, :],
                                                         self.vec(f"gla_ba{l}")[:, e:e + 1], None, ALU.add)\
                                                             .then_inc(step.sem, step.one())
                    dve.wait_ge(step.sem, step.count)
                    nc.vector.scalar_tensor_tensor(tmp[:, :, :], gate[:, :, :], -1.0,
                                                                      gate[:, :, :], ALU.mult, ALU.max)\
                                                                          .then_inc(self.dve_ready.sem, self.dve_ready.one())
                    dve.wait_ge(self.act_ready.sem, self.act_ready.at(1))
                    flat = lambda x: x[:, :, :].rearrange("p e t -> p (e t)")
                    nc.vector.scalar_tensor_tensor(flat(gate), flat(gate), 0.0, flat(tmp), ALU.min,
                                                                  ALU.subtract).then_inc(step.sem, step.one())
                    dve.wait_ge(step.sem, step.count)
                    nc.vector.tensor_scalar(flat(gate), flat(gate), 1.0 / 16.0, None, ALU.mult)\
                        .then_inc(step.sem, step.one())
                    dve.wait_ge(step.sem, step.count)
                    dve.wait_ge(self.pool_ready.sem, self.pool_ready.at(2))
                    for e in range(2):
                        for s in range(2):
                            nc.vector.tensor_tensor_scan(cum[:, e, s, 1:S + 1], self.tab("ones"),
                                                                  gate[:, e, S * s:S * s + S], 0.0, ALU.mult, ALU.add)\
                                                                      .then_inc(step.sem, step.one())

            side = self.plan_side(SIDES[l].get("ends"), f"b_ada{l}", 2)
            with self.stage() as block:
                if side:
                    @block.sync
                    def _(sp):
                        self.refill(sp, side["chunks"])

                @block.vector
                def _(dve):
                    step = self.dve_step
                    nc.vector.tensor_scalar(tmp[:, 0, 0:S], cum[:, 0, 1, 1:S + 1],
                                                           cum[:, 0, 1, S:S + 1], -1.0, ALU.subtract, ALU.mult)\
                                                               .then_inc(step.sem, step.one())
                    dve.wait_ge(step.sem, step.count)
                    nc.vector.tensor_copy(tmp[:, 1, 0:S], cum[:, 1, 1, 0:S])\
                        .then_inc(self.dve_ready.sem, self.dve_ready.one())
                    dve.wait_ge(self.act_ready.sem, self.act_ready.at(1))
                    for e in range(2):
                        nc.vector.tensor_tensor(kend[:, e, :], gk[:, S:2 * S], tmp[:, e, 0:S], ALU.mult)\
                            .then_inc(self.dve_ready.sem, self.dve_ready.one())
                    dve.wait_ge(self.pe_ready.sem, self.pe_ready.at(1))
                    nc.vector.tensor_copy(kend_t[:, :, :, :].rearrange("p e t d -> p (e t d)"),
                                                             self.bank[0][:, :])\
                                                                 .then_inc(self.dve_ready.sem, self.dve_ready.one())
                    dve.wait_ge(self.pe_ready.sem, self.pe_ready.at(2))
                    for e in range(2):
                        nc.vector.tensor_tensor(state[:, e, :], self.bank[1 + e][:, 0:2 * P], self.tab("headdiag"), ALU.mult)
                    if side:
                        self.side_bias(dve, side)

                @block.scalar
                def _(act):
                    act.wait_ge(self.dve_ready.sem, self.dve_ready.at(1))
                    nc.scalar.activation(tmp[:, :, 0:S], tmp[:, :, 0:S], ACT.Exp)\
                        .then_inc(self.act_ready.sem, self.act_ready.one())
                    for x in range(side["chunks"] if side else 0):
                        self.side_copy(act, nc.scalar.copy, side, x)

                @block.tensor
                def _(pe):
                    for step in range(8 if side else 0):
                        self.side_step(pe, side, step)
                    pe.wait_ge(self.dve_ready.sem, self.dve_ready.at(3))
                    for e in range(2):
                        for t in range(2):
                            mm = nc.tensor.transpose(self.bank[0][:, P * (2 * e + t):P * (2 * e + t) + P],
                                                     kend[:, e, P * t:P * t + P], self.tab("ident"))
                    mm.then_inc(self.pe_ready.sem, self.pe_ready.one())
                    for step in range(8, 10 if side else 0):
                        self.side_step(pe, side, step)
                    pe.wait_ge(self.dve_ready.sem, self.dve_ready.at(4))
                    for e in range(2):
                        for t in range(2):
                            mm = nc.tensor.matmul(self.bank[1 + e][:, 0:2 * P], kend_t[:, e, t, :],
                                                  tok[:, 2 + t, GLV:GLV + 2 * P], start=(t == 0), stop=(t == 1))
                    mm.then_inc(self.pe_ready.sem, self.pe_ready.one())
                    if side:
                        for step in range(10, 4 * side["chunks"]):
                            self.side_step(pe, side, step)
                        self.side_last(pe, side)

    def linear_stream(self, l, s, gq, gk, gg, vz, cum, state, levels):
        nc = self.nc
        side = self.plan_side(SIDES[l][f"stream{s}"], f"b_ada{l}", 2)
        early = 8
        with ExitStack() as ctx:
            q4 = self.h[:, 0:2, :].rearrange("p c (a t) -> p (c a) t", t=S)
            decay = self.sb("gs_decay", [P, 2, 8, S], ctx=ctx)
            keys = self.sb("gs_keys", [P, 2, 8, S], ctx=ctx)
            moving = self.sb("gs_moving", [P, 2, GH, P], ctx=ctx)
            att = self.sb("gs_att", [P, 2, GH, S], ctx=ctx)
            carry = self.stat[:, :, 0:S]
            out = self.h[:, 5:8, :].rearrange("p x (c t) -> p x c t", t=S)
            q, k = gq[:, S * s:S * s + S], gk[:, S * s:S * s + S]
            hm = self.tab("headmask").unsqueeze(2).to_broadcast([P, GH, S])
            products = [(None, None, t, t) for t in range(2)] + [(0, 0, 1, 0), (1, 0, 0, 1)]
            products += [(e, i, t, t) for e in range(2) for i in range(1, 8) for t in range(2)]
            with self.stage() as block:
                @block.vector
                def _(dve):
                    step = self.dve_step
                    nc.vector.tensor_tensor(q4[:, :, :], q.unsqueeze(1).to_broadcast([P, GH, S]),
                                                               hm, ALU.mult)\
                                                                   .then_inc(self.dve_ready.sem, self.dve_ready.one())
                    for e in range(2):
                        b = cum[:, e, s, 1 - e:S + 1 - e]
                        for i, m in enumerate(LEVELS):
                            blocks = S // (2 * m)
                            border = cum[:, e, s, m:S:2 * m].unsqueeze(2).to_broadcast([P, blocks, 2 * m])
                            nc.vector.tensor_tensor(
                                decay[:, e, i, :].rearrange("p (b w) -> p b w", w=2 * m),
                                b.rearrange("p (b w) -> p b w", w=2 * m), border, ALU.subtract)\
                                    .then_inc(step.sem, step.one())
                        dve.wait_ge(step.sem, step.count)
                        nc.vector.scalar_tensor_tensor(decay[:, e, :, :], decay[:, e, :, :], -1.0,
                                                                          decay[:, e, :, :], ALU.mult, ALU.max)\
                                                                              .then_inc(self.dve_ready.sem, self.dve_ready.one())
                    for e in range(2):
                        dve.wait_ge(self.act_ready.sem, self.act_ready.at(e + 1))
                        nc.vector.tensor_tensor(
                            keys[:, e, :, :], k.unsqueeze(1).to_broadcast([P, 8, S]), decay[:, e, :, :], ALU.mult)\
                                .then_inc(self.dve_ready.sem, self.dve_ready.one())
                    for g, (e, i, t, sp) in enumerate(products):
                        dst = att[:, sp, :, P * t:P * t + P]
                        src = self.bank[g % 4][:, :].rearrange("p (h t) -> p h t", t=P)
                        dve.wait_ge(self.sums_ready.sem, self.sums_ready.at(g + 1))
                        if e is None:
                            mask = self.tab("ident2").unsqueeze(1).to_broadcast([P, GH, P])
                            o = nc.vector.tensor_tensor(dst, src, mask, ALU.mult)
                        elif i == 0:
                            o = nc.vector.tensor_copy(dst, src)
                        else:
                            mask = levels[:, e, i - 1, :].bitcast(I32).unsqueeze(1).to_broadcast([P, GH, P])
                            if g >= 2:
                                dve.wait_ge(self.sums_taken.sem, self.sums_taken.at(g))
                            o = nc.vector.copy_predicated(dst, mask, src)
                        o.then_inc(self.sums_taken.sem, self.sums_taken.one())
                    if s == 0:
                        dve.wait_ge(self.act_ready.sem, self.act_ready.at(4))
                        for e in range(2):
                            nc.vector.tensor_tensor(carry[:, e, :], carry[:, e, :], q, ALU.mult)\
                                .then_inc(step.sem, step.one())
                        dve.wait_ge(step.sem, step.count)
                        nc.vector.tensor_scalar(carry[:, :, :], carry[:, :, :], GDK ** -0.5, None,
                                                                   ALU.mult)\
                                                                       .then_inc(self.dve_ready.sem, self.dve_ready.one())
                    else:
                        nc.vector.tensor_copy(carry[:, 0, 0:1], q[:, 0:1])\
                            .then_inc(self.dve_ready.sem, self.dve_ready.one())
                    dve.wait_ge(self.pe_ready.sem, self.pe_ready.at(1))
                    o = self.bank[4][:, :].rearrange("p (c t) -> p c t", t=S)
                    nc.vector.tensor_copy(out[:, 0, :, :], o).then_inc(step.sem, step.one())
                    dve.wait_ge(step.sem, step.count)
                    nc.vector.tensor_tensor(out[:, 1, :, :], out[:, 0, :, :], out[:, 0, :, :], ALU.mult)\
                        .then_inc(self.dve_ready.sem, self.dve_ready.one())
                    dve.wait_ge(self.pe_ready.sem, self.pe_ready.at(2))
                    nc.vector.tensor_scalar(
                        out[:, 1, :, :], self.bank[5][:, :].rearrange("p (c t) -> p c t", t=S), 1.0 / GDV, EPS_RMS,
                        ALU.mult, ALU.add).then_inc(self.dve_ready.sem, self.dve_ready.one())
                    flat = lambda x: out[:, x, :, :].rearrange("p c t -> p (c t)")
                    dve.wait_ge(self.act_ready.sem, self.act_ready.at(6 if s == 0 else 4))
                    nc.vector.scalar_tensor_tensor(flat(0), flat(0), self.vec(f"gla_nw{l}"), flat(1),
                                                                  ALU.mult, ALU.mult).then_inc(step.sem, step.one())
                    dve.wait_ge(step.sem, step.count)
                    g = gg[:, :, S * s:S * s + S]
                    nc.vector.tensor_tensor(out[:, 2, :, :], out[:, 2, :, :], g, ALU.mult)\
                        .then_inc(step.sem, step.one())
                    dve.wait_ge(step.sem, step.count)
                    nc.vector.tensor_tensor(self.h[:, 3:5, S * s:S * s + S], out[:, 0, :, :], out[:, 2, :, :], ALU.mult)
                    self.side_bias(dve, side)

                @block.scalar
                def _(act):
                    for e in range(2):
                        act.wait_ge(self.dve_ready.sem, self.dve_ready.at(2 + e))
                        nc.scalar.activation(decay[:, e, :, :], decay[:, e, :, :], ACT.Exp, scale=-1.0)\
                            .then_inc(self.act_ready.sem, self.act_ready.one())
                        self.side_copy(act, nc.scalar.copy, side, e)
                    if s == 0:
                        nc.scalar.activation(carry[:, 0, :], cum[:, 0, s, 1:S + 1], ACT.Exp)\
                            .then_inc(self.act_ready.sem, self.act_ready.one())
                        nc.scalar.activation(carry[:, 1, :], cum[:, 1, s, 0:S], ACT.Exp, scale=-1.0,
                                                                bias=cum[:, 1, s, S:S + 1])\
                                                                    .then_inc(self.act_ready.sem, self.act_ready.one())
                    for x in range(2, side["chunks"]):
                        self.side_copy(act, nc.scalar.copy, side, x)
                    act.wait_ge(self.dve_ready.sem, self.dve_ready.at(8))
                    nc.scalar.activation(out[:, 1, :, :], out[:, 1, :, :], ACT.Ln)\
                        .then_inc(self.act_step.sem, self.act_step.one())
                    act.wait_ge(self.act_step.sem, self.act_step.count)
                    nc.scalar.activation(out[:, 1, :, :], out[:, 1, :, :], ACT.Exp, scale=-0.5)\
                        .then_inc(self.act_ready.sem, self.act_ready.one())
                    nc.scalar.activation(out[:, 2, :, :], gg[:, :, S * s:S * s + S], ACT.Sigmoid)\
                        .then_inc(self.act_ready.sem, self.act_ready.one())

                @block.sync
                def _(sp):
                    self.refill(sp, side["chunks"])

                @block.gpsimd
                def _(pool):
                    pool.wait_ge(self.dve_ready.sem, self.dve_ready.at(1))
                    for g, (e, i, t, sp) in enumerate(products[2:]):
                        if i == 0 or (g >= 2 and i == 1 and t == 0):
                            pool.wait_ge(self.dve_ready.sem, self.dve_ready.at(4 + e))
                        if g >= 2:
                            pool.wait_ge(self.sums_ready.sem, self.sums_ready.at(g + 1))
                        nc.gpsimd.tensor_tensor(
                            moving[:, g % 2, :, :], q4[:, :, P * t:P * t + P],
                            decay[:, e, i, P * t:P * t + P].unsqueeze(1).to_broadcast([P, GH, P]), ALU.mult)\
                                .then_inc(self.pool_ready.sem, self.pool_ready.one())
                    pool.wait_ge(self.pool_ready.sem, self.pool_ready.count)

                @block.tensor
                def _(pe):
                    pe.wait_ge(self.dve_ready.sem, self.dve_ready.at(1))
                    for g, (e, i, t, sp) in enumerate(products):
                        if g >= 4:
                            pe.wait_ge(self.sums_taken.sem, self.sums_taken.at(g - 3))
                        if e is None:
                            lhs, rhs = k[:, P * sp:P * sp + P], q4[:, :, P * t:P * t + P]
                        else:
                            pe.wait_ge(self.pool_ready.sem, self.pool_ready.at(g - 1))
                            if i == 0:
                                pe.wait_ge(self.dve_ready.sem, self.dve_ready.at(4 + e))
                            lhs, rhs = keys[:, e, i, P * sp:P * sp + P], moving[:, g % 2, :, :]
                        nc.tensor.matmul(self.bank[g % 4][:, :].rearrange("p (h t) -> p h t", t=P),
                                                             lhs, rhs, start=True, stop=True)\
                                                                 .then_inc(self.sums_ready.sem, self.sums_ready.one())
                        if g == 1:
                            for step in range(early):
                                self.side_step(pe, side, step)
                        elif g > 1:
                            todo, levels_ = 4 * side["chunks"] - early, len(products) - 2
                            for step in range(todo * (g - 2) // levels_, todo * (g - 1) // levels_):
                                self.side_step(pe, side, early + step)
                    self.side_last(pe, side)
                    pe.wait_ge(self.sums_taken.sem, self.sums_taken.at(len(products)))
                    pe.wait_ge(self.dve_ready.sem, self.dve_ready.at(6))
                    for c in range(2):
                        o = self.bank[4][:, S * c:S * c + S]
                        last = None
                        terms = [(vz[:, 2 * s + sp, h, :], att[:, sp, h, :]) for sp in range(2) for h in (2 * c, 2 * c + 1)]
                        if s == 0:
                            terms += [(state[:, e, P * c:P * c + P], carry[:, e, :]) for e in range(2)]
                        for x, (lhs, rhs) in enumerate(terms):
                            mm = nc.tensor.matmul(o, lhs, rhs, start=(x == 0), stop=(x == len(terms) - 1))
                    mm.then_inc(self.pe_ready.sem, self.pe_ready.one())
                    pe.wait_ge(self.dve_ready.sem, self.dve_ready.at(7))
                    nc.tensor.matmul(self.bank[5][:, :], self.tab("halves"), out[:, 1, :, :],
                                                       start=True, stop=True)\
                                                           .then_inc(self.pe_ready.sem, self.pe_ready.one())

    def second_block(self):
        nc = self.nc
        for l in range(LAYERS):
            context_out = l < LAYERS - 1
            v = 2 if context_out else 1
            width = S * v
            self.modulate(2 * S, 2, 0, 1)
            with ExitStack() as ctx:
                tok = self.sb(f"b2_tok{l}", [P, 4, TOKW], ctx=ctx)
                gq = self.sb(f"b2_gq{l}", [P, 2 * S], ctx=ctx)
                gk = self.sb(f"b2_gk{l}", [P, 2 * S], ctx=ctx)
                gg = self.sb(f"b2_gg{l}", [P, 2, 2 * S], ctx=ctx)
                lr = self.sb(f"b2_lr{l}", [32, 2 * S], ctx=ctx)
                feat = [gq[:, :], gk[:, :], gg[:, 0, :], gg[:, 1, :], lr[:, :]]
                asks = lambda c0: width if c0 in (0, 1952) else 2 * S
                layout = [[((0, w), "tok", c0, asks(c0))] for c0, w in IN2[:5]]
                layout += [[((0, P), "feat", 0, width), ((P, CW), "feat", 1)], [((0, CW), "tok", GLV)],
                           [((0, P), "feat", 2, width), ((P, CW), "feat", 3, width)], [((0, 32), "feat", 4)]]
                layout += [[((0, w), "tok", c0 - 1952 + GAQ, asks(c0))] for c0, w in IN2[9:]]
                self.project(layout, 2 * S, tok, feat)
                with ExitStack() as inner:
                    vz = self.sb(f"b2_vz{l}", [P, 4, GH, P], ctx=inner)
                    self.linear_and_norms(tok, vz, 4, 2 * v, l)
                    self.linear_attention(l, (1, 0) if context_out else (0,), gq[:, :], gk[:, :], gg, lr[:, :], tok, vz)
                ytok = self.sb(f"b2_y{l}", [P, 4, HEADS * HD], ctx=ctx)
                bias = self.sb(f"b2_bias{l}", [P, 2, HEADS, S], ctx=ctx)
                self.neighbour_window(bias, l)
                for kind in range(2):
                    with ExitStack() as inner:
                        nk = HEADS if kind == 0 else KV_HEADS
                        qk = self.sb(f"b2_qk{l}{kind}", [HD, HEADS + nk, 2 * S], ctx=inner)
                        q0 = NAQ if kind == 0 else GAQ
                        v0 = NAV if kind == 0 else GAV
                        self.transposes([([tok[:, t, q0 + HD * h:q0 + HD * h + HD] for t in range(n)], HD,
                                          qk[:, h, 0:P * n]) for h in range(HEADS + nk)
                                         for n in (2 * v if h < HEADS else 4,)])
                        units = []
                        for h in range(HEADS):
                            kv = h if kind == 0 else h // (HEADS // KV_HEADS)
                            for t in range(2 * v):
                                k0 = 0 if t < 2 else 2
                                units.append(dict(
                                    q=qk[:, h, P * t:P * t + P], key=qk[:, HEADS + kv, P * k0:2 * S],
                                    add=[(bias[:, t, h, :], 0)] if kind == 0 and t < 2 else [], hide=None,
                                    values=[tok[:, b, v0 + HD * kv:v0 + HD * kv + HD] for b in range(k0, 4)],
                                    out=ytok[:, t, HD * h:HD * h + HD]))
                        side = self.plan_side((0, FRONT2) if kind == 1 and context_out else None, f"b_ada{l + 1}", 2)
                        self.attention(units, f"b2a{l}{kind}", side)
                        self.transposes([([ytok[:, t, P * c:P * c + P] for t in range(2 * v)], P,
                                          self.h[:, 5 * kind + c, 0:width]) for c in range(3)])
            self.out_project(width, v, True)
            self.layer_norm(width, "ln1_g", "ln1_b", l)
            self.modulate(width, v, 3, 4)
            self.feed_forward(width, v)
            self.layer_norm(width, "ln2_g", "ln2_b", l)

    def finish(self):
        nc = self.nc
        with self.stage() as block:
            @block.sync
            def _(sp):
                self.load(sp, self.dram["out"], self.res[:, :, 0:S])
                sp.wait_ge(self.loaded, self.n_loaded)


def hybrid_then_latent_kernel(nc, dram, where, twhere):
    b = Builder(nc, dram, where)
    b.twhere = twhere
    with b.ctx:
        b.allocate()
        b.plan_chunks()
        b.start()
        b.first_block()
        b.second_block()
        b.finish()


_WHOLE = ["w_ada", "w_in", "w_out", "w_mlp1", "w_mlp2", "b_mlp2", "w_ada_2", "w_in_2", "gla_wa2_2", "w_out_2",
          "w_ffn_in_2", "w_ffn_out_2"]


def kernel(**inputs):
    import concourse.bacc as bacc
    from concourse.bass_utils import run_bass_kernel_spmd as run

    inputs = {k: np.asarray(v) for k, v in inputs.items()}
    tokens = lambda a: np.ascontiguousarray(a[0].T.reshape(KC, P, S).transpose(1, 0, 2))
    arrays = {n: np.ascontiguousarray(inputs[n]) for n in _WHOLE}
    arrays["x"], arrays["ctx"] = tokens(inputs["x"]), tokens(inputs["ctx_2"])
    arrays["vecs"], where = pack(packed_vectors(inputs))
    arrays["tables"], twhere = pack(shape_tables())
    arrays["levels"] = level_masks()
    arrays["na_bias"] = neighbour_bias(inputs["na_rpb_2"])
    nc = bacc.Bacc("TRN2", target_bir_lowering=False, num_devices=1)
    dram = {n: nc.dram_tensor(f"in_{n}", a.shape, mybir.dt.from_np(a.dtype), kind="ExternalInput").ap()
            for n, a in arrays.items()}
    dram["out"] = nc.dram_tensor("out_0", (P, KC, S), F32, kind="ExternalOutput").ap()
    hybrid_then_latent_kernel(nc, dram, where, twhere)
    r = run(nc, [{f"in_{n}": a for n, a in arrays.items()}], core_ids=[0])
    out = r.results[0]["out_0"]
    return np.ascontiguousarray(out.transpose(1, 0, 2).reshape(D, S).T)[None]
```
